# Optimizing a Trainium2 kernel written in Bass

```python
import math
import jax, jax.numpy as jnp
from jax import lax
import numpy as np
import jax
import jax.numpy as jnp

D_MODEL = 1024
BATCH = 1
SEQ = 256
DEPTH = 2

GRID_W = 64
N_HEADS = 16
HEAD_DIM = D_MODEL // N_HEADS
MAX_WIN_ROWS = 8
WIN_COLS = 16
COL_QBLOCK = 16
COL_BAND = COL_QBLOCK + WIN_COLS
NEG_INF = -1e30
CONV_WIDTH = 3
PEER_HEADS = 8
PEER_N_KEYS = 128
PEER_N_EXPERTS = PEER_N_KEYS * PEER_N_KEYS
PEER_TOPK = 16
PEER_KEY_DIM = 256
PEER_HALF_DIM = PEER_KEY_DIM // 2
PEER_TOK_CHUNK = 128
N_MIXERS = 2
RMS_EPS = 1e-6


def rms_norm(x, gain):
    x32 = x.astype(jnp.float32)
    y = x32 * lax.rsqrt(jnp.mean(x32 * x32, axis=-1, keepdims=True) + RMS_EPS)
    return (y * gain.astype(jnp.float32)).astype(x.dtype)

def _col_window_tables():
    n_blk = GRID_W // COL_QBLOCK
    qcol = np.arange(GRID_W).reshape(n_blk, COL_QBLOCK)
    band_start = np.clip(np.arange(n_blk) * COL_QBLOCK - WIN_COLS // 2, 0, GRID_W - COL_BAND)
    band_cols = band_start[:, None] + np.arange(COL_BAND)
    win_start = np.clip(qcol - WIN_COLS // 2, 0, GRID_W - WIN_COLS)
    kc = band_cols[:, None, :]
    mask = (kc >= win_start[..., None]) & (kc < win_start[..., None] + WIN_COLS)
    col_off = np.clip(kc - qcol[..., None] + WIN_COLS - 1, 0, 2 * WIN_COLS - 2)
    return (jnp.asarray(band_cols, jnp.int32), jnp.asarray(mask),
            jnp.asarray(col_off, jnp.int32))

def neighbourhood_attention(h, w_qkv, w_o, rel_bias):
    b, s, d = h.shape
    rows = s // GRID_W
    win_rows = min(MAX_WIN_ROWS, rows)
    n_cblk = GRID_W // COL_QBLOCK
    band_cols, col_mask, col_off = _col_window_tables()
    qkv = (h @ w_qkv).reshape(b, rows, GRID_W, 3, N_HEADS, HEAD_DIM)
    qkv = qkv.transpose(3, 0, 4, 1, 2, 5)
    q = qkv[0] * (1.0 / math.sqrt(HEAD_DIM))
    k = qkv[1]
    v = qkv[2]

    def one_row(r):
        rs = jnp.clip(r - win_rows // 2, 0, rows - win_rows)
        q_r = lax.dynamic_index_in_dim(q, r, axis=2, keepdims=False)
        q_r = q_r.reshape(b, N_HEADS, n_cblk, COL_QBLOCK, HEAD_DIM)
        k_band = lax.dynamic_slice_in_dim(k, rs, win_rows, axis=2)[:, :, :, band_cols]
        v_band = lax.dynamic_slice_in_dim(v, rs, win_rows, axis=2)[:, :, :, band_cols]
        scores = jnp.einsum('bhjqd,bhrjkd->bhjqrk', q_r.astype(jnp.float32),
                            k_band.astype(jnp.float32))
        row_off = rs + jnp.arange(win_rows) - r + MAX_WIN_ROWS - 1
        bias = rel_bias[:, row_off[None, None, :, None], col_off[:, :, None, :]]
        scores = jnp.where(col_mask[:, :, None, :], scores + bias.astype(jnp.float32), NEG_INF)
        p = jax.nn.softmax(scores, axis=(-2, -1)).astype(v.dtype)
        o = jnp.einsum('bhjqrk,bhrjkd->bhjqd', p, v_band)
        return o.reshape(b, N_HEADS, GRID_W, HEAD_DIM)

    out = lax.map(one_row, jnp.arange(rows))
    out = out.transpose(1, 0, 3, 2, 4).reshape(b, s, d)
    return out @ w_o

def short_conv_mixer(h, w_in, w_conv, w_out):
    s = h.shape[1]
    gate_b, gate_c, val = jnp.split(h @ w_in, 3, axis=-1)
    u = gate_c * val
    pad = CONV_WIDTH // 2
    up = jnp.pad(u, ((0, 0), (pad, CONV_WIDTH - 1 - pad), (0, 0)))
    conv = sum(up[:, j:j + s] * w_conv[j] for j in range(CONV_WIDTH))
    return (gate_b * conv) @ w_out

def peer_mixer(h, w_query, sub_keys, w_up, w_down):
    b, s, d = h.shape
    xt = h.reshape(-1, PEER_TOK_CHUNK, d)
    keys32 = sub_keys.astype(jnp.float32)

    def chunk(xc):
        c = xc.shape[0]
        q = (xc @ w_query).reshape(c, PEER_HEADS, 2, PEER_HALF_DIM).astype(jnp.float32)
        sc = jnp.einsum('chpd,hpnd->chpn', q, keys32)
        sv, si = lax.top_k(sc, PEER_TOPK)
        cand = (sv[:, :, 0, :, None] + sv[:, :, 1, None, :]).reshape(c, PEER_HEADS, -1)
        cidx = (si[:, :, 0, :, None] * PEER_N_KEYS + si[:, :, 1, None, :]).reshape(c, PEER_HEADS, -1)
        best, pos = lax.top_k(cand, PEER_TOPK)
        eidx = jnp.take_along_axis(cidx, pos, axis=-1)
        g = jax.nn.softmax(best, axis=-1)
        u = w_up[eidx]
        a = jnp.einsum('cd,chkd->chk', xc, u).astype(jnp.float32)
        act = (jax.nn.gelu(a, approximate=False) * g).astype(xc.dtype)
        vv = w_down[eidx]
        return jnp.einsum('chk,chkd->cd', act, vv)

    return lax.map(chunk, xt).reshape(b, s, d)

def first_inputs(seed: int = 0) -> dict:
    key = jax.random.key(seed)
    ks = jax.random.split(key, 16)
    n_attn = (DEPTH + 1) // 2
    n_conv = DEPTH // 2
    d = D_MODEL
    nrm = jax.random.normal
    f32 = jnp.float32
    return {
        "x": nrm(ks[0], (BATCH, SEQ, d), f32),
        "norm_mix": 1.0 + 0.02 * nrm(ks[1], (DEPTH, d), f32),
        "norm_ffn": 1.0 + 0.02 * nrm(ks[2], (DEPTH, d), f32),
        "norm_final": 1.0 + 0.02 * nrm(ks[3], (d,), f32),
        "attn_w_qkv": nrm(ks[4], (n_attn, d, 3 * d), f32) * d ** -0.5,
        "attn_w_o": nrm(ks[5], (n_attn, d, d), f32) * d ** -0.5,
        "attn_rel_bias": 0.1 * nrm(ks[6], (n_attn, N_HEADS, 2 * MAX_WIN_ROWS - 1, 2 * WIN_COLS - 1), f32),
        "conv_w_in": nrm(ks[7], (n_conv, d, 3 * d), f32) * d ** -0.5,
        "conv_w_conv": nrm(ks[8], (n_conv, CONV_WIDTH, d), f32) * CONV_WIDTH ** -0.5,
        "conv_w_out": nrm(ks[9], (n_conv, d, d), f32) * d ** -0.5,
        "peer_w_query": nrm(ks[10], (DEPTH, d, PEER_HEADS * PEER_KEY_DIM), f32) * d ** -0.5,
        "peer_sub_keys": nrm(ks[11], (DEPTH, PEER_HEADS, 2, PEER_N_KEYS, PEER_HALF_DIM), f32) * PEER_HALF_DIM ** -0.5,
        "peer_w_up": nrm(ks[12], (DEPTH, PEER_N_EXPERTS, d), f32) * d ** -0.5,
        "peer_w_down": nrm(ks[13], (DEPTH, PEER_N_EXPERTS, d), f32) * (PEER_HEADS * PEER_TOPK) ** -0.5,
    }

def first_block(x, norm_mix, norm_ffn, norm_final, attn_w_qkv, attn_w_o, attn_rel_bias,
              conv_w_in, conv_w_conv, conv_w_out, peer_w_query, peer_sub_keys,
              peer_w_up, peer_w_down):
    h = x
    for i in range(DEPTH):
        j = i // N_MIXERS
        hn = rms_norm(h, norm_mix[i])
        if i % N_MIXERS == 0:
            h = h + neighbourhood_attention(hn, attn_w_qkv[j], attn_w_o[j], attn_rel_bias[j])
        else:
            h = h + short_conv_mixer(hn, conv_w_in[j], conv_w_conv[j], conv_w_out[j])
        hn = rms_norm(h, norm_ffn[i])
        h = h + peer_mixer(hn, peer_w_query[i], peer_sub_keys[i], peer_w_up[i], peer_w_down[i])
    return rms_norm(h, norm_final)


HEAD_DIM_2 = 64
ROPE_THETA = 10000.0
NORM_EPS = 1e-6
Q_BLOCK = 128
NEG_INF_2 = -1e30
FORCE_SELECT = 1e9

NSA_HEADS = 8
NSA_KV_GROUPS = 2
NSA_HEADS_PER_GROUP = NSA_HEADS // NSA_KV_GROUPS
NSA_CMP_LEN = 32
NSA_CMP_STRIDE = 16
NSA_SEL_LEN = 64
NSA_SEL_TOPK = 16
NSA_WINDOW = 512
NSA_BRANCHES = 3

MOBA_HEADS = 8
MOBA_BLOCK = 256
MOBA_TOPK = 3

MEM_LEN = 256
MEM_HEADS = 4

RET_HEADS = 4
RET_QK_DIM = D_MODEL // RET_HEADS
RET_V_DIM = 2 * D_MODEL // RET_HEADS
RET_CHUNK = 128

NSA_Q_W = NSA_HEADS * HEAD_DIM_2
NSA_KV_W = NSA_KV_GROUPS * HEAD_DIM_2
MOBA_W = MOBA_HEADS * HEAD_DIM_2
MEM_W = MEM_HEADS * HEAD_DIM_2
RET_QK_W = RET_HEADS * RET_QK_DIM
RET_V_W = RET_HEADS * RET_V_DIM

EVEN_SPLITS = (NSA_Q_W, NSA_KV_W, NSA_KV_W, NSA_KV_W, NSA_KV_W, NSA_KV_W, NSA_KV_W,
               NSA_BRANCHES * NSA_HEADS, NSA_Q_W,
               MOBA_W, MOBA_W, MOBA_W, MOBA_W,
               MEM_W, MEM_W)
ODD_SPLITS = (RET_QK_W, RET_QK_W, RET_V_W, RET_V_W, MEM_W, MEM_W)
EVEN_IN_W = sum(EVEN_SPLITS)
EVEN_OUT_W = NSA_Q_W + MOBA_W + MEM_W
ODD_IN_W = sum(ODD_SPLITS)
ODD_OUT_W = RET_V_W + MEM_W


def _split(h, sizes):
    cuts = np.cumsum(np.array(sizes))[:-1].tolist()
    return jnp.split(h, cuts, axis=-1)

def rms_norm_2(x, g):
    xf = x.astype(jnp.float32)
    y = xf * lax.rsqrt(jnp.mean(xf * xf, axis=-1, keepdims=True) + NORM_EPS)
    return (y * g.astype(jnp.float32)).astype(x.dtype)

def rotary_tables(positions, inv_freq):
    ang = positions.astype(jnp.float32)[..., None] * inv_freq
    return jnp.cos(ang), jnp.sin(ang)

def apply_rotary(x, cos, sin):
    x1, x2 = jnp.split(x, 2, axis=-1)
    c = cos[:, :, None, :].astype(x.dtype)
    s = sin[:, :, None, :].astype(x.dtype)
    return jnp.concatenate([x1 * c - x2 * s, x1 * s + x2 * c], axis=-1)

def masked_softmax(s, mask):
    s = jnp.where(mask, s.astype(jnp.float32), NEG_INF_2)
    m = jnp.max(s, axis=-1, keepdims=True)
    p = jnp.where(mask, jnp.exp(s - m), 0.0)
    return p / jnp.maximum(jnp.sum(p, axis=-1, keepdims=True), 1e-30)

def nsa_compress(a, pe, w1, w2):
    T = a.shape[1]
    n_cmp = (T - NSA_CMP_LEN) // NSA_CMP_STRIDE + 1
    idx = np.arange(n_cmp)[:, None] * NSA_CMP_STRIDE + np.arange(NSA_CMP_LEN)[None, :]
    blocks = a[:, idx] + pe[None, None, :, None, :].astype(a.dtype)
    hid = jax.nn.silu(jnp.einsum('bnlgd,lde->bnge', blocks, w1))
    return jnp.einsum('bnge,ef->bngf', hid, w2)

def nsa_attention(q, kc, vc, ks, vs, kw, vw, gates):
    Bsz, T = q.shape[0], q.shape[1]
    G, I, D = NSA_KV_GROUPS, NSA_HEADS_PER_GROUP, HEAD_DIM_2
    n_cmp = kc.shape[1]
    n_sel = T // NSA_SEL_LEN
    k_sel = min(NSA_SEL_TOPK, n_sel)
    scale = HEAD_DIM_2 ** -0.5
    cmp_start = jnp.arange(n_cmp) * NSA_CMP_STRIDE
    cmp_end = cmp_start + NSA_CMP_LEN - 1
    sel_start = jnp.arange(n_sel) * NSA_SEL_LEN
    overlap = ((cmp_start[:, None] < sel_start[None, :] + NSA_SEL_LEN) &
               (cmp_start[:, None] + NSA_CMP_LEN > sel_start[None, :])).astype(jnp.float32)
    ks_blk = ks.reshape(Bsz, n_sel, NSA_SEL_LEN, G, D).transpose(0, 3, 1, 2, 4)
    vs_blk = vs.reshape(Bsz, n_sel, NSA_SEL_LEN, G, D).transpose(0, 3, 1, 2, 4)
    kw_pad = jnp.pad(kw, ((0, 0), (NSA_WINDOW, 0), (0, 0), (0, 0)))
    vw_pad = jnp.pad(vw, ((0, 0), (NSA_WINDOW, 0), (0, 0), (0, 0)))
    b_idx = jnp.arange(Bsz)[:, None, None, None]
    g_idx = jnp.arange(G)[None, :, None, None]
    sel_blocks = jnp.arange(n_sel)

    def block(bi):
        t0 = bi * Q_BLOCK
        t = t0 + jnp.arange(Q_BLOCK)
        qb = lax.dynamic_slice_in_dim(q, t0, Q_BLOCK, axis=1).reshape(Bsz, Q_BLOCK, G, I, D)
        gb = lax.dynamic_slice_in_dim(gates, t0, Q_BLOCK, axis=1).reshape(Bsz, Q_BLOCK, NSA_BRANCHES, G, I)
        s_c = jnp.einsum('bqgid,bngd->bgiqn', qb, kc) * scale
        p_c = masked_softmax(s_c, cmp_end[None, :] <= t[:, None])
        o_c = jnp.einsum('bgiqn,bngd->bqgid', p_c.astype(vc.dtype), vc)
        imp = jnp.einsum('bgiqn,ns->bgqs', p_c, overlap)
        cur = t // NSA_SEL_LEN
        forced = ((sel_blocks[None, :] == 0) | (sel_blocks[None, :] == cur[:, None]) |
                  (sel_blocks[None, :] == cur[:, None] - 1))
        imp = jnp.where(forced, FORCE_SELECT, imp)
        imp = jnp.where(sel_blocks[None, :] <= cur[:, None], imp, NEG_INF_2)
        _, sel = lax.top_k(imp, k_sel)
        k_g = ks_blk[b_idx, g_idx, sel]
        v_g = vs_blk[b_idx, g_idx, sel]
        kpos = sel[..., None] * NSA_SEL_LEN + jnp.arange(NSA_SEL_LEN)
        mask_s = (kpos <= t[None, None, :, None, None]).reshape(Bsz, G, 1, Q_BLOCK, k_sel * NSA_SEL_LEN)
        s_s = jnp.einsum('bqgid,bgqkld->bgiqkl', qb, k_g).reshape(Bsz, G, I, Q_BLOCK, k_sel * NSA_SEL_LEN) * scale
        p_s = masked_softmax(s_s, mask_s).reshape(Bsz, G, I, Q_BLOCK, k_sel, NSA_SEL_LEN)
        o_s = jnp.einsum('bgiqkl,bgqkld->bqgid', p_s.astype(v_g.dtype), v_g)
        kwb = lax.dynamic_slice_in_dim(kw_pad, t0, Q_BLOCK + NSA_WINDOW, axis=1)
        vwb = lax.dynamic_slice_in_dim(vw_pad, t0, Q_BLOCK + NSA_WINDOW, axis=1)
        wpos = t0 - NSA_WINDOW + jnp.arange(Q_BLOCK + NSA_WINDOW)
        mask_w = ((wpos[None, :] <= t[:, None]) & (wpos[None, :] > t[:, None] - NSA_WINDOW) &
                  (wpos[None, :] >= 0))
        s_w = jnp.einsum('bqgid,bjgd->bgiqj', qb, kwb) * scale
        p_w = masked_softmax(s_w, mask_w)
        o_w = jnp.einsum('bgiqj,bjgd->bqgid', p_w.astype(vwb.dtype), vwb)
        o = (gb[:, :, 0, :, :, None] * o_c + gb[:, :, 1, :, :, None] * o_s +
             gb[:, :, 2, :, :, None] * o_w)
        return o.reshape(Bsz, Q_BLOCK, NSA_Q_W)

    out = lax.map(block, jnp.arange(T // Q_BLOCK))
    return out.transpose(1, 0, 2, 3).reshape(Bsz, T, NSA_Q_W)

def moba_attention(q, k, v):
    Bsz, T, H, D = q.shape
    n_blk = -(-T // MOBA_BLOCK)
    pad = n_blk * MOBA_BLOCK - T
    k_pad = jnp.pad(k, ((0, 0), (0, pad), (0, 0), (0, 0)))
    v_pad = jnp.pad(v, ((0, 0), (0, pad), (0, 0), (0, 0)))
    k_blk = k_pad.reshape(Bsz, n_blk, MOBA_BLOCK, H, D)
    k_mean = jnp.mean(k_blk.astype(jnp.float32), axis=2).astype(k.dtype)
    k_blk = k_blk.transpose(0, 3, 1, 2, 4)
    v_blk = v_pad.reshape(Bsz, n_blk, MOBA_BLOCK, H, D).transpose(0, 3, 1, 2, 4)
    top = max(1, min(MOBA_TOPK, n_blk - 1))
    scale = HEAD_DIM_2 ** -0.5
    b_idx = jnp.arange(Bsz)[:, None, None, None]
    h_idx = jnp.arange(H)[None, :, None, None]
    blocks = jnp.arange(n_blk)

    def block(bi):
        t0 = bi * Q_BLOCK
        t = t0 + jnp.arange(Q_BLOCK)
        cur = t0 // MOBA_BLOCK
        qb = lax.dynamic_slice_in_dim(q, t0, Q_BLOCK, axis=1)
        gate = jnp.einsum('bqhd,bnhd->bhqn', qb, k_mean).astype(jnp.float32)
        gate = jnp.where(blocks < cur, gate, NEG_INF_2)
        _, sel = lax.top_k(gate, top)
        k_g = k_blk[b_idx, h_idx, sel]
        v_g = v_blk[b_idx, h_idx, sel]
        s_sel = jnp.einsum('bqhd,bhqksd->bhqks', qb, k_g).reshape(Bsz, H, Q_BLOCK, top * MOBA_BLOCK)
        m_sel = jnp.broadcast_to((sel < cur)[..., None],
                                 (Bsz, H, Q_BLOCK, top, MOBA_BLOCK)).reshape(Bsz, H, Q_BLOCK, top * MOBA_BLOCK)
        k_own = lax.dynamic_slice_in_dim(k_pad, cur * MOBA_BLOCK, MOBA_BLOCK, axis=1)
        v_own = lax.dynamic_slice_in_dim(v_pad, cur * MOBA_BLOCK, MOBA_BLOCK, axis=1)
        s_own = jnp.einsum('bqhd,bshd->bhqs', qb, k_own)
        own_pos = cur * MOBA_BLOCK + jnp.arange(MOBA_BLOCK)
        m_own = jnp.broadcast_to(own_pos[None, :] <= t[:, None], (Bsz, H, Q_BLOCK, MOBA_BLOCK))
        p = masked_softmax(jnp.concatenate([s_sel, s_own], axis=-1) * scale,
                           jnp.concatenate([m_sel, m_own], axis=-1)).astype(v.dtype)
        p_sel = p[..., :top * MOBA_BLOCK].reshape(Bsz, H, Q_BLOCK, top, MOBA_BLOCK)
        p_own = p[..., top * MOBA_BLOCK:]
        o = (jnp.einsum('bhqks,bhqksd->bqhd', p_sel, v_g) +
             jnp.einsum('bhqs,bshd->bqhd', p_own, v_own))
        return o.reshape(Bsz, Q_BLOCK, H * D)

    out = lax.map(block, jnp.arange(T // Q_BLOCK))
    return out.transpose(1, 0, 2, 3).reshape(Bsz, T, H * D)

def memory_attention(q, mem_n, w_mem_kv):
    Bsz, T = q.shape[0], q.shape[1]
    k, v = jnp.split(mem_n @ w_mem_kv, 2, axis=-1)
    k = k.reshape(Bsz, -1, MEM_HEADS, HEAD_DIM_2)
    v = v.reshape(Bsz, -1, MEM_HEADS, HEAD_DIM_2)
    s = jnp.einsum('bthd,bmhd->bhtm', q, k).astype(jnp.float32) * (HEAD_DIM_2 ** -0.5)
    p = jax.nn.softmax(s, axis=-1).astype(v.dtype)
    return jnp.einsum('bhtm,bmhd->bthd', p, v).reshape(Bsz, T, MEM_W)

def retention(q, k, v):
    Bsz, T, H, _ = q.shape
    C = RET_CHUNK
    NC = T // C
    log_g = jnp.log(1.0 - 2.0 ** (-5.0 - jnp.arange(H, dtype=jnp.float32)))
    i = jnp.arange(C, dtype=jnp.float32)
    diff = i[:, None] - i[None, :]
    decay = jnp.where(diff >= 0, jnp.exp(jnp.maximum(diff, 0.0)[None] * log_g[:, None, None]), 0.0)
    q_decay = jnp.exp((i + 1.0)[None, :] * log_g[:, None])
    k_decay = jnp.exp((C - 1.0 - i)[None, :] * log_g[:, None])
    chunk_decay = jnp.exp(C * log_g)

    def to_chunks(a):
        return a.astype(jnp.float32).reshape(Bsz, NC, C, H, -1).transpose(1, 0, 3, 2, 4)

    def step(state, inp):
        qc, kc, vc = inp
        inner = jnp.einsum('bhid,bhjd->bhij', qc, kc) * decay
        o = (jnp.einsum('bhij,bhjv->bhiv', inner, vc) +
             jnp.einsum('bhid,bhdv->bhiv', qc, state) * q_decay[None, :, :, None])
        state = (state * chunk_decay[None, :, None, None] +
                 jnp.einsum('bhjd,bhjv->bhdv', kc * k_decay[None, :, :, None], vc))
        return state, o

    state0 = jnp.zeros((Bsz, H, q.shape[-1], v.shape[-1]), jnp.float32)
    _, o = lax.scan(step, state0, (to_chunks(q), to_chunks(k), to_chunks(v)))
    return o.transpose(1, 0, 3, 2, 4).reshape(Bsz, T, H, v.shape[-1])

def head_group_norm(o):
    mu = jnp.mean(o, axis=-1, keepdims=True)
    var = jnp.mean(jnp.square(o - mu), axis=-1, keepdims=True)
    return (o - mu) * lax.rsqrt(var + NORM_EPS)

def even_layer(x, mem_n, cos, sin, norm_g, w_in, gate_b, pe_k, w1_k, w2_k, pe_v, w1_v, w2_v, w_mem_kv, w_out):
    Bsz, T, _ = x.shape
    h = rms_norm_2(x, norm_g)
    (nq, nkc, nvc, nks, nvs, nkw, nvw, ng, nz, mq, mk, mv, mz, eq, ez) = _split(h @ w_in, EVEN_SPLITS)

    def heads(a):
        return a.reshape(Bsz, T, -1, HEAD_DIM_2)

    def rot(a):
        return apply_rotary(heads(a), cos, sin)

    kc = nsa_compress(rot(nkc), pe_k, w1_k, w2_k)
    vc = nsa_compress(heads(nvc), pe_v, w1_v, w2_v)
    gates = jax.nn.sigmoid(ng + gate_b).reshape(Bsz, T, NSA_BRANCHES, NSA_HEADS)
    a_out = nsa_attention(rot(nq), kc, vc, rot(nks), heads(nvs), rot(nkw), heads(nvw), gates)
    b_out = moba_attention(rot(mq), rot(mk), heads(mv))
    m_out = memory_attention(heads(eq), mem_n, w_mem_kv)
    y = jnp.concatenate([a_out * jax.nn.silu(nz), b_out * jax.nn.silu(mz),
                         m_out * jax.nn.silu(ez)], axis=-1) @ w_out
    return x + y

def odd_layer(x, mem_n, rcos, rsin, norm_g, w_in, w_mem_kv, w_out):
    Bsz, T, _ = x.shape
    h = rms_norm_2(x, norm_g)
    rq, rk, rv, rz, eq, ez = _split(h @ w_in, ODD_SPLITS)
    q = apply_rotary(rq.reshape(Bsz, T, RET_HEADS, RET_QK_DIM), rcos, rsin)
    k = apply_rotary(rk.reshape(Bsz, T, RET_HEADS, RET_QK_DIM), rcos, rsin) * (RET_QK_DIM ** -0.5)
    v = rv.reshape(Bsz, T, RET_HEADS, RET_V_DIM)
    r_out = head_group_norm(retention(q, k, v)).reshape(Bsz, T, RET_V_W).astype(x.dtype)
    m_out = memory_attention(eq.reshape(Bsz, T, MEM_HEADS, HEAD_DIM_2), mem_n, w_mem_kv)
    y = jnp.concatenate([r_out * jax.nn.silu(rz), m_out * jax.nn.silu(ez)], axis=-1) @ w_out
    return x + y

def second_inputs(seed: int = 0) -> dict:
    key = jax.random.key(seed)
    ks = jax.random.split(key, 24)

    def nrm(k, shape, scale):
        return jax.random.normal(k, shape, jnp.float32) * scale

    def gain(k):
        return 1.0 + nrm(k, (D_MODEL,), 0.02)

    x = nrm(ks[0], (BATCH, SEQ, D_MODEL), 1.0)
    mem = nrm(ks[1], (BATCH, MEM_LEN, D_MODEL), 1.0)
    positions = jnp.broadcast_to(jnp.arange(SEQ, dtype=jnp.int32)[None, :], (BATCH, SEQ))
    cmp_in = NSA_CMP_LEN * HEAD_DIM_2
    return {
        'x': x,
        'mem': mem,
        'positions': positions,
        'l0_norm_g': gain(ks[2]),
        'l0_w_in': nrm(ks[3], (D_MODEL, EVEN_IN_W), D_MODEL ** -0.5),
        'l0_nsa_gate_b': nrm(ks[4], (NSA_BRANCHES * NSA_HEADS,), 0.1),
        'l0_cmp_pe_k': nrm(ks[5], (NSA_CMP_LEN, HEAD_DIM_2), 0.1),
        'l0_cmp_w1_k': nrm(ks[6], (NSA_CMP_LEN, HEAD_DIM_2, HEAD_DIM_2), cmp_in ** -0.5),
        'l0_cmp_w2_k': nrm(ks[7], (HEAD_DIM_2, HEAD_DIM_2), HEAD_DIM_2 ** -0.5),
        'l0_cmp_pe_v': nrm(ks[8], (NSA_CMP_LEN, HEAD_DIM_2), 0.1),
        'l0_cmp_w1_v': nrm(ks[9], (NSA_CMP_LEN, HEAD_DIM_2, HEAD_DIM_2), cmp_in ** -0.5),
        'l0_cmp_w2_v': nrm(ks[10], (HEAD_DIM_2, HEAD_DIM_2), HEAD_DIM_2 ** -0.5),
        'l0_w_mem_kv': nrm(ks[11], (D_MODEL, 2 * MEM_W), D_MODEL ** -0.5),
        'l0_w_out': nrm(ks[12], (EVEN_OUT_W, D_MODEL), EVEN_OUT_W ** -0.5),
        'l1_norm_g': gain(ks[13]),
        'l1_w_in': nrm(ks[14], (D_MODEL, ODD_IN_W), D_MODEL ** -0.5),
        'l1_w_mem_kv': nrm(ks[15], (D_MODEL, 2 * MEM_W), D_MODEL ** -0.5),
        'l1_w_out': nrm(ks[16], (ODD_OUT_W, D_MODEL), ODD_OUT_W ** -0.5),
        'mem_norm_g': gain(ks[17]),
        'final_norm_g': gain(ks[18]),
    }

def second_block(x, mem, positions, l0_norm_g, l0_w_in, l0_nsa_gate_b, l0_cmp_pe_k, l0_cmp_w1_k, l0_cmp_w2_k,
              l0_cmp_pe_v, l0_cmp_w1_v, l0_cmp_w2_v, l0_w_mem_kv, l0_w_out,
              l1_norm_g, l1_w_in, l1_w_mem_kv, l1_w_out, mem_norm_g, final_norm_g):
    attn_inv = 1.0 / (ROPE_THETA ** (jnp.arange(0, HEAD_DIM_2, 2, dtype=jnp.float32) / HEAD_DIM_2))
    ret_inv = 1.0 / (ROPE_THETA ** jnp.linspace(0.0, 1.0, RET_QK_DIM // 2, dtype=jnp.float32))
    cos, sin = rotary_tables(positions, attn_inv)
    rcos, rsin = rotary_tables(positions, ret_inv)
    mem_n = rms_norm_2(mem, mem_norm_g)
    layer_params = (
        (l0_norm_g, l0_w_in, l0_nsa_gate_b, l0_cmp_pe_k, l0_cmp_w1_k, l0_cmp_w2_k,
         l0_cmp_pe_v, l0_cmp_w1_v, l0_cmp_w2_v, l0_w_mem_kv, l0_w_out),
        (l1_norm_g, l1_w_in, l1_w_mem_kv, l1_w_out),
    )
    for layer in range(DEPTH):
        if layer % 2 == 0:
            x = even_layer(x, mem_n, cos, sin, *layer_params[layer])
        else:
            x = odd_layer(x, mem_n, rcos, rsin, *layer_params[layer])
    return rms_norm_2(x, final_norm_g)


def setup_inputs(seed=0):
    out = dict(first_inputs(seed))
    for name, value in second_inputs(seed + 1).items():
        if name != "x":
            out[name + "_2"] = value
    return out


def reference(
    x, norm_mix, norm_ffn, norm_final, attn_w_qkv, attn_w_o, attn_rel_bias, conv_w_in,
    conv_w_conv, conv_w_out, peer_w_query, peer_sub_keys, peer_w_up, peer_w_down, mem_2,
    positions_2, l0_norm_g_2, l0_w_in_2, l0_nsa_gate_b_2, l0_cmp_pe_k_2, l0_cmp_w1_k_2,
    l0_cmp_w2_k_2, l0_cmp_pe_v_2, l0_cmp_w1_v_2, l0_cmp_w2_v_2, l0_w_mem_kv_2, l0_w_out_2,
    l1_norm_g_2, l1_w_in_2, l1_w_mem_kv_2, l1_w_out_2, mem_norm_g_2, final_norm_g_2,
):
    x = first_block(
        x, norm_mix, norm_ffn, norm_final, attn_w_qkv, attn_w_o, attn_rel_bias, conv_w_in,
        conv_w_conv, conv_w_out, peer_w_query, peer_sub_keys, peer_w_up, peer_w_down,
    )
    return second_block(
        x, mem_2, positions_2, l0_norm_g_2, l0_w_in_2, l0_nsa_gate_b_2, l0_cmp_pe_k_2,
        l0_cmp_w1_k_2, l0_cmp_w2_k_2, l0_cmp_pe_v_2, l0_cmp_w1_v_2, l0_cmp_w2_v_2,
        l0_w_mem_kv_2, l0_w_out_2, l1_norm_g_2, l1_w_in_2, l1_w_mem_kv_2, l1_w_out_2,
        mem_norm_g_2, final_norm_g_2,
    )


_drawn_inputs = setup_inputs


def setup_inputs(seed=0):
    import zlib

    import numpy as np

    out = dict(_drawn_inputs(seed))
    spreads = {}
    factors = {'norm_ffn': 4.047,
     'l0_norm_g_2': 8.0,
     'l0_nsa_gate_b_2': 8.0,
     'l0_cmp_pe_k_2': 8.0,
     'l0_cmp_pe_v_2': 3.538,
     'l1_norm_g_2': 2.773,
     'l1_w_mem_kv_2': 3.07,
     'mem_norm_g_2': 8.0,
     'final_norm_g_2': 2.791}
    for name, (base, spread) in spreads.items():
        noise = np.random.default_rng([zlib.crc32(name.encode()), seed]).standard_normal(out[name].shape)
        drawn = base * np.exp(spread * noise) if base else spread * noise
        out[name] = jnp.asarray(drawn.astype(out[name].dtype))
    for name, factor in factors.items():
        out[name] = (out[name] * factor).astype(out[name].dtype)
    return out
```

```python
import math
from contextlib import ExitStack

import numpy as np

import concourse.bass as bass
from concourse import mybir

F32 = mybir.dt.float32
U32 = mybir.dt.uint32
I32 = mybir.dt.int32
ALU = mybir.AluOpType
ACT = mybir.ActivationFunctionType
AX = mybir.AxisListType.X

P = 128
SEQ, D = 256, 1024
TT = SEQ // P
KT = D // P
CHUNK = 512
NEG = -1e30
LOWEST = -3.0e38
EPS = 1e-6

ROWS, GRID_W, WIN_COLS, MAX_WIN_ROWS = 4, 64, 16, 8
NA_HEADS, HEAD = 16, 64
PEER_HEADS, N_KEYS, TOPK = 8, 128, 16
HP = 2 * PEER_HEADS
HK = PEER_HEADS * TOPK

NSA_HEADS, NSA_GROUPS = 8, 2
CMP_LEN, CMP_STRIDE = 32, 16
N_CMP = (SEQ - CMP_LEN) // CMP_STRIDE + 1
MOBA_HEADS, MEM_HEADS = 8, 4
RET_HEADS, RET_QK, RET_V = 4, 256, 512
ROPE = 32
RET_ROPE = 128
ROPES = ROPE + RET_ROPE

EVEN = {}
_at = 0
for _name, _w in (("nq", 512), ("nkc", 128), ("nvc", 128), ("nks", 128), ("nvs", 128), ("nkw", 128),
                  ("nvw", 128), ("ng", 24), ("nz", 512), ("mq", 512), ("mk", 512), ("mv", 512),
                  ("mz", 512), ("eq", 256), ("ez", 256)):
    EVEN[_name] = _at
    _at += _w
EVEN_W = _at
EVEN_OUT = 1280
ODD = {"rq": 0, "rk": 1024, "rv": 2048, "rz": 4096, "eq": 6144, "ez": 6400}
ODD_W = 6656
ODD_OUT = 2304

NORMS = ("attn", "peer0", "conv", "peer1", "mem", "even", "odd")

ARENA = 32768
A_XS = 19968
L_QT, L_KT, L_V, L_BIAS, L_O, L_OT = 0, 2048, 4096, 6144, 14336, 16384
P_QT, P_SC, P_KEYS, P_TOP = 0, 4096, 8192, 10240
C_GATE, C_C, C_U, C_Y = 0, 2048, 4096, 8192
E_PROJ, E_T, E_ROPED = 0, 8752, 13872
E_NSA = A_XS
M_K, M_V = 23344, 24368
E_W1K, E_W1V, E_APE, E_TMP = 25392, 27440, 29488, 30448
ROPE_AT = 31472
E_YT = E_T
O_PROJ, O_ROPED, O_T = 0, 13312, 17408
O_DECAY = 22016
O_YT = 25392

RING = 2
DEBUG = False


class Jobs:

    BANKS = 8

    def __init__(self):
        self.first, self.n = {}, 0

    def add(self, name, count):
        self.first[name] = self.n
        self.n += count

    def of(self, name, k=0):
        return self.first[name] + k


def attention_order(heads):
    order = []
    for s in range(heads + 2):
        if s < heads:
            order.append(("S", s))
        if 0 <= s - 1 < heads:
            order.append(("T", s - 1))
        if s >= 2:
            order.append(("O", s - 2))
    return order


def build(nc, d, out):
    ctx = ExitStack()
    with ctx:
        def sb(name, shape, dt=F32):
            return ctx.enter_context(nc.sbuf_tensor(name, shape, dt))

        sems = {}

        def sem(name):
            if name not in sems:
                sems[name] = ctx.enter_context(nc.semaphore(name))
            return sems[name]

        resid = sb("resid", [P, TT, D])
        xT = sb("xT", [P, KT, SEQ])
        ring = sb("ring", [P, RING, KT * CHUNK])
        arena = sb("arena", [P, ARENA])
        aux = sb("aux", [P, 4096])
        ident = sb("ident", [P, P])
        gains = sb("gains", [P, len(NORMS), KT])
        small = sb("small", [P, 64])
        iota = sb("iota", [P, P])
        causal = sb("causal", [P, TT, SEQ])
        cmp_mask = sb("cmp_mask", [P, 2, TT, 16])
        convw = sb("convw", [P, KT, 3])
        inv_freq = sb("inv_freq", [P, ROPES])
        pos_i = sb("pos_i", [P, TT], I32)
        gate_b = sb("gate_b", [P, 24])
        pe_k = sb("pe_k", [P, CMP_LEN])
        pe_v = sb("pe_v", [P, CMP_LEN])
        w2k = sb("w2k", [P, 2, HEAD])
        w2v = sb("w2v", [P, HEAD])
        cmp_small = sb("cmp_small", [P, 320])
        ret_stats = sb("ret_stats", [P, RET_HEADS * TT, 2])
        bn = sb("bn", [P, 6])
        banks = [ctx.enter_context(nc.psum_tensor(f"bank{b}", [P, 512], F32)) for b in range(8)]

        def view(off, *shape):
            n = math.prod(shape)
            names = "abcd"[:len(shape)]
            v = arena[:, off:off + n]
            if len(shape) == 1:
                return v
            return v.rearrange(f"p ({' '.join(names)}) -> p {' '.join(names)}",
                               **{c: s for c, s in zip(names[1:], shape[1:])})

        def aux_view(off, *shape):
            n = math.prod(shape)
            names = "abcd"[:len(shape)]
            v = aux[:, off:off + n]
            if len(shape) == 1:
                return v
            return v.rearrange(f"p ({' '.join(names)}) -> p {' '.join(names)}",
                               **{c: s for c, s in zip(names[1:], shape[1:])})

        J = Jobs()
        chunks = []
        last_piece = []
        first_chunk = {}

        def weight(name, w, cols, pieces=(KT,)):
            first_chunk[name] = len(chunks)
            for c0 in range(0, cols, CHUNK):
                n, k0 = min(CHUNK, cols - c0), 0
                for kts in pieces:
                    src = w[k0 * P:(k0 + kts) * P, c0:c0 + n].rearrange("(k p) n -> p k n", p=P)
                    chunks.append((src, kts, n))
                    k0 += kts
                    last_piece.append(k0 == sum(pieces))

        weight("qkv", d["attn_w_qkv"], 3 * D)
        weight("wo", d["attn_w_o"], D)
        weight("query0", d["peer_w_query"][0], 2048)
        peer_after = [len(chunks)]
        weight("conv_in", d["conv_w_in"], 3 * D)
        weight("conv_out", d["conv_w_out"], D)
        weight("query1", d["peer_w_query"][1], 2048)
        peer_after.append(len(chunks))
        weight("mem0", d["l0_w_mem_kv_2"], 512)
        weight("mem1", d["l1_w_mem_kv_2"], 512)
        weight("even_in", d["l0_w_in_2"], EVEN_W)
        weight("even_out", d["l0_w_out_2"], D, (5, 5))
        weight("odd_in", d["l1_w_in_2"], ODD_W)
        weight("odd_out", d["l1_w_out_2"], D, (6, 6, 6))

        NA = attention_order(NA_HEADS)
        SEC = [("nsa_s", NSA_HEADS), ("nsa_w", NSA_HEADS), ("moba", MOBA_HEADS), ("mem_e", MEM_HEADS)]
        J.add("norm_attn", 4); J.add("qkv", 12); J.add("na", len(NA)); J.add("na_oT", 4); J.add("wo", 4)
        J.add("norm_peer0", 4); J.add("query0", 8); J.add("scores0", 8); J.add("idxT0", 2)
        J.add("norm_conv", 4); J.add("conv_in", 12); J.add("conv_out", 4)
        J.add("norm_peer1", 4); J.add("query1", 8); J.add("scores1", 8); J.add("idxT1", 2)
        J.add("norm_mem", 4); J.add("mem0", 2); J.add("mem1", 2)
        J.add("norm_even", 4); J.add("even_in", 18); J.add("even_T", 10)
        J.add("hid", 2); J.add("kvc", 2); J.add("cmp_S", 2); J.add("cmp_T", 1); J.add("cmp_O", 2)
        EV = attention_order(sum(n for _, n in SEC))
        J.add("ev", len(EV)); J.add("even_yT", 5); J.add("even_out", 4)
        J.add("norm_odd", 4); J.add("odd_in", 26); J.add("odd_T", 9)
        RET = [(k, h) for s in range(RET_HEADS + 1) for k, h in (("S", s), ("O", s - 1))
               if 0 <= h < RET_HEADS]
        ret_job, n = {}, 0
        for k, h in RET:
            ret_job[k, h] = n
            n += 1 if k == "S" else 2
        J.add("ret", n)
        OM = attention_order(MEM_HEADS)
        J.add("om", len(OM)); J.add("odd_yT", 9); J.add("odd_out", 4)

        chunk_job, piece_no = {}, {}
        for _name in ("qkv", "wo", "query0", "conv_in", "conv_out", "query1", "mem0", "mem1", "even_in",
                      "even_out", "odd_in", "odd_out"):
            c, k = first_chunk[_name], 0
            ends = [x for x in first_chunk.values() if x > c] + [len(chunks)]
            while c < min(ends):
                if last_piece[c]:
                    chunk_job[c] = J.of(_name, 2 * k + 1)
                    k += 1
                else:
                    piece_no[c] = len(piece_no) + 1
                c += 1

        def bank(j):
            return banks[j % 8]

        filled = [sem(f"bank{b}_filled") for b in range(8)]
        read = [sem(f"bank{b}_read") for b in range(8)]

        def wait_filled(eng, j):
            eng.wait_ge(filled[j % 8], j // 8 + 1)

        def wait_read(eng, j):
            eng.wait_ge(read[j % 8], j // 8 + 1)

        counts = {}

        def count(name):
            counts[name] = counts.get(name, 0) + 1
            return counts[name]

        const_loaded = sem("const_loaded")
        N_CONST = 17
        x_loaded = sem("x_loaded")
        landed = [sem(f"ring{s}_landed") for s in range(RING)]
        piece_used = sem("ring_piece_used")
        peer_up_landed = [sem(f"peer_up{s}_landed") for s in range(4)]
        peer_dn_landed = [sem(f"peer_dn{s}_landed") for s in range(4)]
        tile_used = sem("expert_tile_used")
        extra_loaded = {n: sem(f"{n}_loaded") for n in ("bias", "keys", "cmpw", "decay", "gain", "mem")}
        block_step = sem("residual_ready")
        RES = {n: i + 1 for i, n in enumerate(("wo", "peer0", "conv", "peer1", "between", "even", "odd"))}
        dve_step, act_step = sem("dve_step"), sem("act_step")
        norm_root, norm_scaled = sem("norm_root"), sem("norm_scaled")
        scores_shifted, weights_ready = sem("scores_shifted"), sem("weights_ready")
        top_ready, top_exp = sem("top_ready"), sem("top_exp")
        onehots, products, stored = sem("onehots_ready"), sem("token_products"), sem("router_stored")
        up_done, gelu_done, gated = sem("up_done"), sem("gelu_done"), sem("gated")
        y_ready = sem("gated_y_ready")
        roped = sem("roped")
        cmp_ready, cmp_exp_in, cmp_exp = sem("cmp_ready"), sem("cmp_exp_in"), sem("cmp_exp")
        tables = sem("rope_tables")
        stored_out = sem("output_stored")
        nsa_gate = sem("nsa_gate")
        silu_done = sem("silu_done")
        ret_ready = sem("ret_scores_ready")
        ret_root_in, ret_root = sem("ret_var"), sem("ret_root")
        conv_ready = sem("conv_ready")
        final_ready = sem("final_ready")
        gate_in = sem("gate_in")
        angle_ready = sem("angle_ready")

        def up_slot(s):
            return ring[:, s // 2, (s % 2) * 2048:(s % 2) * 2048 + 1024].rearrange("p (k e) -> p k e", k=KT)

        def down_slot(s):
            return ring[:, s // 2, (s % 2) * 2048 + 1024:(s % 2) * 2048 + 2048]

        idxT = aux_view(0, 3, SEQ)
        onehot = aux_view(768, 2, 2, 4, P)
        gelu_buf = aux_view(2816, 2, SEQ)
        gated_buf = aux_view(3328, 2, SEQ)
        s_buf = aux_view(0, 3, TT, SEQ)
        pT_buf = aux_view(1536, 2, 2, TT, P)
        gain_bc = aux_view(3072, D)
        router = view(0, N_KEYS, SEQ)

        eT = view(E_T, 20, SEQ)
        EQ, EMQ, EMK, EEQ, EKC, EVC, EKS, EKW = 0, 4, 8, 12, 14, 15, 16, 18
        ev_proj = view(E_PROJ, TT, EVEN_W)
        od_proj = view(O_PROJ, TT, ODD_W)
        mem_kT = view(M_K, 2, 2, SEQ)
        mem_v = view(M_V, 2, TT, 256)
        oT = view(O_T, 18, SEQ)

        def half(t, h, a, b):
            r = (h % 2) * HEAD
            return t[r:r + HEAD, h // 2, a:b]

        ev_heads = []
        for name, n in SEC:
            for h in range(n):
                r, g = (h % 2) * HEAD, h // 4
                if name in ("nsa_s", "nsa_w"):
                    kt = (EKS if name == "nsa_s" else EKW) + g
                    v0 = EVEN["nvs" if name == "nsa_s" else "nvw"] + g * HEAD
                    ev_heads.append((name, h, eT[r:r + HEAD, EQ + h // 2, :], eT[r:r + HEAD, kt, :],
                                     [ev_proj[:, k, v0:v0 + HEAD] for k in range(TT)]))
                elif name == "moba":
                    v0 = EVEN["mv"] + h * HEAD
                    ev_heads.append((name, h, eT[r:r + HEAD, EMQ + h // 2, :],
                                     eT[r:r + HEAD, EMK + h // 2, :],
                                     [ev_proj[:, k, v0:v0 + HEAD] for k in range(TT)]))
                else:
                    ev_heads.append((name, h, eT[r:r + HEAD, EEQ + h // 2, :],
                                     mem_kT[r:r + HEAD, 0, h // 2, :],
                                     [mem_v[:, 0, k, h * HEAD:(h + 1) * HEAD] for k in range(TT)]))
        na_q, na_k = view(L_QT, KT, SEQ), view(L_KT, KT, SEQ)
        na_v, na_o, na_oT = view(L_V, TT, D), view(L_O, TT, D), view(L_OT, KT, SEQ)
        na_bias = view(L_BIAS, NA_HEADS, TT, SEQ)
        na_heads = [("na", h, half(na_q, h, 0, SEQ), half(na_k, h, 0, SEQ),
                     [na_v[:, k, h * HEAD:(h + 1) * HEAD] for k in range(TT)]) for h in range(NA_HEADS)]
        om_heads = [("mem_o", h, oT[(h % 2) * HEAD:(h % 2) * HEAD + HEAD, 16 + h // 2, :],
                     mem_kT[(h % 2) * HEAD:(h % 2) * HEAD + HEAD, 1, h // 2, :],
                     [mem_v[:, 1, k, h * HEAD:(h + 1) * HEAD] for k in range(TT)]) for h in range(MEM_HEADS)]
        head_base = {"na": 0, "ev": NA_HEADS, "om": NA_HEADS + len(ev_heads)}
        ev_T_src = []
        rp = E_ROPED
        e_nq, e_mq, e_mk = view(rp, TT, 512), view(rp + 1024, TT, 512), view(rp + 2048, TT, 512)
        e_kc = view(rp + 3072, TT, 128)
        e_ks, e_kw = view(rp + 3328, TT, NSA_GROUPS, 2, HEAD), view(rp + 3840, TT, NSA_GROUPS, 2, HEAD)
        for i in range(4):
            ev_T_src.append([e_nq[:, t, i * P:(i + 1) * P] for t in range(TT)])
        for i in range(4):
            ev_T_src.append([e_mq[:, t, i * P:(i + 1) * P] for t in range(TT)])
        for i in range(4):
            ev_T_src.append([e_mk[:, t, i * P:(i + 1) * P] for t in range(TT)])
        for i in range(2):
            ev_T_src.append([ev_proj[:, t, EVEN["eq"] + i * P:EVEN["eq"] + (i + 1) * P] for t in range(TT)])
        ev_T_src.append([e_kc[:, t, :] for t in range(TT)])
        ev_T_src.append([ev_proj[:, t, EVEN["nvc"]:EVEN["nvc"] + P] for t in range(TT)])
        for g in range(NSA_GROUPS):
            ev_T_src.append([e_ks[:, t, g].rearrange("p a b -> p (a b)") for t in range(TT)])
        for g in range(NSA_GROUPS):
            ev_T_src.append([e_kw[:, t, g].rearrange("p a b -> p (a b)") for t in range(TT)])
        ev_y_src = [ev_proj[:, :, EVEN["nz"] + i * P:EVEN["nz"] + (i + 1) * P] for i in range(4)]
        ev_y_src += [ev_proj[:, :, EVEN["mz"] + i * P:EVEN["mz"] + (i + 1) * P] for i in range(4)]
        ev_y_src += [ev_proj[:, :, EVEN["ez"] + i * P:EVEN["ez"] + (i + 1) * P] for i in range(2)]
        ev_yT = view(E_YT, 10, SEQ)
        o_q, o_k = view(O_ROPED, TT, D), view(O_ROPED + 2048, TT, D)
        od_T_src = [[o_q[:, t, i * P:(i + 1) * P] for t in range(TT)] for i in range(8)]
        od_T_src += [[o_k[:, t, i * P:(i + 1) * P] for t in range(TT)] for i in range(8)]
        od_T_src += [[od_proj[:, t, ODD["eq"] + i * P:ODD["eq"] + (i + 1) * P] for t in range(TT)] for i in range(2)]
        od_y_src = [od_proj[:, :, ODD["rz"] + i * P:ODD["rz"] + (i + 1) * P] for i in range(16)]
        od_y_src += [od_proj[:, :, ODD["ez"] + i * P:ODD["ez"] + (i + 1) * P] for i in range(2)]
        od_yT = view(O_YT, 18, SEQ)
        decay = view(O_DECAY, RET_HEADS, SEQ)
        ret_buf = aux_view(0, 2, 3, P)
        cosT, sinT = view(ROPE_AT, TT, ROPES), view(ROPE_AT + TT * ROPES, TT, ROPES)
        cmp_T = {"k": eT[:, EKC, :], "v": eT[:, EVC, :]}
        w1 = {"k": view(E_W1K, CMP_LEN, HEAD), "v": view(E_W1V, CMP_LEN, HEAD)}
        ape = {"k": view(E_APE, CMP_LEN, N_CMP), "v": view(E_APE + CMP_LEN * N_CMP, CMP_LEN, N_CMP)}
        hid_sb = cmp_small[:, 0:32].rearrange("p (a n) -> p a n", a=2)
        kcT = cmp_small[:, 32:64].rearrange("p (g n) -> p g n", g=2)
        hid_rep = cmp_small[:, 64:192].rearrange("p (i n) -> p i n", i=4)
        cmp_s = view(E_TMP, TT, NSA_HEADS, 32)
        vbd = view(E_APE, NSA_GROUPS, 4, HEAD)
        cmp_pT = view(E_TMP + 512, TT, NSA_GROUPS, P)
        nsa_o = view(E_NSA, TT, 512)

        def top_out(t, i):
            return view(P_TOP, TT, 3, HK)[:, t, i, :]

        block = ctx.enter_context(nc.Block())

        @block.sync
        def _(sp):
            for t in range(TT):
                sp.dma_start(resid[:, t, :], d["x"][t * P:(t + 1) * P, :]).then_inc(x_loaded, 16)

            def wait_used(c):
                if c in chunk_job:
                    wait_filled(sp, chunk_job[c])
                else:
                    sp.wait_ge(piece_used, piece_no[c])

            def load_chunk(c):
                src, kts, n = chunks[c]
                if c >= RING:
                    wait_used(c - RING)
                dst = ring[:, c % RING, 0:kts * n].rearrange("p (k n) -> p k n", k=kts)
                sp.dma_start(dst, src).then_inc(landed[c % RING], 16)

            def load_experts(layer):
                wait_used(peer_after[layer] - 2)
                wait_used(peer_after[layer] - 1)
                base = layer * N_KEYS

                def tile(t, s):
                    up = d["w_upT"][bass.ds(base + t, 1)].rearrange("a p n -> p (a n)")
                    dn = d["w_down"][bass.ds(base + t, 1)].rearrange("a p n -> p (a n)")
                    sp.dma_start(ring[:, s // 2, (s % 2) * 2048:(s % 2) * 2048 + 1024], up)\
                        .then_inc(peer_up_landed[s], 16)
                    sp.dma_start(down_slot(s), dn).then_inc(peer_dn_landed[s], 16)

                for s in range(4):
                    tile(s, s)
                with sp.Fori(1, N_KEYS // 4) as i:
                    for s in range(4):
                        sp.wait_ge(tile_used, i * 4 + (base + s - 3))
                        tile(i * 4 + s, s)

            c = 0
            for layer in range(2):
                while c < peer_after[layer]:
                    load_chunk(c)
                    c += 1
                load_experts(layer)
                sp.wait_ge(tile_used, (layer + 1) * N_KEYS)
            while c < len(chunks):
                load_chunk(c)
                c += 1
            sp.wait_ge(final_ready, 1)
            for t in range(TT):
                sp.dma_start(out[t * P:(t + 1) * P, :], resid[:, t, :]).then_inc(stored_out, 16)
            sp.wait_ge(stored_out, 16 * TT)

        @block.gpsimd
        def _(pool):
            def const(dst, src):
                pool.dma_start(dst, src).then_inc(const_loaded, 16)

            const(ident[:], d["c_ident"])
            const(gains[:], d["gains"])
            pool.dma_start(na_bias, d["na_bias"]).then_inc(extra_loaded["bias"], 16)
            const(iota[:], d["c_iota"].partition_broadcast(P))
            const(causal[:], d["c_causal"])
            const(cmp_mask[:], d["c_cmp_mask"])
            const(convw[:], d["conv_w"])
            const(inv_freq[:], d["c_inv_freq"].partition_broadcast(P))
            const(pos_i[:], d["positions"])
            const(gate_b[:], d["gate_b"].partition_broadcast(P))
            const(pe_k[:], d["pe_k"])
            const(pe_v[:], d["pe_v"])
            for dup in range(2):
                const(w2k[dup * HEAD:(dup + 1) * HEAD, 0, :], d["w2_k"])
                const(w2k[dup * HEAD:(dup + 1) * HEAD, 1, :], d["w2_k"])
            const(w2v[0:HEAD, :], d["w2_v"])
            const(w2v[HEAD:P, :], d["w2_v"])
            def dump(name):
                if DEBUG:
                    pool.wait_ge(block_step, RES[name])
                    pool.dma_start(d["dbg"][RES[name] - 1], resid[:]).then_inc(sem("dbg"), 16)

            for layer, done in enumerate(("wo", "conv")):
                pool.wait_ge(block_step, RES[done])
                pool.dma_start(view(P_KEYS, HP, N_KEYS), d["keysT"][layer])\
                    .then_inc(extra_loaded["keys"], 16)
                dump(done)
                dump(("peer0", "peer1")[layer])
            pool.wait_ge(block_step, RES["peer1"])
            for t in range(TT):
                pool.dma_start(view(0, TT, D)[:, t, :], d["mem"][t * P:(t + 1) * P, :])\
                    .then_inc(extra_loaded["mem"], 16)
            pool.dma_start(gain_bc, d["norm_final"].partition_broadcast(P)).then_inc(extra_loaded["gain"], 16)
            for kv in "kv":
                for g in range(NSA_GROUPS):
                    pool.dma_start(w1[kv][g * HEAD:(g + 1) * HEAD], d[f"w1_{kv}"])\
                        .then_inc(extra_loaded["cmpw"], 16)
            dump("between")
            pool.wait_ge(block_step, RES["even"])
            pool.dma_start(decay, d["c_decay"]).then_inc(extra_loaded["decay"], 16)
            pool.dma_start(gain_bc, d["final_norm"].partition_broadcast(P)).then_inc(extra_loaded["gain"], 16)
            dump("even")
            dump("odd")

        @block.tensor
        def _(pe):
            pe.wait_ge(const_loaded, 16 * N_CONST)
            at = [0]

            def take(name, k):
                j = J.of(name, k)
                assert j == at[0], (name, k, j, at[0])
                at[0] += 1
                if j >= 8:
                    pe.wait_ge(read[j % 8], j // 8)
                return j

            def done(ins, j):
                ins.then_inc(filled[j % 8], 1)

            chunk = [0]

            def norm(name):
                for g in range(4):
                    j = take(f"norm_{name}", g)
                    t, k0 = g // 2, (g % 2) * 4
                    if g % 2 == 0:
                        pe.wait_ge(norm_scaled, count("pe_norm"))
                    xs = view(A_XS, TT, D)
                    for k in range(4):
                        last = pe.transpose(bank(j)[:, k * P:(k + 1) * P],
                                            xs[:, t, (k0 + k) * P:(k0 + k + 1) * P], ident[:])
                    done(last, j)

            def landed_chunk(c):
                pe.wait_ge(landed[c % RING], 16 * (c // RING + 1))
                src, kts, n = chunks[c]
                return ring[:, c % RING, 0:kts * n].rearrange("p (k n) -> p k n", k=kts)

            def project(name, forms, lhs, pieces=(KT,), k=0):
                for form in forms:
                    js = [take(name, k), take(name, k + 1)]
                    k += 2
                    kt0, total = 0, sum(pieces)
                    for kts in pieces:
                        w = landed_chunk(chunk[0])
                        n = chunks[chunk[0]][2]
                        for b in range(2):
                            if form == "N":
                                for kk in range(kts):
                                    last = pe.matmul(bank(js[b])[:, 0:n], lhsT=lhs[:, kt0 + kk, b * P:(b + 1) * P],
                                                     rhs=w[:, kk, :], start=(kt0 + kk == 0), stop=(kt0 + kk == total - 1))
                            elif form == "T" or b == 0:
                                for m in range(2):
                                    for kk in range(kts):
                                        c0 = (2 * b + m) * P
                                        last = pe.matmul(bank(js[b])[:, m * SEQ:(m + 1) * SEQ], lhsT=w[:, kk, c0:c0 + P],
                                                         rhs=lhs[:, kk, :], start=(kk == 0), stop=(kk == kts - 1))
                            else:
                                for m in range(2):
                                    for kk in range(kts):
                                        last = pe.matmul(bank(js[b])[:, m * 256:(m + 1) * 256],
                                                         lhsT=lhs[:, kk, m * P:(m + 1) * P], rhs=w[:, kk, 256:512],
                                                         start=(kk == 0), stop=(kk == kts - 1))
                            if kt0 + kts == total:
                                done(last, js[b])
                        if kt0 + kts < total:
                            last.then_inc(piece_used, 1)
                        kt0 += kts
                        chunk[0] += 1
                return k

            def transposes(name, groups, ready):
                for k, group in enumerate(groups):
                    j = take(name, k)
                    ready(k)
                    for q, src in enumerate(group):
                        last = pe.transpose(bank(j)[:, q * P:(q + 1) * P], src, ident[:])
                    done(last, j)

            def attention(name, order, heads, base):
                for k, (kind, a) in enumerate(order):
                    j = take(name, k)
                    _, _, qT, kT, v = heads[a]
                    if kind == "S":
                        for t in range(TT):
                            last = pe.matmul(bank(j)[:, t * SEQ:(t + 1) * SEQ], lhsT=qT[:, t * P:(t + 1) * P], rhs=kT,
                                             start=True, stop=True)
                    elif kind == "T":
                        pe.wait_ge(weights_ready, base + a + 1)
                        for kt in range(2):
                            for t in range(TT):
                                q = kt * TT + t
                                last = pe.transpose(bank(j)[:, q * P:(q + 1) * P],
                                                    s_buf[:, (base + a) % 3, t, kt * P:(kt + 1) * P], ident[:])
                    else:
                        wait_read(pe, J.of(name, order.index(("T", a))))
                        for t in range(TT):
                            for kt in range(2):
                                last = pe.matmul(bank(j)[:, t * HEAD:(t + 1) * HEAD],
                                                 lhsT=pT_buf[:, (base + a) % 2, kt, t, :], rhs=v[kt],
                                                 start=(kt == 0), stop=(kt == 1))
                    done(last, j)

            def peer(layer):
                for g in range(4):
                    wait_read(pe, J.of(f"norm_peer{layer}", g))
                project(f"query{layer}", "TTTT", xT)
                qT = view(P_QT, HP, SEQ)
                keys = view(P_KEYS, HP, N_KEYS)
                pe.wait_ge(extra_loaded["keys"], 16 * (layer + 1))
                for k in range(8):
                    t, q = k // 4, k % 4
                    j = take(f"scores{layer}", k)
                    for i in range(2):
                        wait_read(pe, J.of(f"query{layer}", 2 * q + i))
                    for i in range(4):
                        last = pe.matmul(bank(j)[:, i * P:(i + 1) * P], lhsT=qT[:, 4 * q + i, t * P:(t + 1) * P],
                                         rhs=keys[:, 4 * q + i, :], start=True, stop=True)
                    done(last, j)
                for t in range(TT):
                    j = take(f"idxT{layer}", t)
                    pe.wait_ge(top_ready, 2 * (TT * layer + t) + 2)
                    for i in range(3):
                        last = pe.transpose(bank(j)[:, i * P:(i + 1) * P], top_out(t, i), ident[:])
                    done(last, j)
                for j in range(at[0] - 8, at[0]):
                    wait_read(pe, j)
                n0 = 64 * layer

                def quad(i, s, first):
                    pe.wait_ge(onehots, i + (n0 + 1))
                    if not first:
                        pe.wait_ge(stored, i + (n0 - 1))
                    for c in range(4):
                        last = pe.matmul(banks[s][:, c * P:(c + 1) * P], lhsT=onehot[:, s, 1, c, :],
                                         rhs=onehot[:, s, 0, c, :], start=True, stop=True)
                    last.then_inc(products, 1)

                quad(0, 0, True)
                quad(1, 1, True)
                with pe.Fori(1, 32) as i:
                    for s in range(2):
                        quad(i * 2 + s, s, False)
                pe.wait_ge(stored, n0 + 64)
                base = layer * N_KEYS

                def up(t, b, s, n):
                    pe.wait_ge(peer_up_landed[s], n)
                    if not (isinstance(t, int) and t < 2):
                        pe.wait_ge(gelu_done, t + (base - 1))
                    w = up_slot(s)
                    for k in range(KT):
                        last = pe.matmul(banks[b][:, 0:SEQ], lhsT=w[:, k, :], rhs=xT[:, k, :],
                                         start=(k == 0), stop=(k == KT - 1))
                    last.then_inc(up_done, 1)

                def down(t, b, s, n, start=False, stop=False):
                    pe.wait_ge(peer_dn_landed[s], n)
                    pe.wait_ge(gated, t + (base + 1))
                    w = down_slot(s)
                    for m in range(TT):
                        for h in range(2):
                            last = pe.matmul(banks[4 + 2 * m + h][:, :], lhsT=gated_buf[:, b, m * P:(m + 1) * P],
                                             rhs=w[:, h * 512:(h + 1) * 512], start=start, stop=stop)
                    last.then_inc(tile_used, 1)

                per = 16 * (N_KEYS // 4)
                for t in range(4):
                    up(t, t % 2, t, layer * per + 16)
                    if t:
                        down(t - 1, (t - 1) % 2, t - 1, layer * per + 16, start=(t == 1))
                with pe.Fori(1, N_KEYS // 4) as i:
                    for s in range(4):
                        up(i * 4 + s, s % 2, s, i * 16 + (layer * per + 16))
                        if s:
                            down(i * 4 + (s - 1), (s - 1) % 2, s - 1, i * 16 + (layer * per + 16))
                        else:
                            down(i * 4 - 1, 1, 3, i * 16 + layer * per)
                down(N_KEYS - 1, 1, 3, (layer + 1) * per, stop=True)

            norm("attn")
            for g in range(4):
                wait_read(pe, J.of("norm_attn", g))
            project("qkv", "TTTTNN", xT)
            for k in range(12):
                wait_read(pe, J.of("qkv", k))
            attention("na", NA, na_heads, head_base["na"])
            for a in range(NA_HEADS):
                wait_read(pe, J.of("na", NA.index(("O", a))))
            transposes("na_oT", [[na_o[:, t, i * P:(i + 1) * P] for i in (2 * g, 2 * g + 1) for t in range(TT)]
                                 for g in range(4)], lambda k: None)
            for g in range(4):
                wait_read(pe, J.of("na_oT", g))
            project("wo", "NN", na_oT)
            norm("peer0")
            peer(0)
            norm("conv")
            for g in range(4):
                wait_read(pe, J.of("norm_conv", g))
            project("conv_in", "TTTTTT", xT)
            pe.wait_ge(conv_ready, 1)
            project("conv_out", "NN", view(C_Y, KT, SEQ))
            norm("peer1")
            peer(1)
            for _ in range(TT):
                count("pe_norm")
            norm("mem")
            for g in range(4):
                wait_read(pe, J.of("norm_mem", g))
            memT = view(E_T, KT, SEQ)
            project("mem0", "M", memT)
            project("mem1", "M", memT)
            norm("even")
            for g in range(4):
                wait_read(pe, J.of("norm_even", g))
            project("even_in", "N" * 9, xT)
            for k in range(18):
                wait_read(pe, J.of("even_in", k))
            pe.wait_ge(roped, 1)
            transposes("even_T", [[ev_T_src[i][t] for i in (2 * g, 2 * g + 1) for t in range(TT)] for g in range(10)],
                       lambda k: None)
            pe.wait_ge(extra_loaded["cmpw"], 64)
            pe.wait_ge(cmp_ready, 1)
            for g in range(NSA_GROUPS):
                j = take("hid", g)
                r = g * HEAD
                for i, kv in enumerate("kv"):
                    for l in range(CMP_LEN):
                        last = pe.matmul(bank(j)[r:r + HEAD, i * 16:i * 16 + N_CMP], lhsT=w1[kv][r:r + HEAD, l, :],
                                         rhs=ape[kv][r:r + HEAD, l, :], start=(l == 0), stop=(l == CMP_LEN - 1))
                done(last, j)
            pe.wait_ge(cmp_ready, 2)
            for g in range(NSA_GROUPS):
                j = take("kvc", g)
                r = g * HEAD
                pe.matmul(bank(j)[:, 0:N_CMP], lhsT=w2k[r:r + HEAD].rearrange("p a b -> p (a b)"),
                          rhs=hid_sb[r:r + HEAD, 0, 0:N_CMP], start=True, stop=True)
                last = pe.matmul(bank(j)[:, 64:64 + HEAD], lhsT=hid_rep[r:r + HEAD].rearrange("p a b -> p (a b)"),
                                 rhs=w2v[r:r + HEAD, :], start=True, stop=True)
                done(last, j)
            for g in range(NSA_GROUPS):
                wait_read(pe, J.of("kvc", g))
            for g in range(10):
                wait_read(pe, J.of("even_T", g))
            for par in range(2):
                j = take("cmp_S", par)
                for hh in range(4):
                    h = 2 * hh + par
                    for t in range(TT):
                        c0 = (hh * TT + t) * 16
                        last = pe.matmul(bank(j)[:, c0:c0 + N_CMP],
                                         lhsT=eT[par * HEAD:par * HEAD + HEAD, EQ + hh, t * P:(t + 1) * P],
                                         rhs=kcT[par * HEAD:par * HEAD + HEAD, h // 4, 0:N_CMP], start=True, stop=True)
                done(last, j)
            j = take("cmp_T", 0)
            pe.wait_ge(cmp_ready, 3)
            for t in range(TT):
                for g in range(NSA_GROUPS):
                    q = t * 2 + g
                    last = pe.transpose(bank(j)[:, q * P:(q + 1) * P],
                                        cmp_s[:, t, 4 * g:4 * g + 4, :].rearrange("p a b -> p (a b)"), ident[:])
            done(last, j)
            wait_read(pe, J.of("cmp_T"))
            for t in range(TT):
                j = take("cmp_O", t)
                for g in range(NSA_GROUPS):
                    last = pe.matmul(bank(j)[:, g * 256:(g + 1) * 256], lhsT=cmp_pT[:, t, g, :],
                                     rhs=vbd[:, g].rearrange("p a b -> p (a b)"), start=True, stop=True)
                done(last, j)
            attention("ev", EV, ev_heads, head_base["ev"])
            pe.wait_ge(y_ready, 1)
            transposes("even_yT", [[ev_y_src[i][:, t, :] for i in (2 * g, 2 * g + 1) for t in range(TT)] for g in range(5)],
                       lambda k: None)
            for g in range(5):
                wait_read(pe, J.of("even_yT", g))
            project("even_out", "NN", ev_yT, (5, 5))
            norm("odd")
            for g in range(4):
                wait_read(pe, J.of("norm_odd", g))
            project("odd_in", "N" * 13, xT)
            for k in range(26):
                wait_read(pe, J.of("odd_in", k))
            pe.wait_ge(roped, 2)
            transposes("odd_T", [[od_T_src[i][t] for i in (2 * g, 2 * g + 1) for t in range(TT)] for g in range(9)],
                       lambda k: None)
            for g in range(9):
                wait_read(pe, J.of("odd_T", g))
            for kind, h in RET:
                j = take("ret", ret_job[kind, h])
                if kind == "S":
                    for kt, q0, q1, c0 in ((0, 0, SEQ, 0), (1, P, SEQ, SEQ)):
                        for dd in range(2):
                            last = pe.matmul(bank(j)[:, c0:c0 + q1 - q0], lhsT=oT[:, 8 + 2 * h + dd, kt * P:(kt + 1) * P],
                                             rhs=oT[:, 2 * h + dd, q0:q1], start=(dd == 0), stop=(dd == 1))
                    done(last, j)
                else:
                    pe.wait_ge(ret_ready, h + 1)
                    for t in range(TT):
                        if t:
                            j = take("ret", ret_job[kind, h] + 1)
                        for kt in range(t + 1):
                            last = pe.matmul(bank(j)[:, :], lhsT=ret_buf[:, h % 2, t if kt == 0 else 2, :],
                                             rhs=od_proj[:, kt, ODD["rv"] + h * RET_V:ODD["rv"] + (h + 1) * RET_V],
                                             start=(kt == 0), stop=(kt == t))
                        done(last, j)
            attention("om", OM, om_heads, head_base["om"])
            pe.wait_ge(y_ready, 2)
            transposes("odd_yT", [[od_y_src[i][:, t, :] for i in (2 * g, 2 * g + 1) for t in range(TT)] for g in range(9)],
                       lambda k: None)
            for g in range(9):
                wait_read(pe, J.of("odd_yT", g))
            project("odd_out", "NN", od_yT, (6, 6, 6))
            assert at[0] == J.n

        @block.scalar
        def _(act):
            def step(ins):
                ins.then_inc(act_step, 1)
                act.wait_ge(act_step, count("act"))

            def evac(dst, j, src=None, func=ACT.Copy, scale=1.0):
                wait_filled(act, j)
                act.activation(dst, bank(j)[:, :] if src is None else src, func, scale=scale).then_inc(read[j % 8], 1)
                wait_read(act, j)

            eps = small[:, 60:61]

            def norm(src, ready):
                ready()
                n = count("norm_a")
                for t in range(TT):
                    step(act.activation(view(A_XS, TT, D)[:, t, :], src[:, t, :], ACT.Square,
                                        accum_out=small[:, t:t + 1]))
                act.activation(small[:, 2:4], small[:, 0:2], ACT.Sqrt, bias=eps, scale=1.0 / D).then_inc(norm_root, 1)
                act.wait_ge(norm_root, n)

            def attention(name, order, heads, base):
                for kind, a in order:
                    n = base + a
                    if kind == "S":
                        act.wait_ge(scores_shifted, n + 1)
                        for t in range(TT):
                            ins = act.activation(s_buf[:, n % 3, t, :], s_buf[:, n % 3, t, :], ACT.Exp,
                                                 bias=small[:, 8 + (n % 4) * 2 + t:9 + (n % 4) * 2 + t],
                                                 accum_out=small[:, 16 + (n % 4) * 2 + t:17 + (n % 4) * 2 + t])
                            if t == 0:
                                step(ins)
                        ins.then_inc(weights_ready, 1)
                        act.wait_ge(weights_ready, n + 1)
                    elif kind == "T":
                        evac(pT_buf[:, n % 2].rearrange("p a b c -> p (a b c)"), J.of(name, order.index(("T", a))))

            def peer(layer):
                qT = view(P_QT, HP, SEQ)
                for k in range(8):
                    evac(qT[:, 2 * k:2 * k + 2, :].rearrange("p a b -> p (a b)"), J.of(f"query{layer}", k))
                sc = view(P_SC, TT, HP, N_KEYS)
                for k in range(8):
                    t, q = k // 4, k % 4
                    evac(sc[:, t, 4 * q:4 * q + 4, :].rearrange("p a b -> p (a b)"), J.of(f"scores{layer}", k))
                for t in range(TT):
                    n = TT * layer + t
                    act.wait_ge(top_ready, 2 * n + 1)
                    g = top_out(t, 2)
                    act.activation(g, g, ACT.Exp).then_inc(top_exp, 1)
                    act.wait_ge(top_exp, n + 1)
                for t in range(TT):
                    evac(idxT[:, :, t * P:(t + 1) * P], J.of(f"idxT{layer}", t),
                         bank(J.of(f"idxT{layer}", t))[:, 0:3 * P].rearrange("p (a b) -> p a b", a=3))
                n0 = 64 * layer
                by_pos = router.rearrange("p i (q c) -> p i q c", c=4)

                def store(i, s):
                    act.wait_ge(products, i + (n0 + 1))
                    dst = by_pos[:, :, bass.ds(i, 1), :].rearrange("p i a c -> p i (a c)")
                    act.activation(dst, banks[s][:, :].rearrange("p (c i) -> p i c", c=4), ACT.Copy).then_inc(stored, 1)

                with act.Fori(0, 32) as i:
                    for s in range(2):
                        store(i * 2 + s, s)
                base = layer * N_KEYS

                def gelu(t, b):
                    act.wait_ge(up_done, t + (base + 1))
                    if not (isinstance(t, int) and t < 2):
                        act.wait_ge(gated, t + (base - 1))
                    act.activation(gelu_buf[:, b, :], banks[b][:, 0:SEQ], ACT.Gelu).then_inc(gelu_done, 1)

                gelu(0, 0)
                gelu(1, 1)
                with act.Fori(1, N_KEYS // 2) as i:
                    for b in range(2):
                        gelu(i * 2 + b, b)

            def residual(n):
                return lambda: act.wait_ge(block_step, n)

            def first():
                act.wait_ge(x_loaded, 16 * TT)
                act.wait_ge(dve_step, 1)

            norm(resid, first)
            for k in range(4):
                evac(na_q[:, 2 * k:2 * k + 2, :].rearrange("p a b -> p (a b)"), J.of("qkv", k), scale=HEAD ** -0.5)
            for k in range(8, 12):
                c, t = (k - 8) // 2, k % 2
                evac(na_v[:, t, c * CHUNK:(c + 1) * CHUNK], J.of("qkv", k))
            attention("na", NA, na_heads, head_base["na"])
            for g in range(4):
                evac(na_oT[:, 2 * g:2 * g + 2, :].rearrange("p a b -> p (a b)"), J.of("na_oT", g))
            norm(resid, residual(RES["wo"]))
            peer(0)
            norm(resid, residual(RES["peer0"]))
            for k in range(8):
                dst = view(C_GATE if k < 4 else C_C, KT, SEQ)
                evac(dst[:, 2 * (k % 4):2 * (k % 4) + 2, :].rearrange("p a b -> p (a b)"), J.of("conv_in", k))
            norm(resid, residual(RES["conv"]))
            peer(1)
            norm(resid, residual(RES["peer1"]))
            mem_rows = view(0, TT, D)

            def mem_in():
                act.wait_ge(block_step, RES["between"])
                act.wait_ge(extra_loaded["mem"], 16 * TT)

            norm(mem_rows, mem_in)
            for l in range(2):
                evac(mem_kT[:, l].rearrange("p a b -> p (a b)"), J.of(f"mem{l}", 0))
                evac(mem_v[:, l].rearrange("p a b -> p (a b)"), J.of(f"mem{l}", 1))
            norm(resid, residual(RES["between"]))
            act.wait_ge(angle_ready, 1)
            act.activation(view(ROPE_AT, 2 * TT * ROPES), view(ROPE_AT, 2 * TT * ROPES), ACT.Sin).then_inc(tables, 1)
            act.wait_ge(tables, 1)
            for k in range(18):
                c, t = k // 2, k % 2
                n = min(CHUNK, EVEN_W - c * CHUNK)
                j = J.of("even_in", k)
                evac(ev_proj[:, t, c * CHUNK:c * CHUNK + n], j, bank(j)[:, 0:n])
            for name, w in (("nz", 512), ("mz", 512), ("ez", 256)):
                z = ev_proj[:, :, EVEN[name]:EVEN[name] + w]
                act.activation(z, z, ACT.Silu).then_inc(silu_done, 1)
            act.wait_ge(silu_done, 3)
            act.wait_ge(gate_in, 1)
            gates = ev_proj[:, :, EVEN["ng"]:EVEN["ng"] + 24]
            act.activation(gates, gates, ACT.Sigmoid).then_inc(nsa_gate, 1)
            for k in range(10):
                if k == 7:
                    continue
                evac(eT[:, 2 * k:2 * k + 2, :].rearrange("p a b -> p (a b)"), J.of("even_T", k))
            for g in range(NSA_GROUPS):
                r = g * HEAD
                j = J.of("hid", g)
                evac(hid_sb[r:r + HEAD, :, 0:N_CMP], j, bank(j)[r:r + HEAD, 0:32].rearrange("p (a n) -> p a n", a=2)[:, :, 0:N_CMP],
                     ACT.Silu)
            act.wait_ge(cmp_exp_in, 1)
            cs = cmp_s.rearrange("p t h n -> p (t h) n")[:, :, 0:N_CMP]
            act.activation(cs, cs, ACT.Exp).then_inc(cmp_exp, 1)
            evac(cmp_pT.rearrange("p t g q -> p (t g q)"), J.of("cmp_T"))
            attention("ev", EV, ev_heads, head_base["ev"])
            for g in range(5):
                evac(ev_yT[:, 2 * g:2 * g + 2, :].rearrange("p a b -> p (a b)"), J.of("even_yT", g))
            norm(resid, residual(RES["even"]))
            for k in range(26):
                c, t = k // 2, k % 2
                evac(od_proj[:, t, c * CHUNK:(c + 1) * CHUNK], J.of("odd_in", k))
            for t in range(TT):
                z = od_proj[:, t, ODD["rz"]:ODD["rz"] + RET_HEADS * RET_V]
                act.activation(z, z, ACT.Silu).then_inc(silu_done, 1)
            z = od_proj[:, :, ODD["ez"]:ODD["ez"] + 256]
            act.activation(z, z, ACT.Silu).then_inc(silu_done, 1)
            for k in range(9):
                evac(oT[:, 2 * k:2 * k + 2, :].rearrange("p a b -> p (a b)"), J.of("odd_T", k))
            for h in range(RET_HEADS):
                for t in range(TT):
                    n = TT * h + t
                    act.wait_ge(ret_root_in, n + 1)
                    act.activation(small[:, 30 + n:31 + n], ret_stats[:, n, 1:2], ACT.Sqrt, bias=eps).then_inc(ret_root, 1)
            attention("om", OM, om_heads, head_base["om"])
            for g in range(9):
                evac(od_yT[:, 2 * g:2 * g + 2, :].rearrange("p a b -> p (a b)"), J.of("odd_yT", g))
            norm(resid, residual(RES["odd"]))

        @block.vector
        def _(dve):
            def step(ins):
                ins.then_inc(dve_step, 1)
                dve.wait_ge(dve_step, count("dve"))

            def tell(ins, s, n):
                ins.then_inc(s, 1)
                dve.wait_ge(s, n)

            def read_out(ins, j):
                ins.then_inc(read[j % 8], 1)
                wait_read(dve, j)

            tt, ts, stt = dve.tensor_tensor, dve.tensor_scalar, dve.scalar_tensor_tensor
            step(dve.memset(small[:, 60:61], EPS))

            def scale_rows(src):
                n = count("norm_v")
                dve.wait_ge(norm_root, n)
                step(dve.reciprocal(small[:, 4:6], small[:, 2:4]))
                for t in range(TT):
                    tell(ts(view(A_XS, TT, D)[:, t, :], src[:, t, :], small[:, 4 + t:5 + t], None, ALU.mult),
                         norm_scaled, 2 * (n - 1) + t + 1)

            def norm(name, src=resid, dst=xT):
                scale_rows(src)
                i = NORMS.index(name)
                for g in range(4):
                    j = J.of(f"norm_{name}", g)
                    t, k0 = g // 2, (g % 2) * 4
                    wait_filled(dve, j)
                    gain = gains[:, i, k0:k0 + 4].unsqueeze(2).to_broadcast([P, 4, P])
                    read_out(tt(dst[:, k0:k0 + 4, t * P:(t + 1) * P], bank(j)[:, :].rearrange("p (k q) -> p k q", k=4),
                                gain, ALU.mult), j)

            def norm_rows(n):
                scale_rows(resid)
                dve.wait_ge(extra_loaded["gain"], 16 * n)
                for t in range(TT):
                    step(tt(resid[:, t, :], view(A_XS, TT, D)[:, t, :], gain_bc, ALU.mult))

            def add_out(name):
                for k in range(4):
                    c, t = k // 2, k % 2
                    j = J.of(name, k)
                    wait_filled(dve, j)
                    r = resid[:, t, c * CHUNK:(c + 1) * CHUNK]
                    read_out(tt(r, bank(j)[:, :], r, ALU.add), j)

            def residual_ready(n):
                dve.nop().then_inc(block_step, 1)
                dve.wait_ge(block_step, n)

            def attention(name, order, heads, base, mask, scale, finish):
                for kind, a in order:
                    n = base + a
                    if kind == "S":
                        j = J.of(name, order.index(("S", a)))
                        wait_filled(dve, j)
                        s = s_buf[:, n % 3]
                        m = mask(a)
                        src = bank(j)[:, :].rearrange("p (t k) -> p t k", t=TT)
                        if m is None:
                            read_out(ts(s, src, scale, None, ALU.mult), j)
                        else:
                            read_out(stt(s, src, scale, m, ALU.mult, ALU.add), j)
                        tell(dve.tensor_reduce(small[:, 8 + (n % 4) * 2:10 + (n % 4) * 2], s, AX, ALU.max, negate=True),
                             scores_shifted, n + 1)
                    elif kind == "O":
                        j = J.of(name, order.index(("O", a)))
                        r = small[:, 24 + (n % 2) * 2:26 + (n % 2) * 2]
                        dve.wait_ge(weights_ready, n + 1)
                        step(dve.reciprocal(r, small[:, 16 + (n % 4) * 2:18 + (n % 4) * 2]))
                        wait_filled(dve, j)
                        finish(a, j, r)

            def peer(layer):
                sc = view(P_SC, TT, HP, N_KEYS)
                at = P_TOP + TT * 3 * HK
                off = [at]

                def scratch(*shape):
                    v = view(off[0], *shape)
                    off[0] += math.prod(shape)
                    return v

                sv = scratch(HP, TOPK)
                si = scratch(HP, TOPK)
                si_f = scratch(HP, TOPK)
                rest = scratch(N_KEYS)
                cand = scratch(PEER_HEADS, TOPK * TOPK)
                rest2 = scratch(TOPK * TOPK)
                best = scratch(PEER_HEADS, TOPK)
                pos_u = scratch(PEER_HEADS, TOPK)
                part = scratch(2, HK)
                part_f = scratch(2, HK)
                pick = scratch(PEER_HEADS, TOPK, TOPK)
                red = scratch(PEER_HEADS)
                assert off[0] <= A_XS

                def top16(values, index, src, tmp):
                    step(dve.max(values[:, 0:8], src))
                    step(dve.max_index(index[:, 0:8].bitcast(U32), values[:, 0:8], src))
                    step(dve.match_replace(tmp, values[:, 0:8], src, LOWEST))
                    step(dve.max(values[:, 8:16], tmp))
                    step(dve.max_index(index[:, 8:16].bitcast(U32), values[:, 8:16], tmp))

                for t in range(TT):
                    n = TT * layer + t
                    for hp in range(HP):
                        if hp % 4 == 0:
                            wait_read(dve, J.of(f"scores{layer}", 4 * t + hp // 4))
                        top16(sv[:, hp], si[:, hp], sc[:, t, hp], rest)
                    step(dve.tensor_copy(si_f, si.bitcast(U32)))
                    svh = sv.rearrange("p (h s) k -> p h s k", s=2)
                    c4 = cand.rearrange("p h (a b) -> p h a b", b=TOPK)
                    step(tt(c4, svh[:, :, 0].unsqueeze(3).to_broadcast([P, PEER_HEADS, TOPK, TOPK]),
                            svh[:, :, 1].unsqueeze(2).to_broadcast([P, PEER_HEADS, TOPK, TOPK]), ALU.add))
                    for h in range(PEER_HEADS):
                        top16(best[:, h], pos_u[:, h], cand[:, h], rest2)
                    g = top_out(t, 2).rearrange("p (h k) -> p h k", k=TOPK)
                    tell(tt(g, best, best[:, :, 0:1].to_broadcast([P, PEER_HEADS, TOPK]), ALU.subtract),
                         top_ready, 2 * n + 1)
                    pu = pos_u.rearrange("p h k -> p (h k)").bitcast(U32)
                    step(ts(part[:, 0].bitcast(U32), pu, 4, None, ALU.logical_shift_right))
                    step(ts(part[:, 1].bitcast(U32), pu, TOPK - 1, None, ALU.bitwise_and))
                    step(dve.tensor_copy(part_f, part.bitcast(U32)))
                    sih = si_f.rearrange("p (h s) k -> p h s k", s=2)
                    for i in range(2):
                        a = part_f[:, i].rearrange("p (h k) -> p h k", k=TOPK).unsqueeze(3)\
                            .to_broadcast([P, PEER_HEADS, TOPK, TOPK])
                        lane = iota[:, 0:TOPK].unsqueeze(1).unsqueeze(1).to_broadcast([P, PEER_HEADS, TOPK, TOPK])
                        step(tt(pick, a, lane, ALU.is_equal))
                        step(tt(pick, pick, sih[:, :, i].unsqueeze(2).to_broadcast([P, PEER_HEADS, TOPK, TOPK]), ALU.mult))
                        step(dve.tensor_reduce(top_out(t, i).rearrange("p (h k) -> p h k", k=TOPK), pick, AX, ALU.add))
                    dve.wait_ge(top_exp, n + 1)
                    step(dve.tensor_reduce(red, g, AX, ALU.add))
                    step(dve.reciprocal(red, red))
                    tell(tt(g, g, red.unsqueeze(2).to_broadcast([P, PEER_HEADS, TOPK]), ALU.mult), top_ready, 2 * n + 2)
                for t in range(TT):
                    wait_read(dve, J.of(f"idxT{layer}", t))
                n0 = 64 * layer

                def quad(i, s, first):
                    if not first:
                        dve.wait_ge(products, i + (n0 - 1))
                    for c in range(4):
                        pos = i * 4 + c

                        def col(k):
                            return idxT[:, k, bass.ds(pos, 1)]

                        ts(onehot[:, s, 0, c, :], iota[:], col(0), col(2), ALU.is_equal, ALU.mult)
                        last = ts(onehot[:, s, 1, c, :], iota[:], col(1), None, ALU.is_equal)
                    last.then_inc(onehots, 1)

                quad(0, 0, True)
                quad(1, 1, True)
                with dve.Fori(1, 32) as i:
                    for s in range(2):
                        quad(i * 2 + s, s, False)
                dve.wait_ge(stored, n0 + 64)
                base = layer * N_KEYS

                def gate(t, b):
                    dve.wait_ge(gelu_done, t + (base + 1))
                    if not (isinstance(t, int) and t < 2):
                        dve.wait_ge(tile_used, t + (base - 1))
                    w = router[:, bass.ds(t, 1), :].rearrange("p a b -> p (a b)")
                    tt(gated_buf[:, b, :], gelu_buf[:, b, :], w, ALU.mult).then_inc(gated, 1)

                gate(0, 0)
                gate(1, 1)
                with dve.Fori(1, N_KEYS // 2) as i:
                    for b in range(2):
                        gate(i * 2 + b, b)
                dve.wait_ge(tile_used, base + N_KEYS)
                for t in range(TT):
                    for c in range(2):
                        r = resid[:, t, c * CHUNK:(c + 1) * CHUNK]
                        step(tt(r, banks[4 + 2 * t + c][:, :], r, ALU.add))

            dve.wait_ge(const_loaded, 16 * N_CONST)
            norm("attn")
            for k in range(4, 8):
                j = J.of("qkv", k)
                wait_filled(dve, j)
                i = 2 * (k - 4)
                read_out(dve.tensor_copy(na_k[:, i:i + 2, :].rearrange("p a b -> p (a b)"), bank(j)[:, :]), j)
            dve.wait_ge(extra_loaded["bias"], 16)

            def na_finish(a, j, r):
                for t in range(TT):
                    ins = ts(na_o[:, t, a * HEAD:(a + 1) * HEAD], bank(j)[:, t * HEAD:(t + 1) * HEAD], r[:, t:t + 1],
                             None, ALU.mult)
                read_out(ins, j)

            attention("na", NA, na_heads, head_base["na"], lambda a: na_bias[:, a], 1.0, na_finish)
            add_out("wo")
            residual_ready(RES["wo"])
            norm("peer0")
            peer(0)
            residual_ready(RES["peer0"])
            u = view(C_U, KT, SEQ + 2)
            step(dve.memset(u[:, :, 0:1], 0.0))
            step(dve.memset(u[:, :, SEQ + 1:SEQ + 2], 0.0))
            norm("conv")
            cT, gT, y = view(C_C, KT, SEQ), view(C_GATE, KT, SEQ), view(C_Y, KT, SEQ)
            for k in range(4):
                wait_read(dve, J.of("conv_in", 4 + k))
                j = J.of("conv_in", 8 + k)
                wait_filled(dve, j)
                read_out(tt(u[:, 2 * k:2 * k + 2, 1:SEQ + 1], cT[:, 2 * k:2 * k + 2, :],
                            bank(j)[:, :].rearrange("p (a b) -> p a b", a=2), ALU.mult), j)
            for k in range(4):
                wait_read(dve, J.of("conv_in", k))
            for k in range(KT):
                step(ts(y[:, k], u[:, k, 0:SEQ], convw[:, k, 0:1], None, ALU.mult))
                for tap in (1, 2):
                    step(stt(y[:, k], u[:, k, tap:tap + SEQ], convw[:, k, tap:tap + 1], y[:, k], ALU.mult, ALU.add))
                step(tt(y[:, k], y[:, k], gT[:, k], ALU.mult))
            tell(dve.nop(), conv_ready, 1)
            add_out("conv_out")
            residual_ready(RES["conv"])
            norm("peer1")
            peer(1)
            residual_ready(RES["peer1"])
            norm_rows(1)
            residual_ready(RES["between"])
            norm("mem", view(0, TT, D), view(E_T, KT, SEQ))
            norm("even")
            pos_f = small[:, 56:58]
            step(dve.tensor_copy(pos_f, pos_i[:]))
            two_pi = 2 * math.pi
            c1 = float(np.float32(6.28125))
            c2 = float(np.float32(two_pi - c1))
            c3 = float(two_pi - c1 - c2)
            turns = view(E_TMP, TT, ROPES)
            for t in range(TT):
                step(ts(sinT[:, t], inv_freq[:], pos_f[:, t:t + 1], None, ALU.mult))
            step(ts(turns, sinT, 1.0 / two_pi, 12582912.0, ALU.mult, ALU.add))
            step(ts(turns, turns, 12582912.0, None, ALU.subtract))
            for c in (c1, c2, c3):
                step(stt(sinT, turns, -c, sinT, ALU.mult, ALU.add))
            step(ts(sinT, sinT, 3.1415925, -3.1415925, ALU.min, ALU.max))
            step(ts(cosT, sinT, -1.0, None, ALU.mult))
            step(tt(cosT, cosT, sinT, ALU.max))
            step(ts(cosT, cosT, -1.0, math.pi / 2, ALU.mult, ALU.add))
            tell(dve.nop(), angle_ready, 1)
            dve.wait_ge(tables, 1)

            def rope(dst, src, heads, hd, f0, dups=1):
                t, dst_v, src_v = src
                x = src_v.rearrange("p (h s f) -> p h s f", s=2, f=hd // 2)
                f = hd // 2
                a = view(E_TMP, heads, 2, f)
                b = view(E_TMP + 512, heads, 2, f)
                cos = cosT[:, t, f0:f0 + f]
                sin = sinT[:, t, f0:f0 + f]
                step(tt(a, x, cos.unsqueeze(1).unsqueeze(1).to_broadcast([P, heads, 2, f]), ALU.mult))
                step(tt(b, x, sin.unsqueeze(1).unsqueeze(1).to_broadcast([P, heads, 2, f]), ALU.mult))
                for o in dst_v:
                    step(tt(o[:, :, 0], a[:, :, 0], b[:, :, 1], ALU.subtract))
                    step(tt(o[:, :, 1], a[:, :, 1], b[:, :, 0], ALU.add))

            for k in range(18):
                wait_read(dve, J.of("even_in", k))

            def as_heads(v, hd):
                return v.rearrange("p (h s f) -> p h s f", s=2, f=hd // 2)

            gates = ev_proj[:, :, EVEN["ng"]:EVEN["ng"] + 24]
            tell(tt(gates, gates, gate_b[:].unsqueeze(1).to_broadcast([P, TT, 24]), ALU.add), gate_in, 1)
            for t in range(TT):
                for name, dst in (("nq", e_nq), ("mq", e_mq), ("mk", e_mk)):
                    rope(None, (t, [as_heads(dst[:, t], HEAD)], ev_proj[:, t, EVEN[name]:EVEN[name] + 512]), 8, HEAD, 0)
                rope(None, (t, [as_heads(e_kc[:, t], HEAD)], ev_proj[:, t, EVEN["nkc"]:EVEN["nkc"] + 128]), 2, HEAD, 0)
                for name, dst in (("nks", e_ks), ("nkw", e_kw)):
                    outs = [dst[:, t, :, dup].rearrange("p g (s f) -> p g s f", s=2) for dup in range(2)]
                    rope(None, (t, outs, ev_proj[:, t, EVEN[name]:EVEN[name] + 128]), 2, HEAD, 0)
            tell(dve.nop(), roped, 1)
            step(dve.memset(cmp_small[:], 0.0))
            j = J.of("even_T", 7)
            wait_filled(dve, j)
            read_out(dve.tensor_copy(eT[:, EKC:EKC + 2, :].rearrange("p a b -> p (a b)"), bank(j)[:, :]), j)
            for kv, pe_sb in (("k", pe_k), ("v", pe_v)):
                by = cmp_T[kv].rearrange("p (n l) -> p l n", l=CMP_STRIDE)
                for part in range(2):
                    l0 = part * CMP_STRIDE
                    step(tt(ape[kv][:, l0:l0 + CMP_STRIDE], by[:, :, part:part + N_CMP],
                            pe_sb[:, l0:l0 + CMP_STRIDE].unsqueeze(2).to_broadcast([P, CMP_STRIDE, N_CMP]), ALU.add))
            tell(dve.nop(), cmp_ready, 1)
            for g in range(NSA_GROUPS):
                wait_read(dve, J.of("hid", g))
            step(dve.tensor_copy(hid_rep[:, :, 0:N_CMP], hid_sb[:, 1:2, 0:N_CMP].to_broadcast([P, 4, N_CMP])))
            tell(dve.nop(), cmp_ready, 2)
            step(dve.memset(vbd, 0.0))
            step(dve.memset(cmp_s, 0.0))
            for g in range(NSA_GROUPS):
                j = J.of("kvc", g)
                wait_filled(dve, j)
                step(dve.tensor_copy(kcT[:, g, 0:N_CMP], bank(j)[:, 0:N_CMP]))
                for i in range(4):
                    ins = dve.tensor_copy(vbd[32 * i:32 * i + 32, g, i, :], bank(j)[32 * i:32 * i + 32, 64:64 + HEAD])
                    if i < 3:
                        step(ins)
                read_out(ins, j)
            for par in range(2):
                j = J.of("cmp_S", par)
                wait_filled(dve, j)
                src = bank(j)[:, 0:128].rearrange("p (h t n) -> p h t n", h=4, t=TT)
                for t in range(TT):
                    dst = cmp_s[:, t, par:8:2, 0:N_CMP]
                    ins = stt(dst, src[:, :, t, 0:N_CMP], HEAD ** -0.5,
                              cmp_mask[:, 0, t:t + 1, 0:N_CMP].to_broadcast([P, 4, N_CMP]), ALU.mult, ALU.add)
                    if t == 0:
                        step(ins)
                read_out(ins, j)
            cs = cmp_s.rearrange("p t h n -> p (t h) n")[:, :, 0:N_CMP]
            cm = cmp_small[:, 256:272]
            step(dve.tensor_reduce(cm, cs, AX, ALU.max))
            tell(tt(cs, cs, cm.unsqueeze(2).to_broadcast([P, 16, N_CMP]), ALU.subtract), cmp_exp_in, 1)
            dve.wait_ge(cmp_exp, 1)
            dve.wait_ge(nsa_gate, 1)
            for t in range(TT):
                c = cmp_s[:, t, :, 0:N_CMP]
                step(tt(c, c, cmp_mask[:, 1, t:t + 1, 0:N_CMP].to_broadcast([P, 8, N_CMP]), ALU.mult))
            step(dve.tensor_reduce(cm, cs, AX, ALU.add))
            step(ts(cm, cm, 1e-30, None, ALU.max))
            step(dve.reciprocal(cm, cm))
            step(tt(cm.rearrange("p (t h) -> p t h", t=TT), cm.rearrange("p (t h) -> p t h", t=TT), gates[:, :, 0:8], ALU.mult))
            step(tt(cs, cs, cm.unsqueeze(2).to_broadcast([P, 16, N_CMP]), ALU.mult))
            tell(dve.nop(), cmp_ready, 3)
            for t in range(TT):
                j = J.of("cmp_O", t)
                wait_filled(dve, j)
                read_out(dve.tensor_copy(nsa_o[:, t], bank(j)[:, :]), j)
            dve.wait_ge(silu_done, 3)

            def ev_finish(a, j, r):
                name, h = ev_heads[a][:2]
                if name in ("nsa_s", "nsa_w"):
                    br = 1 if name == "nsa_s" else 2
                    step(tt(r, r, gates[:, :, br * 8 + h:br * 8 + h + 1].rearrange("p a b -> p (a b)"), ALU.mult))
                for t in range(TT):
                    o = bank(j)[:, t * HEAD:(t + 1) * HEAD]
                    if name in ("nsa_s", "nsa_w"):
                        dst = nsa_o[:, t, h * HEAD:(h + 1) * HEAD]
                        ins = stt(dst, o, r[:, t:t + 1], dst, ALU.mult, ALU.add)
                    else:
                        z = EVEN["mz" if name == "moba" else "ez"] + h * HEAD
                        dst = ev_proj[:, t, z:z + HEAD]
                        ins = stt(dst, o, r[:, t:t + 1], dst, ALU.mult, ALU.mult)
                read_out(ins, j)

            attention("ev", EV, ev_heads, head_base["ev"],
                      lambda a: None if ev_heads[a][0] == "mem_e" else causal[:], HEAD ** -0.5, ev_finish)
            z = ev_proj[:, :, EVEN["nz"]:EVEN["nz"] + 512]
            tell(tt(z, z, nsa_o, ALU.mult), y_ready, 1)
            add_out("even_out")
            residual_ready(RES["even"])
            norm("odd")
            for k in range(26):
                wait_read(dve, J.of("odd_in", k))
            for t in range(TT):
                for name, dst in (("rq", o_q), ("rk", o_k)):
                    for hh in range(2):
                        c = ODD[name] + hh * 512
                        rope(None, (t, [as_heads(dst[:, t, hh * 512:(hh + 1) * 512], RET_QK)], od_proj[:, t, c:c + 512]),
                             2, RET_QK, ROPE)
            tell(dve.nop(), roped, 2)
            dve.wait_ge(extra_loaded["decay"], 16)
            dve.wait_ge(silu_done, 6)
            for kind, h in RET:
                if kind == "S":
                    j = J.of("ret", ret_job[kind, h])
                    wait_filled(dve, j)
                    if h >= 2:
                        wait_filled(dve, J.of("ret", ret_job["O", h - 2] + 1))
                    step(stt(ret_buf[:, h % 2, 0:2].rearrange("p a b -> p (a b)"), bank(j)[:, 0:SEQ], RET_QK ** -0.5,
                             decay[:, h, :], ALU.mult, ALU.mult))
                    ins = stt(ret_buf[:, h % 2, 2], bank(j)[:, SEQ:SEQ + P], RET_QK ** -0.5, decay[:, h, 0:P],
                              ALU.mult, ALU.mult)
                    read_out(ins, j)
                    tell(dve.nop(), ret_ready, h + 1)
                else:
                    for t in range(TT):
                        n = TT * h + t
                        j = J.of("ret", ret_job[kind, h] + t)
                        wait_filled(dve, j)
                        step(dve.bn_stats(bn[:, 0:6], bank(j)[:, :]))
                        tell(dve.bn_aggr(ret_stats[:, n, :], bn[:, 0:6]), ret_root_in, n + 1)
                        dve.wait_ge(ret_root, n + 1)
                        step(dve.reciprocal(small[:, 38:39], small[:, 30 + n:31 + n]))
                        o = view(E_TMP, RET_V)
                        read_out(ts(o, bank(j)[:, :], ret_stats[:, n, 0:1], small[:, 38:39], ALU.subtract, ALU.mult), j)
                        z = od_proj[:, t, ODD["rz"] + h * RET_V:ODD["rz"] + (h + 1) * RET_V]
                        step(tt(z, z, o, ALU.mult))

            def om_finish(a, j, r):
                for t in range(TT):
                    z = ODD["ez"] + a * HEAD
                    dst = od_proj[:, t, z:z + HEAD]
                    ins = stt(dst, bank(j)[:, t * HEAD:(t + 1) * HEAD], r[:, t:t + 1], dst, ALU.mult, ALU.mult)
                read_out(ins, j)

            attention("om", OM, om_heads, head_base["om"], lambda a: None, HEAD ** -0.5, om_finish)
            tell(dve.nop(), y_ready, 2)
            add_out("odd_out")
            residual_ready(RES["odd"])
            norm_rows(2)
            tell(dve.nop(), final_ready, 1)


def window_bias(rel_bias):
    q, k = np.arange(SEQ)[:, None], np.arange(SEQ)[None, :]
    qc, kc = q % GRID_W, k % GRID_W
    row = k // GRID_W - q // GRID_W + MAX_WIN_ROWS - 1
    start = np.clip(qc - WIN_COLS // 2, 0, GRID_W - WIN_COLS)
    inside = (kc >= start) & (kc < start + WIN_COLS)
    col = np.clip(kc - qc + WIN_COLS - 1, 0, 2 * WIN_COLS - 2)
    full = np.where(inside[None], rel_bias[:, row, col], np.float32(NEG))
    return full.reshape(NA_HEADS, TT, P, SEQ).transpose(2, 0, 1, 3)


def constants():
    q, k = np.arange(SEQ)[:, None], np.arange(SEQ)[None, :]
    causal = np.where(k <= q, 0.0, NEG).reshape(TT, P, SEQ).transpose(1, 0, 2)
    n = np.arange(16)[None, :]
    seen = (n * CMP_STRIDE + CMP_LEN - 1 <= q) & (n < N_CMP)
    cmp_mask = np.stack([np.where(seen, 0.0, NEG), seen * 1.0]).reshape(2, TT, P, 16).transpose(2, 0, 1, 3)
    f = np.float32
    inv = np.concatenate([f(1) / f(10000.0) ** (np.arange(0, 64, 2, dtype=f) / f(64)),
                          f(1) / f(10000.0) ** np.linspace(0, 1, RET_ROPE, dtype=f)])
    log_g = np.log(f(1) - f(2) ** (f(-5) - np.arange(RET_HEADS, dtype=f))).astype(f)
    dist = (k[0][None, :] - np.arange(P)[:, None]).astype(f)
    decay = np.where(dist[:, None] >= 0, np.exp(np.maximum(dist, 0)[:, None] * log_g[None, :, None]), 0)
    c = {"c_ident": np.eye(P), "c_iota": np.arange(P), "c_causal": causal, "c_cmp_mask": cmp_mask,
         "c_inv_freq": inv, "c_decay": decay}
    return {name: np.ascontiguousarray(a, dtype=f) for name, a in c.items()}


def kernel(**inputs):
    import concourse.bacc as _bacc
    from concourse.bass_utils import run_bass_kernel_spmd as _run

    i = {name: np.asarray(a) for name, a in inputs.items()}
    gains = np.stack([i["norm_mix"][0], i["norm_ffn"][0], i["norm_mix"][1], i["norm_ffn"][1],
                      i["mem_norm_g_2"], i["l0_norm_g_2"], i["l1_norm_g_2"]])
    arrays = {
        "x": i["x"][0], "mem": i["mem_2"][0],
        "positions": i["positions_2"].reshape(TT, P).T,
        "gains": gains.reshape(len(NORMS), KT, P).transpose(2, 0, 1),
        "norm_final": i["norm_final"], "final_norm": i["final_norm_g_2"],
        "attn_w_qkv": i["attn_w_qkv"][0], "attn_w_o": i["attn_w_o"][0],
        "na_bias": window_bias(i["attn_rel_bias"][0]),
        "conv_w_in": i["conv_w_in"][0], "conv_w_out": i["conv_w_out"][0],
        "conv_w": i["conv_w_conv"][0].reshape(3, KT, P).transpose(2, 1, 0),
        "peer_w_query": i["peer_w_query"],
        "keysT": i["peer_sub_keys"].reshape(2, HP, N_KEYS, P).transpose(0, 3, 1, 2),
        "w_upT": i["peer_w_up"].reshape(2 * N_KEYS, N_KEYS, KT, P).transpose(0, 3, 2, 1).reshape(2 * N_KEYS, P, KT * N_KEYS),
        "w_down": i["peer_w_down"].reshape(2 * N_KEYS, N_KEYS, D),
        "l0_w_in_2": i["l0_w_in_2"], "l0_w_out_2": i["l0_w_out_2"], "l0_w_mem_kv_2": i["l0_w_mem_kv_2"],
        "l1_w_in_2": i["l1_w_in_2"], "l1_w_out_2": i["l1_w_out_2"], "l1_w_mem_kv_2": i["l1_w_mem_kv_2"],
        "gate_b": i["l0_nsa_gate_b_2"],
        "pe_k": np.concatenate([i["l0_cmp_pe_k_2"].T] * 2), "pe_v": np.concatenate([i["l0_cmp_pe_v_2"].T] * 2),
        "w1_k": i["l0_cmp_w1_k_2"].transpose(1, 0, 2), "w1_v": i["l0_cmp_w1_v_2"].transpose(1, 0, 2),
        "w2_k": i["l0_cmp_w2_k_2"], "w2_v": i["l0_cmp_w2_v_2"],
        **constants(),
    }
    nc = _bacc.Bacc("TRN2", target_bir_lowering=False, num_devices=1)
    d, fed = {}, {}
    for name, a in arrays.items():
        a = np.ascontiguousarray(a)
        fed[f"in_{name}"] = a
        d[name] = nc.dram_tensor(f"in_{name}", a.shape, mybir.dt.from_np(a.dtype), kind="ExternalInput").ap()
    out = nc.dram_tensor("out_rows", (SEQ, D), F32, kind="ExternalOutput").ap()
    if DEBUG:
        d["dbg"] = nc.dram_tensor("dbg", (7, P, TT, D), F32, kind="ExternalOutput").ap()
    build(nc, d, out)
    r = _run(nc, [fed], core_ids=[0])
    return r.results[0]["out_rows"].reshape(1, SEQ, D)
```

```python
import math
from contextlib import ExitStack

import numpy as np

import concourse.bass as bass
from concourse import mybir

F32 = mybir.dt.float32
F32R = mybir.dt.float32r
BF16 = mybir.dt.bfloat16
U32 = mybir.dt.uint32
I32 = mybir.dt.int32
ALU = mybir.AluOpType
ACT = mybir.ActivationFunctionType
AX = mybir.AxisListType.X

P = 128
SEQ, D = 256, 1024
TT = SEQ // P
KT = D // P
CHUNK = 512
NEG = -1e30
LOWEST = -3.0e38
EPS = 1e-6

ROWS, GRID_W, WIN_COLS, MAX_WIN_ROWS = 4, 64, 16, 8
NA_HEADS, HEAD = 16, 64
PEER_HEADS, N_KEYS, TOPK = 8, 128, 16
HP = 2 * PEER_HEADS
HK = PEER_HEADS * TOPK

NSA_HEADS, NSA_GROUPS = 8, 2
CMP_LEN, CMP_STRIDE = 32, 16
N_CMP = (SEQ - CMP_LEN) // CMP_STRIDE + 1
MOBA_HEADS, MEM_HEADS = 8, 4
RET_HEADS, RET_QK, RET_V = 4, 256, 512
ROPE = 32
RET_ROPE = 128
ROPES = ROPE + RET_ROPE

EVEN = {}
_at = 0
for _name, _w in (("nq", 512), ("nkc", 128), ("nvc", 128), ("nks", 128), ("nvs", 128), ("nkw", 128),
                  ("nvw", 128), ("ng", 24), ("nz", 512), ("mq", 512), ("mk", 512), ("mv", 512),
                  ("mz", 512), ("eq", 256), ("ez", 256)):
    EVEN[_name] = _at
    _at += _w
EVEN_W = _at
EVEN_OUT = 1280
ODD = {"rq": 0, "rk": 1024, "rv": 2048, "rz": 4096, "eq": 6144, "ez": 6400}
ODD_W = 6656
ODD_OUT = 2304

NORMS = ("attn", "peer0", "conv", "peer1", "mem", "even", "odd")

ARENA = 32768
A_XS = 19968
L_QT, L_KT, L_V, L_BIAS, L_O, L_OT = 0, 2048, 4096, 6144, 14336, 16384
P_LOW = 16384
P_QT, P_SC, P_KEYS, P_TOP = P_LOW, P_LOW + 4096, P_LOW + 8192, P_LOW + 10240
C_GATE, C_C, C_U, C_Y, C_YT = 0, 2048, 4096, 8192, 10240
E_PROJ, E_T, E_ROPED = 0, 8752, 13872
E_NSA = A_XS
M_K, M_V = 23344, 24368
E_W1K, E_W1V, E_APE, E_TMP = 25392, 27440, 29488, 30448
ROPE_AT = 31472
E_YT = E_T
O_PROJ, O_ROPED, O_T = 0, 13312, 17408
O_DECAY = 22016
O_YT = O_ROPED

UNIT = 1024
UKT = 2
RAW, SPLIT = 4, 2
HALF = N_KEYS // 2
GROUP = 8
LEAD = 4
DEBUG = False


class Jobs:

    BANKS = 8

    def __init__(self):
        self.first, self.n = {}, 0
        self.own, self.told = [], [0] * self.BANKS

    def add(self, name, count, own=True):
        self.first[name] = self.n
        for _ in range(count):
            b = self.n % self.BANKS
            self.told[b] += own
            self.own.append(self.told[b] if own else None)
            self.n += 1

    def of(self, name, k=0):
        return self.first[name] + k


def attention_order(heads):
    order = []
    for s in range(heads + 2):
        if s < heads:
            order.append(("S", s))
        if 0 <= s - 1 < heads:
            order.append(("T", s - 1))
        if s >= 2:
            order.append(("O", s - 2))
    return order


def build(nc, d, out):
    ctx = ExitStack()
    with ctx:
        def sb(name, shape, dt=F32):
            return ctx.enter_context(nc.sbuf_tensor(name, shape, dt))

        sems = {}

        def sem(name):
            if name not in sems:
                sems[name] = ctx.enter_context(nc.semaphore(name))
            return sems[name]

        place_at = [(nc.sbuf_base + 63) // 64 * 64]

        def place(name, shape, dt=F32, at=None):
            size = math.prod(shape[1:]) * (2 if dt == BF16 else 4)
            if at is None:
                at = place_at[0]
                place_at[0] += (size + 63) // 64 * 64
            place_of[name] = at
            return nc.alloc_sbuf_tensor_at(name, list(shape), dt, offset=at)

        place_of = {}
        resid = place("resid", [P, TT, D])
        xh, xl = place("xh", [P, KT, SEQ], F32R), place("xl", [P, KT, SEQ], F32R)
        raw = place("raw", [P, RAW, UNIT])
        wh, wl = place("wh", [P, SPLIT, UNIT], F32R), place("wl", [P, SPLIT, UNIT], F32R)
        arena = place("arena", [P, ARENA])
        aux = place("aux", [P, 5248])
        ident = place("ident", [P, P])
        gains = place("gains", [P, len(NORMS), KT])
        small = place("small", [P, 64])
        iota = place("iota", [P, TOPK])
        convw = place("convw", [P, KT, 3])
        pos_i = place("pos_i", [P, TT], I32)
        gate_b = place("gate_b", [P, 24])
        pe_k = place("pe_k", [P, CMP_LEN])
        pe_v = place("pe_v", [P, CMP_LEN])
        w2k = place("w2k", [P, 2, HEAD])
        w2v = place("w2v", [P, HEAD])
        ret_stats = place("ret_stats", [P, RET_HEADS * TT, 2])
        bn = place("bn", [P, 6])
        assert place_at[0] <= nc.sbuf_usable_end, (place_at[0], nc.sbuf_usable_end)

        def parts(name, words, tiles):
            size = tiles * SEQ
            return [place(f"{name}_{p}", [P, tiles, SEQ], F32R, place_of["arena"] + 4 * (words + k * size))
                    for k, p in enumerate("hl")]

        na_out = parts("na_out", L_OT, KT)
        conv_out = parts("conv_out", C_YT, KT)
        mem_in_T = parts("mem_in", E_T, KT)
        ev_out = parts("ev_out", E_YT, EVEN_OUT // P)
        od_out = parts("od_out", O_YT, ODD_OUT // P)
        x_in = [xh, xl]

        at = place_of["aux"]
        lanes = place("lanes", [P, N_KEYS, GROUP], BF16, at)
        at += 2 * N_KEYS * GROUP
        choice = place("choice", [P, 5, SEQ], BF16, at)
        at += 2 * 5 * SEQ
        second = place("second", [P, 2, N_KEYS, GROUP], BF16, at)
        at += 2 * 2 * N_KEYS * GROUP
        first_eq = place("first_eq", [P, 2, HALF, GROUP], BF16, at)
        at += 2 * 2 * HALF * GROUP
        first = place("first", [P, 2, 3, HALF, GROUP], BF16, at)
        at += 2 * 2 * 3 * HALF * GROUP
        gh, gl = (place(n, [P, SPLIT, SEQ], F32R, at + k * 4 * SPLIT * SEQ) for k, n in enumerate(("gh", "gl")))
        assert at + 8 * SPLIT * SEQ <= place_of["ident"]
        banks = [ctx.enter_context(nc.psum_tensor(f"bank{b}", [P, 512], F32)) for b in range(8)]

        def view(off, *shape):
            n = math.prod(shape)
            names = "abcd"[:len(shape)]
            v = arena[:, off:off + n]
            if len(shape) == 1:
                return v
            return v.rearrange(f"p ({' '.join(names)}) -> p {' '.join(names)}",
                               **{c: s for c, s in zip(names[1:], shape[1:])})

        def aux_view(off, *shape):
            n = math.prod(shape)
            names = "abcd"[:len(shape)]
            v = aux[:, off:off + n]
            if len(shape) == 1:
                return v
            return v.rearrange(f"p ({' '.join(names)}) -> p {' '.join(names)}",
                               **{c: s for c, s in zip(names[1:], shape[1:])})

        J = Jobs()
        units = []
        first_unit, chunk_end = {}, {}

        def weight(name, w, cols):
            first_unit[name], chunk_end[name] = len(units), []
            for c0 in range(0, cols, CHUNK):
                n = min(CHUNK, cols - c0)
                for k0 in range(0, w.shape[0], UKT * P):
                    units.append((w[k0:k0 + UKT * P, c0:c0 + n].rearrange("(k p) n -> p k n", p=P), UKT, n))
                chunk_end[name].append(len(units))

        def experts(layer):
            first_unit[f"up{layer}"] = len(units)
            units.extend([None] * N_KEYS)
            first_unit[f"down{layer}"] = len(units)
            units.extend([None] * N_KEYS)

        weight("qkv", d["attn_w_qkv"], 3 * D)
        weight("wo", d["attn_w_o"], D)
        weight("query0", d["peer_w_query"][0], 2048)
        experts(0)
        weight("conv_in", d["conv_w_in"], 3 * D)
        weight("conv_out", d["conv_w_out"], D)
        weight("query1", d["peer_w_query"][1], 2048)
        experts(1)
        weight("mem0", d["l0_w_mem_kv_2"], 512)
        weight("mem1", d["l1_w_mem_kv_2"], 512)
        weight("even_in", d["l0_w_in_2"], EVEN_W)
        weight("even_out", d["l0_w_out_2"], D)
        weight("odd_in", d["l1_w_in_2"], ODD_W)
        weight("odd_out", d["l1_w_out_2"], D)

        NA = attention_order(NA_HEADS)
        SEC = [("nsa_s", NSA_HEADS), ("nsa_w", NSA_HEADS), ("moba", MOBA_HEADS), ("mem_e", MEM_HEADS)]
        J.add("norm_attn", 4); J.add("qkv", 12, own=False); J.add("na", len(NA)); J.add("na_oT", 4); J.add("wo", 4, own=False)
        J.add("norm_peer0", 4); J.add("query0", 8, own=False); J.add("scores0", 8); J.add("idxT0", 2)
        J.add("norm_conv", 4); J.add("conv_in", 12, own=False); J.add("conv_out", 4, own=False)
        J.add("norm_peer1", 4); J.add("query1", 8, own=False); J.add("scores1", 8); J.add("idxT1", 2)
        J.add("norm_mem", 4); J.add("mem0", 2, own=False); J.add("mem1", 2, own=False)
        J.add("norm_even", 4); J.add("even_in", 18, own=False); J.add("even_T", 10)
        J.add("hid", 2); J.add("kvc", 2); J.add("cmp_S", 2); J.add("cmp_T", 1); J.add("cmp_O", 2)
        EV = attention_order(sum(n for _, n in SEC))
        J.add("ev", len(EV)); J.add("even_yT", 5); J.add("even_out", 4, own=False)
        J.add("norm_odd", 4); J.add("odd_in", 26, own=False); J.add("odd_T", 9)
        RET = [(k, h) for s in range(RET_HEADS + 1) for k, h in (("S", s), ("O", s - 1))
               if 0 <= h < RET_HEADS]
        ret_job, n = {}, 0
        for k, h in RET:
            ret_job[k, h] = n
            n += 1 if k == "S" else 2
        J.add("ret", n)
        OM = attention_order(MEM_HEADS)
        J.add("om", len(OM)); J.add("odd_yT", 9); J.add("odd_out", 4, own=False)

        unit_of = {}
        for name, ends in chunk_end.items():
            for k, end in enumerate(ends):
                unit_of[J.of(name, 2 * k)] = unit_of[J.of(name, 2 * k + 1)] = end

        def bank(j):
            return banks[j % 8]

        filled = [sem(f"bank{b}_filled") for b in range(8)]
        read = [sem(f"bank{b}_read") for b in range(8)]

        def wait_filled(eng, j):
            if j in unit_of:
                eng.wait_ge(units_used, unit_of[j])
            else:
                eng.wait_ge(filled[j % 8], J.own[j])

        def wait_read(eng, j):
            eng.wait_ge(read[j % 8], j // 8 + 1)

        counts = {}

        def count(name):
            counts[name] = counts.get(name, 0) + 1
            return counts[name]

        const_loaded = sem("const_loaded")
        N_CONST = 14
        x_loaded = sem("x_loaded")
        landed = [sem(f"raw{s}_landed") for s in range(RAW)]
        hi_ready, lo_ready = sem("unit_high_ready"), sem("unit_low_ready")
        units_used = sem("units_used")
        x_whole, x_high, x_low = sem("x_whole"), sem("x_high"), sem("x_low")
        extra_loaded = {n: sem(f"{n}_loaded") for n in ("bias", "keys", "cmpw", "decay", "gain", "mem", "masks", "lanes")}
        block_step = sem("residual_ready")
        RES = {n: i + 1 for i, n in enumerate(("wo", "peer0", "conv", "peer1", "between", "even", "odd"))}
        dve_step, act_step = sem("dve_step"), sem("act_step")
        norm_root, norm_scaled = sem("norm_root"), sem("norm_scaled")
        scores_shifted, weights_ready = sem("scores_shifted"), sem("weights_ready")
        top_ready, top_exp = sem("top_ready"), sem("top_exp")
        top_split = sem("choices_split")
        eq_ready, onehots = sem("first_keys_compared"), sem("onehots_ready")
        products, weighted = sem("router_products"), sem("experts_weighted")
        gelu_done = sem("gelu_done")
        g_high, g_low = sem("gated_high"), sem("gated_low")
        y_ready = sem("gated_y_ready")
        roped = sem("roped")
        cmp_ready, cmp_exp_in, cmp_exp = sem("cmp_ready"), sem("cmp_exp_in"), sem("cmp_exp")
        tables = sem("rope_tables")
        stored_out = sem("output_stored")
        nsa_gate = sem("nsa_gate")
        silu_done = sem("silu_done")
        ret_ready = sem("ret_scores_ready")
        ret_root_in, ret_root = sem("ret_var"), sem("ret_root")
        conv_ready = sem("conv_ready")
        final_ready = sem("final_ready")
        gate_in = sem("gate_in")
        angle_ready = sem("angle_ready")

        def unit_wait(base, i):
            return i * 4 + base

        def split_groups():
            order, n = {}, 0
            for name, count_ in (("norm_attn", 4), ("na_oT", 4), ("norm_peer0", 4), ("norm_conv", 4), ("conv", 8),
                                 ("norm_peer1", 4), ("norm_mem", 4), ("norm_even", 4), ("even_yT", 5),
                                 ("norm_odd", 4), ("odd_yT", 9)):
                order[name] = n
                n += count_
            return order

        XG = split_groups()
        s_buf = aux_view(0, 3, TT, SEQ)
        pT_buf = aux_view(1536, 2, 2, TT, P)
        gain_bc = aux_view(2560, D)
        causal = aux_view(3584, TT, SEQ)
        cmp_mask = aux_view(4096, 2, TT, 16)
        inv_freq = aux_view(4160, ROPES)
        cmp_small = aux_view(4320, 320)
        x_tmp = aux_view(0, 2, 4 * P)
        acts = view(0, N_KEYS, SEQ)

        eT = view(E_T, 20, SEQ)
        EQ, EMQ, EMK, EEQ, EKC, EVC, EKS, EKW = 0, 4, 8, 12, 14, 15, 16, 18
        ev_proj = view(E_PROJ, TT, EVEN_W)
        od_proj = view(O_PROJ, TT, ODD_W)
        mem_kT = view(M_K, 2, 2, SEQ)
        mem_v = view(M_V, 2, TT, 256)
        oT = view(O_T, 18, SEQ)

        def half(t, h, a, b):
            r = (h % 2) * HEAD
            return t[r:r + HEAD, h // 2, a:b]

        ev_heads = []
        for name, n in SEC:
            for h in range(n):
                r, g = (h % 2) * HEAD, h // 4
                if name in ("nsa_s", "nsa_w"):
                    kt = (EKS if name == "nsa_s" else EKW) + g
                    v0 = EVEN["nvs" if name == "nsa_s" else "nvw"] + g * HEAD
                    ev_heads.append((name, h, eT[r:r + HEAD, EQ + h // 2, :], eT[r:r + HEAD, kt, :],
                                     [ev_proj[:, k, v0:v0 + HEAD] for k in range(TT)]))
                elif name == "moba":
                    v0 = EVEN["mv"] + h * HEAD
                    ev_heads.append((name, h, eT[r:r + HEAD, EMQ + h // 2, :],
                                     eT[r:r + HEAD, EMK + h // 2, :],
                                     [ev_proj[:, k, v0:v0 + HEAD] for k in range(TT)]))
                else:
                    ev_heads.append((name, h, eT[r:r + HEAD, EEQ + h // 2, :],
                                     mem_kT[r:r + HEAD, 0, h // 2, :],
                                     [mem_v[:, 0, k, h * HEAD:(h + 1) * HEAD] for k in range(TT)]))
        na_q, na_k = view(L_QT, KT, SEQ), view(L_KT, KT, SEQ)
        na_v, na_o = view(L_V, TT, D), view(L_O, TT, D)
        na_bias = view(L_BIAS, NA_HEADS, TT, SEQ)
        na_heads = [("na", h, half(na_q, h, 0, SEQ), half(na_k, h, 0, SEQ),
                     [na_v[:, k, h * HEAD:(h + 1) * HEAD] for k in range(TT)]) for h in range(NA_HEADS)]
        om_heads = [("mem_o", h, oT[(h % 2) * HEAD:(h % 2) * HEAD + HEAD, 16 + h // 2, :],
                     mem_kT[(h % 2) * HEAD:(h % 2) * HEAD + HEAD, 1, h // 2, :],
                     [mem_v[:, 1, k, h * HEAD:(h + 1) * HEAD] for k in range(TT)]) for h in range(MEM_HEADS)]
        head_base = {"na": 0, "ev": NA_HEADS, "om": NA_HEADS + len(ev_heads)}
        ev_T_src = []
        rp = E_ROPED
        e_nq, e_mq, e_mk = view(rp, TT, 512), view(rp + 1024, TT, 512), view(rp + 2048, TT, 512)
        e_kc = view(rp + 3072, TT, 128)
        e_ks, e_kw = view(rp + 3328, TT, NSA_GROUPS, 2, HEAD), view(rp + 3840, TT, NSA_GROUPS, 2, HEAD)
        for i in range(4):
            ev_T_src.append([e_nq[:, t, i * P:(i + 1) * P] for t in range(TT)])
        for i in range(4):
            ev_T_src.append([e_mq[:, t, i * P:(i + 1) * P] for t in range(TT)])
        for i in range(4):
            ev_T_src.append([e_mk[:, t, i * P:(i + 1) * P] for t in range(TT)])
        for i in range(2):
            ev_T_src.append([ev_proj[:, t, EVEN["eq"] + i * P:EVEN["eq"] + (i + 1) * P] for t in range(TT)])
        ev_T_src.append([e_kc[:, t, :] for t in range(TT)])
        ev_T_src.append([ev_proj[:, t, EVEN["nvc"]:EVEN["nvc"] + P] for t in range(TT)])
        for g in range(NSA_GROUPS):
            ev_T_src.append([e_ks[:, t, g].rearrange("p a b -> p (a b)") for t in range(TT)])
        for g in range(NSA_GROUPS):
            ev_T_src.append([e_kw[:, t, g].rearrange("p a b -> p (a b)") for t in range(TT)])
        ev_y_src = [ev_proj[:, :, EVEN["nz"] + i * P:EVEN["nz"] + (i + 1) * P] for i in range(4)]
        ev_y_src += [ev_proj[:, :, EVEN["mz"] + i * P:EVEN["mz"] + (i + 1) * P] for i in range(4)]
        ev_y_src += [ev_proj[:, :, EVEN["ez"] + i * P:EVEN["ez"] + (i + 1) * P] for i in range(2)]
        o_q, o_k = view(O_ROPED, TT, D), view(O_ROPED + 2048, TT, D)
        od_T_src = [[o_q[:, t, i * P:(i + 1) * P] for t in range(TT)] for i in range(8)]
        od_T_src += [[o_k[:, t, i * P:(i + 1) * P] for t in range(TT)] for i in range(8)]
        od_T_src += [[od_proj[:, t, ODD["eq"] + i * P:ODD["eq"] + (i + 1) * P] for t in range(TT)] for i in range(2)]
        od_y_src = [od_proj[:, :, ODD["rz"] + i * P:ODD["rz"] + (i + 1) * P] for i in range(16)]
        od_y_src += [od_proj[:, :, ODD["ez"] + i * P:ODD["ez"] + (i + 1) * P] for i in range(2)]
        decay = view(O_DECAY, RET_HEADS, SEQ)
        ret_buf = aux_view(0, 2, 3, P)
        cosT, sinT = view(ROPE_AT, TT, ROPES), view(ROPE_AT + TT * ROPES, TT, ROPES)
        cmp_T = {"k": eT[:, EKC, :], "v": eT[:, EVC, :]}
        w1 = {"k": view(E_W1K, CMP_LEN, HEAD), "v": view(E_W1V, CMP_LEN, HEAD)}
        ape = {"k": view(E_APE, CMP_LEN, N_CMP), "v": view(E_APE + CMP_LEN * N_CMP, CMP_LEN, N_CMP)}
        hid_sb = cmp_small[:, 0:32].rearrange("p (a n) -> p a n", a=2)
        kcT = cmp_small[:, 32:64].rearrange("p (g n) -> p g n", g=2)
        hid_rep = cmp_small[:, 64:192].rearrange("p (i n) -> p i n", i=4)
        cmp_s = view(E_TMP, TT, NSA_HEADS, 32)
        vbd = view(E_APE, NSA_GROUPS, 4, HEAD)
        cmp_pT = view(E_TMP + 512, TT, NSA_GROUPS, P)
        nsa_o = view(E_NSA, TT, 512)

        def top_out(t, i):
            return view(P_TOP, TT, 3, HK)[:, t, i, :]

        NORM_ORDER = ("attn", "peer0", "conv", "peer1", "mem", "even", "odd")
        block = ctx.enter_context(nc.Block())

        @block.sync
        def _(sp):
            for t in range(TT):
                sp.dma_start(resid[:, t, :], d["x"][t * P:(t + 1) * P, :]).then_inc(x_loaded, 16)

            def load(n):
                src, kts, cols = units[n]
                if n >= RAW:
                    sp.wait_ge(lo_ready, n - RAW + 1)
                dst = raw[:, n % RAW, 0:kts * cols].rearrange("p (k n) -> p k n", k=kts)
                sp.dma_start(dst, src).then_inc(landed[n % RAW], 16)

            n = 0
            while n < len(units):
                if units[n] is not None:
                    load(n)
                    n += 1
                    continue
                layer = 0 if n == first_unit["up0"] else 1
                for name in ("w_upT", "w_down"):
                    with sp.Fori(0, N_KEYS // RAW) as i:
                        for k in range(RAW):
                            sp.wait_ge(lo_ready, unit_wait(n + k - RAW + 1, i))
                            src = d[name][bass.ds(i * RAW + (layer * N_KEYS + k), 1)]
                            sp.dma_start(raw[:, (n + k) % RAW, :], src.rearrange("a p n -> p (a n)"))\
                                .then_inc(landed[(n + k) % RAW], 16)
                    n += N_KEYS
            sp.wait_ge(final_ready, 1)
            for t in range(TT):
                sp.dma_start(out[t * P:(t + 1) * P, :], resid[:, t, :]).then_inc(stored_out, 16)
            sp.wait_ge(stored_out, 16 * TT)

        @block.gpsimd
        def _(pool):
            def const(dst, src):
                pool.dma_start(dst, src).then_inc(const_loaded, 16)

            const(ident[:], d["c_ident"])
            const(gains[:], d["gains"])
            pool.dma_start(na_bias, d["na_bias"]).then_inc(extra_loaded["bias"], 16)
            const(iota[:], d["c_iota"].partition_broadcast(P))
            const(convw[:], d["conv_w"])
            const(pos_i[:], d["positions"])
            const(gate_b[:], d["gate_b"].partition_broadcast(P))
            const(pe_k[:], d["pe_k"])
            const(pe_v[:], d["pe_v"])
            for dup in range(2):
                const(w2k[dup * HEAD:(dup + 1) * HEAD, 0, :], d["w2_k"])
                const(w2k[dup * HEAD:(dup + 1) * HEAD, 1, :], d["w2_k"])
            const(w2v[0:HEAD, :], d["w2_v"])
            const(w2v[HEAD:P, :], d["w2_v"])
            def dump(name):
                if DEBUG:
                    pool.wait_ge(block_step, RES[name])
                    pool.dma_start(d["dbg"][RES[name] - 1], resid[:]).then_inc(sem("dbg"), 16)

            for layer, done in enumerate(("wo", "conv")):
                pool.wait_ge(block_step, RES[done])
                pool.dma_start(view(P_KEYS, HP, N_KEYS), d["keysT"][layer])\
                    .then_inc(extra_loaded["keys"], 16)
                pool.wait_ge(x_low, XG[f"norm_peer{layer}"] + 4)
                pool.dma_start(lanes[:], d["c_lanes"].partition_broadcast(P)).then_inc(extra_loaded["lanes"], 16)
                dump(done)
                dump(("peer0", "peer1")[layer])
            pool.wait_ge(block_step, RES["peer1"])
            for t in range(TT):
                pool.dma_start(view(0, TT, D)[:, t, :], d["mem"][t * P:(t + 1) * P, :])\
                    .then_inc(extra_loaded["mem"], 16)
            pool.dma_start(gain_bc, d["norm_final"].partition_broadcast(P)).then_inc(extra_loaded["gain"], 16)
            pool.dma_start(inv_freq, d["c_inv_freq"].partition_broadcast(P)).then_inc(extra_loaded["masks"], 16)
            pool.dma_start(causal, d["c_causal"]).then_inc(extra_loaded["masks"], 16)
            pool.dma_start(cmp_mask, d["c_cmp_mask"]).then_inc(extra_loaded["masks"], 16)
            for kv in "kv":
                for g in range(NSA_GROUPS):
                    pool.dma_start(w1[kv][g * HEAD:(g + 1) * HEAD], d[f"w1_{kv}"])\
                        .then_inc(extra_loaded["cmpw"], 16)
            dump("between")
            pool.wait_ge(block_step, RES["even"])
            pool.dma_start(decay, d["c_decay"]).then_inc(extra_loaded["decay"], 16)
            pool.dma_start(gain_bc, d["final_norm"].partition_broadcast(P)).then_inc(extra_loaded["gain"], 16)
            dump("even")
            dump("odd")

        @block.tensor
        def _(pe):
            pe.wait_ge(const_loaded, 16 * N_CONST)
            at = [0]

            def take(name, k):
                j = J.of(name, k)
                assert j == at[0], (name, k, j, at[0])
                at[0] += 1
                if j >= 8:
                    pe.wait_ge(read[j % 8], j // 8)
                return j

            def done(ins, j):
                ins.then_inc(filled[j % 8], 1)

            unit = [0]

            def split_ready(name, n):
                pe.wait_ge(x_low, XG[name] + n)

            def norm(name):
                for g in range(4):
                    j = take(f"norm_{name}", g)
                    t, k0 = g // 2, (g % 2) * 4
                    if g % 2 == 0:
                        pe.wait_ge(norm_scaled, count("pe_norm"))
                    xs = view(A_XS, TT, D)
                    for k in range(4):
                        last = pe.transpose(bank(j)[:, k * P:(k + 1) * P],
                                            xs[:, t, (k0 + k) * P:(k0 + k + 1) * P], ident[:])
                    done(last, j)

            def project(name, forms, lhs, tiles=KT, k=0):
                for form in forms:
                    js = [take(name, k), take(name, k + 1)]
                    k += 2
                    for k0 in range(0, tiles, UKT):
                        n = unit[0]
                        cols = units[n][2]
                        w = [t[:, n % SPLIT, 0:UKT * cols].rearrange("p (k n) -> p k n", k=UKT) for t in (wh, wl)]
                        for part in range(2):
                            pe.wait_ge((hi_ready, lo_ready)[part], n + 1)
                            for kk in range(UKT):
                                kt = k0 + kk
                                for xp in range(2 - part):
                                    x = lhs[xp]
                                    flags = {"start": kt == 0 and part == 0 and xp == 0,
                                             "stop": kt == tiles - 1 and part == 1, "skip_group_check": True}
                                    for b in range(2):
                                        if form == "N":
                                            last = pe.matmul(bank(js[b])[:, 0:cols], lhsT=x[:, kt, b * P:(b + 1) * P],
                                                             rhs=w[part][:, kk, :], **flags)
                                        elif form == "T" or b == 0:
                                            for m in range(2):
                                                c0 = (2 * b + m) * P
                                                f = dict(flags, start=flags["start"] and m == 0)
                                                last = pe.matmul(bank(js[b])[:, m * SEQ:(m + 1) * SEQ],
                                                                 lhsT=w[part][:, kk, c0:c0 + P], rhs=x[:, kt, :], **f)
                                        else:
                                            for m in range(2):
                                                f = dict(flags, start=flags["start"] and m == 0)
                                                last = pe.matmul(bank(js[b])[:, m * 256:(m + 1) * 256],
                                                                 lhsT=x[:, kt, m * P:(m + 1) * P],
                                                                 rhs=w[part][:, kk, 256:512], **f)
                        last.then_inc(units_used, 1)
                        unit[0] += 1
                return k

            def transposes(name, groups, ready):
                for k, group in enumerate(groups):
                    j = take(name, k)
                    ready(k)
                    for q, src in enumerate(group):
                        last = pe.transpose(bank(j)[:, q * P:(q + 1) * P], src, ident[:])
                    done(last, j)

            def attention(name, order, heads, base):
                for k, (kind, a) in enumerate(order):
                    j = take(name, k)
                    _, _, qT, kT, v = heads[a]
                    if kind == "S":
                        for t in range(TT):
                            last = pe.matmul(bank(j)[:, t * SEQ:(t + 1) * SEQ], lhsT=qT[:, t * P:(t + 1) * P], rhs=kT,
                                             start=True, stop=True)
                    elif kind == "T":
                        pe.wait_ge(weights_ready, base + a + 1)
                        for kt in range(2):
                            for t in range(TT):
                                q = kt * TT + t
                                last = pe.transpose(bank(j)[:, q * P:(q + 1) * P],
                                                    s_buf[:, (base + a) % 3, t, kt * P:(kt + 1) * P], ident[:])
                    else:
                        wait_read(pe, J.of(name, order.index(("T", a))))
                        for t in range(TT):
                            for kt in range(2):
                                last = pe.matmul(bank(j)[:, t * HEAD:(t + 1) * HEAD],
                                                 lhsT=pT_buf[:, (base + a) % 2, kt, t, :], rhs=v[kt],
                                                 start=(kt == 0), stop=(kt == 1))
                    done(last, j)

            def peer(layer):
                split_ready(f"norm_peer{layer}", 4)
                project(f"query{layer}", "TTTT", x_in)
                qT = view(P_QT, HP, SEQ)
                keys = view(P_KEYS, HP, N_KEYS)
                pe.wait_ge(extra_loaded["keys"], 16 * (layer + 1))
                for k in range(8):
                    t, q = k // 4, k % 4
                    j = take(f"scores{layer}", k)
                    for i in range(2):
                        wait_read(pe, J.of(f"query{layer}", 2 * q + i))
                    for i in range(4):
                        last = pe.matmul(bank(j)[:, i * P:(i + 1) * P], lhsT=qT[:, 4 * q + i, t * P:(t + 1) * P],
                                         rhs=keys[:, 4 * q + i, :], start=True, stop=True)
                    done(last, j)
                u0, d0 = first_unit[f"up{layer}"], first_unit[f"down{layer}"]
                for j in range(at[0] - 8, at[0]):
                    wait_read(pe, j)
                g0, q0 = 64 * layer, 128 * layer

                def up(t, i=0):
                    n, b = u0 + t, t % 2
                    w = [x[:, n % SPLIT, :].rearrange("p (k e) -> p k e", k=KT) for x in (wh, wl)]
                    if t >= 2 or not isinstance(i, int):
                        pe.wait_ge(gelu_done, unit_wait(N_KEYS * layer + t - 1, i))
                    for part in range(2):
                        pe.wait_ge((hi_ready, lo_ready)[part], unit_wait(n + 1, i))
                        for k in range(KT):
                            for xp in range(2 - part):
                                last = pe.matmul(banks[b][:, 0:SEQ], lhsT=w[part][:, k, :], rhs=x_in[xp][:, k, :],
                                                 start=(k == 0 and part == 0 and xp == 0), stop=(k == KT - 1 and part == 1))
                    last.then_inc(units_used, 1)

                def down(t, i=0, start=False, stop=False):
                    n = d0 + t
                    g = [x[:, t % SPLIT, :] for x in (gh, gl)]
                    for part in range(2):
                        pe.wait_ge((hi_ready, lo_ready)[part], unit_wait(n + 1, i))
                        w = (wh, wl)[part][:, n % SPLIT, :]
                        for gp in range(2 - part):
                            if part == 0:
                                pe.wait_ge((g_high, g_low)[gp], unit_wait(N_KEYS * layer + t + 1, i))
                            for m in range(TT):
                                for h in range(2):
                                    last = pe.matmul(banks[4 + 2 * m + h][:, :], lhsT=g[gp][:, m * P:(m + 1) * P],
                                                     rhs=w[:, h * 512:(h + 1) * 512],
                                                     start=start and part == 0 and gp == 0, stop=stop and part == 1)
                    last.then_inc(units_used, 1)

                def router(half, q, i=0):
                    s, c0 = q // 2 % 2, q % 2 * 4
                    pe.wait_ge(onehots, i * 2 + (g0 + 32 * half + q // 2 + 1))
                    if half or q >= 2 or not isinstance(i, int):
                        pe.wait_ge(weighted, unit_wait(q0 + 64 * half + q - 1, i))
                    for c in range(4):
                        for p in range(3):
                            last = pe.matmul(banks[2 + q % 2][:, c * HALF:(c + 1) * HALF],
                                             lhsT=second[:, s, :, c0 + c], rhs=first[:, s, p, :, c0 + c],
                                             start=(p == 0), stop=(p == 2))
                    last.then_inc(products, 1)

                for t in range(2):
                    up(t)
                with pe.Fori(0, (HALF - 4) // 4) as i:
                    for t in range(2, 6):
                        up(t, i)
                for t in range(HALF - 2, HALF + 2):
                    up(t)
                for t in range(TT):
                    j = take(f"idxT{layer}", t)
                    if t == 0:
                        pe.wait_ge(gelu_done, N_KEYS * layer + HALF + 2)
                    pe.wait_ge(top_ready, 4 * layer + 2 + t + 1)
                    for i in range(3):
                        last = pe.transpose(bank(j)[:, i * P:(i + 1) * P], top_out(t, i), ident[:])
                    done(last, j)
                for t in range(TT):
                    wait_read(pe, J.of(f"idxT{layer}", t))
                for t in range(HALF + 2, HALF + LEAD):
                    up(t)
                for k in range(4):
                    up(HALF + LEAD + k)
                    router(0, k)
                with pe.Fori(1, (HALF - LEAD) // 4) as i:
                    for k in range(4):
                        up(HALF + LEAD + k, i)
                        router(0, k, i)
                for q in range(HALF - LEAD, HALF):
                    router(0, q)
                for k in range(4):
                    down(k, start=(k == 0))
                    router(1, k)
                with pe.Fori(1, HALF // 4) as i:
                    for k in range(4):
                        down(k, i)
                        router(1, k, i)
                with pe.Fori(HALF // 4, N_KEYS // 4 - 1) as i:
                    for k in range(4):
                        down(k, i)
                for t in range(N_KEYS - 4, N_KEYS):
                    down(t, stop=(t == N_KEYS - 1))
                unit[0] += 2 * N_KEYS

            norm("attn")
            split_ready("norm_attn", 4)
            project("qkv", "TTTTNN", x_in)
            for k in range(12):
                wait_read(pe, J.of("qkv", k))
            attention("na", NA, na_heads, head_base["na"])
            for a in range(NA_HEADS):
                wait_read(pe, J.of("na", NA.index(("O", a))))
            transposes("na_oT", [[na_o[:, t, i * P:(i + 1) * P] for i in (2 * g, 2 * g + 1) for t in range(TT)]
                                 for g in range(4)], lambda k: None)
            split_ready("na_oT", 4)
            project("wo", "NN", na_out)
            norm("peer0")
            peer(0)
            norm("conv")
            split_ready("norm_conv", 4)
            project("conv_in", "TTTTTT", x_in)
            split_ready("conv", KT)
            project("conv_out", "NN", conv_out)
            norm("peer1")
            peer(1)
            for _ in range(TT):
                count("pe_norm")
            norm("mem")
            split_ready("norm_mem", 4)
            project("mem0", "M", mem_in_T)
            project("mem1", "M", mem_in_T)
            norm("even")
            split_ready("norm_even", 4)
            project("even_in", "N" * 9, x_in)
            for k in range(18):
                wait_read(pe, J.of("even_in", k))
            pe.wait_ge(roped, 1)
            transposes("even_T", [[ev_T_src[i][t] for i in (2 * g, 2 * g + 1) for t in range(TT)] for g in range(10)],
                       lambda k: None)
            pe.wait_ge(extra_loaded["cmpw"], 64)
            pe.wait_ge(cmp_ready, 1)
            for g in range(NSA_GROUPS):
                j = take("hid", g)
                r = g * HEAD
                for i, kv in enumerate("kv"):
                    for l in range(CMP_LEN):
                        last = pe.matmul(bank(j)[r:r + HEAD, i * 16:i * 16 + N_CMP], lhsT=w1[kv][r:r + HEAD, l, :],
                                         rhs=ape[kv][r:r + HEAD, l, :], start=(l == 0), stop=(l == CMP_LEN - 1))
                done(last, j)
            pe.wait_ge(cmp_ready, 2)
            for g in range(NSA_GROUPS):
                j = take("kvc", g)
                r = g * HEAD
                pe.matmul(bank(j)[:, 0:N_CMP], lhsT=w2k[r:r + HEAD].rearrange("p a b -> p (a b)"),
                          rhs=hid_sb[r:r + HEAD, 0, 0:N_CMP], start=True, stop=True)
                last = pe.matmul(bank(j)[:, 64:64 + HEAD], lhsT=hid_rep[r:r + HEAD].rearrange("p a b -> p (a b)"),
                                 rhs=w2v[r:r + HEAD, :], start=True, stop=True)
                done(last, j)
            for g in range(NSA_GROUPS):
                wait_read(pe, J.of("kvc", g))
            for g in range(10):
                wait_read(pe, J.of("even_T", g))
            for par in range(2):
                j = take("cmp_S", par)
                for hh in range(4):
                    h = 2 * hh + par
                    for t in range(TT):
                        c0 = (hh * TT + t) * 16
                        last = pe.matmul(bank(j)[:, c0:c0 + N_CMP],
                                         lhsT=eT[par * HEAD:par * HEAD + HEAD, EQ + hh, t * P:(t + 1) * P],
                                         rhs=kcT[par * HEAD:par * HEAD + HEAD, h // 4, 0:N_CMP], start=True, stop=True)
                done(last, j)
            j = take("cmp_T", 0)
            pe.wait_ge(cmp_ready, 3)
            for t in range(TT):
                for g in range(NSA_GROUPS):
                    q = t * 2 + g
                    last = pe.transpose(bank(j)[:, q * P:(q + 1) * P],
                                        cmp_s[:, t, 4 * g:4 * g + 4, :].rearrange("p a b -> p (a b)"), ident[:])
            done(last, j)
            wait_read(pe, J.of("cmp_T"))
            for t in range(TT):
                j = take("cmp_O", t)
                for g in range(NSA_GROUPS):
                    last = pe.matmul(bank(j)[:, g * 256:(g + 1) * 256], lhsT=cmp_pT[:, t, g, :],
                                     rhs=vbd[:, g].rearrange("p a b -> p (a b)"), start=True, stop=True)
                done(last, j)
            attention("ev", EV, ev_heads, head_base["ev"])
            pe.wait_ge(y_ready, 1)
            transposes("even_yT", [[ev_y_src[i][:, t, :] for i in (2 * g, 2 * g + 1) for t in range(TT)] for g in range(5)],
                       lambda k: None)
            split_ready("even_yT", 5)
            project("even_out", "NN", ev_out, EVEN_OUT // P)
            norm("odd")
            split_ready("norm_odd", 4)
            project("odd_in", "N" * 13, x_in)
            for k in range(26):
                wait_read(pe, J.of("odd_in", k))
            pe.wait_ge(roped, 2)
            transposes("odd_T", [[od_T_src[i][t] for i in (2 * g, 2 * g + 1) for t in range(TT)] for g in range(9)],
                       lambda k: None)
            for g in range(9):
                wait_read(pe, J.of("odd_T", g))
            for kind, h in RET:
                j = take("ret", ret_job[kind, h])
                if kind == "S":
                    for kt, q0, q1, c0 in ((0, 0, SEQ, 0), (1, P, SEQ, SEQ)):
                        for dd in range(2):
                            last = pe.matmul(bank(j)[:, c0:c0 + q1 - q0], lhsT=oT[:, 8 + 2 * h + dd, kt * P:(kt + 1) * P],
                                             rhs=oT[:, 2 * h + dd, q0:q1], start=(dd == 0), stop=(dd == 1))
                    done(last, j)
                else:
                    pe.wait_ge(ret_ready, h + 1)
                    for t in range(TT):
                        if t:
                            j = take("ret", ret_job[kind, h] + 1)
                        for kt in range(t + 1):
                            last = pe.matmul(bank(j)[:, :], lhsT=ret_buf[:, h % 2, t if kt == 0 else 2, :],
                                             rhs=od_proj[:, kt, ODD["rv"] + h * RET_V:ODD["rv"] + (h + 1) * RET_V],
                                             start=(kt == 0), stop=(kt == t))
                        done(last, j)
            attention("om", OM, om_heads, head_base["om"])
            pe.wait_ge(y_ready, 2)
            transposes("odd_yT", [[od_y_src[i][:, t, :] for i in (2 * g, 2 * g + 1) for t in range(TT)] for g in range(9)],
                       lambda k: None)
            split_ready("odd_yT", 9)
            project("odd_out", "NN", od_out, ODD_OUT // P)
            assert at[0] == J.n

        @block.scalar
        def _(act):
            def step(ins):
                ins.then_inc(act_step, 1)
                act.wait_ge(act_step, count("act"))

            def evac(dst, j, src=None, func=ACT.Copy, scale=1.0):
                wait_filled(act, j)
                act.activation(dst, bank(j)[:, :] if src is None else src, func, scale=scale).then_inc(read[j % 8], 1)
                wait_read(act, j)

            eps = small[:, 60:61]
            issued = [0]

            def high(n, i=0):
                kts, cols = (1, UNIT) if units[n] is None else units[n][1:]
                act.wait_ge(landed[n % RAW], i * 16 + 16 * (n // RAW + 1))
                if n >= SPLIT:
                    act.wait_ge(units_used, unit_wait(n - SPLIT + 1, i))
                act.activation(wh[:, n % SPLIT, 0:kts * cols], raw[:, n % RAW, 0:kts * cols], ACT.Copy)\
                    .then_inc(hi_ready, 1)

            def highs(end):
                while issued[0] < min(end + SPLIT, len(units)):
                    high(issued[0])
                    issued[0] += 1

            def split_x(name, dst, tiles_of=2, count_=4, whole=None):
                for g in range(count_):
                    n = XG[name] + g
                    if whole is None:
                        j = J.of(name, g)
                        wait_filled(act, j)
                        act.activation(dst[0][:, 2 * g:2 * g + 2, :].rearrange("p a b -> p (a b)"), bank(j)[:, :],
                                       ACT.Copy).then_inc(x_high, 1)
                    else:
                        act.wait_ge(x_whole, whole(g)[0])
                        act.activation(whole(g)[1], whole(g)[2], ACT.Copy).then_inc(x_high, 1)

            def norm_split(name, dst=x_in):
                t0 = NORM_ORDER.index(name) * 4

                def whole(g):
                    t, k0 = g // 2, (g % 2) * 4
                    return (t0 + g + 1, dst[0][:, k0:k0 + 4, t * P:(t + 1) * P],
                            x_tmp[:, g % 2].rearrange("p (k q) -> p k q", k=4))

                split_x(f"norm_{name}", dst, whole=whole)

            def norm(src, ready):
                ready()
                n = count("norm_a")
                for t in range(TT):
                    step(act.activation(view(A_XS, TT, D)[:, t, :], src[:, t, :], ACT.Square,
                                        accum_out=small[:, t:t + 1]))
                act.activation(small[:, 2:4], small[:, 0:2], ACT.Sqrt, bias=eps, scale=1.0 / D).then_inc(norm_root, 1)
                act.wait_ge(norm_root, n)

            def attention(name, order, heads, base):
                for kind, a in order:
                    n = base + a
                    if kind == "S":
                        act.wait_ge(scores_shifted, n + 1)
                        for t in range(TT):
                            ins = act.activation(s_buf[:, n % 3, t, :], s_buf[:, n % 3, t, :], ACT.Exp,
                                                 bias=small[:, 8 + (n % 4) * 2 + t:9 + (n % 4) * 2 + t],
                                                 accum_out=small[:, 16 + (n % 4) * 2 + t:17 + (n % 4) * 2 + t])
                            if t == 0:
                                step(ins)
                        ins.then_inc(weights_ready, 1)
                        act.wait_ge(weights_ready, n + 1)
                    elif kind == "T":
                        evac(pT_buf[:, n % 2].rearrange("p a b c -> p (a b c)"), J.of(name, order.index(("T", a))))

            def peer(layer):
                norm_split(f"peer{layer}")
                qT = view(P_QT, HP, SEQ)
                for k in range(8):
                    highs(unit_of[J.of(f"query{layer}", k)])
                    evac(qT[:, 2 * k:2 * k + 2, :].rearrange("p a b -> p (a b)"), J.of(f"query{layer}", k))
                sc = view(P_SC, TT, HP, N_KEYS)
                for k in range(8):
                    t, q = k // 4, k % 4
                    evac(sc[:, t, 4 * q:4 * q + 4, :].rearrange("p a b -> p (a b)"), J.of(f"scores{layer}", k))
                u0, d0 = first_unit[f"up{layer}"], first_unit[f"down{layer}"]
                assert issued[0] == u0 + SPLIT

                def gelu(t, i=0):
                    act.wait_ge(units_used, unit_wait(u0 + t + 1, i))
                    dst = acts[:, bass.ds(i * 4 + t, 1), :].rearrange("p a b -> p (a b)")
                    act.activation(dst, banks[t % 2][:, 0:SEQ], ACT.Gelu).then_inc(gelu_done, 1)

                def tiles(t0, t1):
                    with act.Fori(0, (t1 - t0) // 4) as i:
                        for k in range(4):
                            gelu(t0 + k, i)
                            high(u0 + t0 + k + SPLIT, i)

                tiles(0, HALF)
                for t in range(TT):
                    act.wait_ge(top_ready, 4 * layer + t + 1)
                    g = top_out(t, 2)
                    act.activation(g, g, ACT.Exp).then_inc(top_exp, 1)
                tiles(HALF, N_KEYS)

                def gated_high(t, i=0):
                    if t >= SPLIT or not isinstance(i, int):
                        act.wait_ge(units_used, unit_wait(d0 + t - SPLIT + 1, i))
                    src = acts[:, bass.ds(i * 4 + t, 1), :].rearrange("p a b -> p (a b)")
                    act.activation(gh[:, t % SPLIT, :], src, ACT.Copy).then_inc(g_high, 1)

                act.wait_ge(weighted, 128 * layer + 64)
                for t in range(SPLIT):
                    gated_high(t)
                with act.Fori(0, HALF // 4 - 1) as i:
                    for k in range(2, 6):
                        high(d0 + k, i)
                        gated_high(k, i)
                for t in range(HALF - 2, HALF):
                    high(d0 + t)
                    gated_high(t)
                act.wait_ge(weighted, 128 * layer + 128)
                with act.Fori(0, HALF // 4 - 1) as i:
                    for k in range(HALF, HALF + 4):
                        high(d0 + k, i)
                        gated_high(k, i)
                for t in range(N_KEYS - 4, N_KEYS):
                    high(d0 + t)
                    gated_high(t)
                issued[0] = d0 + N_KEYS
                highs(d0 + N_KEYS)

            def residual(n):
                return lambda: act.wait_ge(block_step, n)

            def first():
                act.wait_ge(x_loaded, 16 * TT)
                act.wait_ge(dve_step, 1)

            norm(resid, first)
            norm_split("attn")
            for k in range(4):
                highs(unit_of[J.of("qkv", k)])
                evac(na_q[:, 2 * k:2 * k + 2, :].rearrange("p a b -> p (a b)"), J.of("qkv", k), scale=HEAD ** -0.5)
            for k in range(8, 12):
                c, t = (k - 8) // 2, k % 2
                highs(unit_of[J.of("qkv", k)])
                evac(na_v[:, t, c * CHUNK:(c + 1) * CHUNK], J.of("qkv", k))
            attention("na", NA, na_heads, head_base["na"])
            split_x("na_oT", na_out)
            highs(unit_of[J.of("wo", 3)])
            norm(resid, residual(RES["wo"]))
            peer(0)
            norm(resid, residual(RES["peer0"]))
            norm_split("conv")
            for k in range(8):
                dst = view(C_GATE if k < 4 else C_C, KT, SEQ)
                highs(unit_of[J.of("conv_in", k)])
                evac(dst[:, 2 * (k % 4):2 * (k % 4) + 2, :].rearrange("p a b -> p (a b)"), J.of("conv_in", k))
            highs(unit_of[J.of("conv_in", 11)])
            for k in range(KT):
                act.wait_ge(conv_ready, k + 1)
                act.activation(conv_out[0][:, k], view(C_Y, KT, SEQ)[:, k], ACT.Copy).then_inc(x_high, 1)
            highs(unit_of[J.of("conv_out", 3)])
            norm(resid, residual(RES["conv"]))
            peer(1)
            norm(resid, residual(RES["peer1"]))
            mem_rows = view(0, TT, D)

            def mem_in():
                act.wait_ge(block_step, RES["between"])
                act.wait_ge(extra_loaded["mem"], 16 * TT)

            norm(mem_rows, mem_in)
            norm_split("mem", mem_in_T)
            for l in range(2):
                highs(unit_of[J.of(f"mem{l}", 0)])
                evac(mem_kT[:, l].rearrange("p a b -> p (a b)"), J.of(f"mem{l}", 0))
                evac(mem_v[:, l].rearrange("p a b -> p (a b)"), J.of(f"mem{l}", 1))
            norm(resid, residual(RES["between"]))
            norm_split("even")
            act.wait_ge(angle_ready, 1)
            act.activation(view(ROPE_AT, 2 * TT * ROPES), view(ROPE_AT, 2 * TT * ROPES), ACT.Sin).then_inc(tables, 1)
            act.wait_ge(tables, 1)
            for k in range(18):
                c, t = k // 2, k % 2
                n = min(CHUNK, EVEN_W - c * CHUNK)
                j = J.of("even_in", k)
                highs(unit_of[j])
                evac(ev_proj[:, t, c * CHUNK:c * CHUNK + n], j, bank(j)[:, 0:n])
            for name, w in (("nz", 512), ("mz", 512), ("ez", 256)):
                z = ev_proj[:, :, EVEN[name]:EVEN[name] + w]
                act.activation(z, z, ACT.Silu).then_inc(silu_done, 1)
            act.wait_ge(silu_done, 3)
            act.wait_ge(gate_in, 1)
            gates = ev_proj[:, :, EVEN["ng"]:EVEN["ng"] + 24]
            act.activation(gates, gates, ACT.Sigmoid).then_inc(nsa_gate, 1)
            for k in range(10):
                if k == 7:
                    continue
                evac(eT[:, 2 * k:2 * k + 2, :].rearrange("p a b -> p (a b)"), J.of("even_T", k))
            for g in range(NSA_GROUPS):
                r = g * HEAD
                j = J.of("hid", g)
                evac(hid_sb[r:r + HEAD, :, 0:N_CMP], j, bank(j)[r:r + HEAD, 0:32].rearrange("p (a n) -> p a n", a=2)[:, :, 0:N_CMP],
                     ACT.Silu)
            act.wait_ge(cmp_exp_in, 1)
            cs = cmp_s.rearrange("p t h n -> p (t h) n")[:, :, 0:N_CMP]
            act.activation(cs, cs, ACT.Exp).then_inc(cmp_exp, 1)
            evac(cmp_pT.rearrange("p t g q -> p (t g q)"), J.of("cmp_T"))
            attention("ev", EV, ev_heads, head_base["ev"])
            split_x("even_yT", ev_out, count_=5)
            highs(unit_of[J.of("even_out", 3)])
            norm(resid, residual(RES["even"]))
            norm_split("odd")
            for k in range(26):
                c, t = k // 2, k % 2
                highs(unit_of[J.of("odd_in", k)])
                evac(od_proj[:, t, c * CHUNK:(c + 1) * CHUNK], J.of("odd_in", k))
            for t in range(TT):
                z = od_proj[:, t, ODD["rz"]:ODD["rz"] + RET_HEADS * RET_V]
                act.activation(z, z, ACT.Silu).then_inc(silu_done, 1)
            z = od_proj[:, :, ODD["ez"]:ODD["ez"] + 256]
            act.activation(z, z, ACT.Silu).then_inc(silu_done, 1)
            for k in range(9):
                evac(oT[:, 2 * k:2 * k + 2, :].rearrange("p a b -> p (a b)"), J.of("odd_T", k))
            for h in range(RET_HEADS):
                for t in range(TT):
                    n = TT * h + t
                    act.wait_ge(ret_root_in, n + 1)
                    act.activation(small[:, 30 + n:31 + n], ret_stats[:, n, 1:2], ACT.Sqrt, bias=eps).then_inc(ret_root, 1)
            attention("om", OM, om_heads, head_base["om"])
            split_x("odd_yT", od_out, count_=9)
            highs(unit_of[J.of("odd_out", 3)])
            norm(resid, residual(RES["odd"]))

        @block.vector
        def _(dve):
            def step(ins):
                ins.then_inc(dve_step, 1)
                dve.wait_ge(dve_step, count("dve"))

            def tell(ins, s, n):
                ins.then_inc(s, 1)
                dve.wait_ge(s, n)

            def read_out(ins, j):
                ins.then_inc(read[j % 8], 1)
                wait_read(dve, j)

            tt, ts, stt = dve.tensor_tensor, dve.tensor_scalar, dve.scalar_tensor_tensor
            step(dve.memset(small[:, 60:61], EPS))
            issued = [0]

            def low(n, i=0):
                kts, cols = (1, UNIT) if units[n] is None else units[n][1:]
                dve.wait_ge(hi_ready, unit_wait(n + 1, i))
                tt(wl[:, n % SPLIT, 0:kts * cols], raw[:, n % RAW, 0:kts * cols],
                   wh[:, n % SPLIT, 0:kts * cols].bitcast(F32), ALU.subtract).then_inc(lo_ready, 1)

            def lows(end):
                while issued[0] < min(end + SPLIT, len(units)):
                    low(issued[0])
                    issued[0] += 1

            def split_low(name, dst, count_):
                for g in range(count_):
                    n, j = XG[name] + g, J.of(name, g)
                    dve.wait_ge(x_high, n + 1)
                    hi = dst[0][:, 2 * g:2 * g + 2, :].rearrange("p a b -> p (a b)")
                    lo = dst[1][:, 2 * g:2 * g + 2, :].rearrange("p a b -> p (a b)")
                    tell(tt(lo, bank(j)[:, :], hi.bitcast(F32), ALU.subtract), x_low, n + 1)
                    read_out(dve.nop(), j)

            def scale_rows(src):
                n = count("norm_v")
                dve.wait_ge(norm_root, n)
                step(dve.reciprocal(small[:, 4:6], small[:, 2:4]))
                for t in range(TT):
                    tell(ts(view(A_XS, TT, D)[:, t, :], src[:, t, :], small[:, 4 + t:5 + t], None, ALU.mult),
                         norm_scaled, 2 * (n - 1) + t + 1)

            def norm(name, src=resid, dst=x_in):
                scale_rows(src)
                i, w0, x0 = NORMS.index(name), 4 * NORM_ORDER.index(name), XG[f"norm_{name}"]

                def lower(g):
                    t, k0 = g // 2, (g % 2) * 4
                    dve.wait_ge(x_high, x0 + g + 1)
                    tell(tt(dst[1][:, k0:k0 + 4, t * P:(t + 1) * P], x_tmp[:, g % 2].rearrange("p (k q) -> p k q", k=4),
                            dst[0][:, k0:k0 + 4, t * P:(t + 1) * P].bitcast(F32), ALU.subtract), x_low, x0 + g + 1)

                for g in range(4):
                    j = J.of(f"norm_{name}", g)
                    if g >= 2:
                        lower(g - 2)
                    wait_filled(dve, j)
                    gain = gains[:, i, (g % 2) * 4:(g % 2) * 4 + 4].unsqueeze(2).to_broadcast([P, 4, P])
                    tell(tt(x_tmp[:, g % 2].rearrange("p (k q) -> p k q", k=4),
                            bank(j)[:, :].rearrange("p (k q) -> p k q", k=4), gain, ALU.mult), x_whole, w0 + g + 1)
                    read_out(dve.nop(), j)
                lower(2)
                lower(3)

            def norm_rows(n):
                scale_rows(resid)
                dve.wait_ge(extra_loaded["gain"], 16 * n)
                for t in range(TT):
                    step(tt(resid[:, t, :], view(A_XS, TT, D)[:, t, :], gain_bc, ALU.mult))

            def add_out(name):
                for k in range(4):
                    c, t = k // 2, k % 2
                    j = J.of(name, k)
                    lows(unit_of[j])
                    wait_filled(dve, j)
                    r = resid[:, t, c * CHUNK:(c + 1) * CHUNK]
                    read_out(tt(r, bank(j)[:, :], r, ALU.add), j)

            def residual_ready(n):
                dve.nop().then_inc(block_step, 1)
                dve.wait_ge(block_step, n)

            def attention(name, order, heads, base, mask, scale, finish):
                for kind, a in order:
                    n = base + a
                    if kind == "S":
                        j = J.of(name, order.index(("S", a)))
                        wait_filled(dve, j)
                        s = s_buf[:, n % 3]
                        m = mask(a)
                        src = bank(j)[:, :].rearrange("p (t k) -> p t k", t=TT)
                        if m is None:
                            read_out(ts(s, src, scale, None, ALU.mult), j)
                        else:
                            read_out(stt(s, src, scale, m, ALU.mult, ALU.add), j)
                        tell(dve.tensor_reduce(small[:, 8 + (n % 4) * 2:10 + (n % 4) * 2], s, AX, ALU.max, negate=True),
                             scores_shifted, n + 1)
                    elif kind == "O":
                        j = J.of(name, order.index(("O", a)))
                        r = small[:, 24 + (n % 2) * 2:26 + (n % 2) * 2]
                        dve.wait_ge(weights_ready, n + 1)
                        step(dve.reciprocal(r, small[:, 16 + (n % 4) * 2:18 + (n % 4) * 2]))
                        wait_filled(dve, j)
                        finish(a, j, r)

            def peer(layer):
                u0, d0 = first_unit[f"up{layer}"], first_unit[f"down{layer}"]
                lows(u0)
                sc = view(P_SC, TT, HP, N_KEYS)
                ops, tile = [0], [SPLIT]

                def between():
                    ops[0] += 1
                    if ops[0] % 4 == 0 and tile[0] < HALF:
                        low(u0 + tile[0])
                        tile[0] += 1
                at = P_TOP + TT * 3 * HK
                off = [at]

                def scratch(*shape):
                    v = view(off[0], *shape)
                    off[0] += math.prod(shape)
                    return v

                sv = scratch(HP, TOPK)
                si = scratch(HP, TOPK)
                si_f = scratch(HP, TOPK)
                rest = scratch(N_KEYS)
                cand = scratch(PEER_HEADS, TOPK * TOPK)
                rest2 = scratch(TOPK * TOPK)
                best = scratch(PEER_HEADS, TOPK)
                pos_u = scratch(PEER_HEADS, TOPK)
                part = scratch(2, HK)
                part_f = scratch(2, HK)
                pick = view(P_KEYS, PEER_HEADS, TOPK, TOPK)
                red = scratch(PEER_HEADS)
                small_w = scratch(1, P)
                assert off[0] <= ARENA

                def top16(values, index, src, tmp):
                    pstep(dve.max(values[:, 0:8], src))
                    pstep(dve.max_index(index[:, 0:8].bitcast(U32), values[:, 0:8], src))
                    pstep(dve.match_replace(tmp, values[:, 0:8], src, LOWEST))
                    pstep(dve.max(values[:, 8:16], tmp))
                    pstep(dve.max_index(index[:, 8:16].bitcast(U32), values[:, 8:16], tmp))

                def pstep(ins):
                    step(ins)
                    between()

                wait_read(dve, J.of(f"scores{layer}", 7))
                for t in range(TT):
                    for hp in range(HP):
                        if hp % 4 == 0:
                            wait_read(dve, J.of(f"scores{layer}", 4 * t + hp // 4))
                        top16(sv[:, hp], si[:, hp], sc[:, t, hp], rest)
                    pstep(dve.tensor_copy(si_f, si.bitcast(U32)))
                    svh = sv.rearrange("p (h s) k -> p h s k", s=2)
                    c4 = cand.rearrange("p h (a b) -> p h a b", b=TOPK)
                    pstep(tt(c4, svh[:, :, 0].unsqueeze(3).to_broadcast([P, PEER_HEADS, TOPK, TOPK]),
                            svh[:, :, 1].unsqueeze(2).to_broadcast([P, PEER_HEADS, TOPK, TOPK]), ALU.add))
                    for h in range(PEER_HEADS):
                        top16(best[:, h], pos_u[:, h], cand[:, h], rest2)
                    g = top_out(t, 2).rearrange("p (h k) -> p h k", k=TOPK)
                    tell(tt(g, best, best[:, :, 0:1].to_broadcast([P, PEER_HEADS, TOPK]), ALU.subtract),
                         top_ready, 4 * layer + t + 1)
                    pu = pos_u.rearrange("p h k -> p (h k)").bitcast(U32)
                    pstep(ts(part[:, 0].bitcast(U32), pu, 4, None, ALU.logical_shift_right))
                    pstep(ts(part[:, 1].bitcast(U32), pu, TOPK - 1, None, ALU.bitwise_and))
                    pstep(dve.tensor_copy(part_f, part.bitcast(U32)))
                    sih = si_f.rearrange("p (h s) k -> p h s k", s=2)
                    for i in range(2):
                        a = part_f[:, i].rearrange("p (h k) -> p h k", k=TOPK).unsqueeze(3)\
                            .to_broadcast([P, PEER_HEADS, TOPK, TOPK])
                        lane = iota[:, 0:TOPK].unsqueeze(1).unsqueeze(1).to_broadcast([P, PEER_HEADS, TOPK, TOPK])
                        pstep(tt(pick, a, lane, ALU.is_equal))
                        pstep(tt(pick, pick, sih[:, :, i].unsqueeze(2).to_broadcast([P, PEER_HEADS, TOPK, TOPK]), ALU.mult))
                        pstep(dve.tensor_reduce(top_out(t, i).rearrange("p (h k) -> p h k", k=TOPK), pick, AX, ALU.add))
                while tile[0] < HALF:
                    low(u0 + tile[0])
                    tile[0] += 1
                for t in range(TT):
                    n = TT * layer + t
                    low(u0 + HALF + t)
                    g = top_out(t, 2).rearrange("p (h k) -> p h k", k=TOPK)
                    dve.wait_ge(top_exp, n + 1)
                    step(dve.tensor_reduce(red, g, AX, ALU.add))
                    step(dve.reciprocal(red, red))
                    tell(tt(g, g, red.unsqueeze(2).to_broadcast([P, PEER_HEADS, TOPK]), ALU.mult), top_ready, 4 * layer + 2 + t + 1)
                for t in range(TT):
                    j = J.of(f"idxT{layer}", t)
                    wait_filled(dve, j)
                    cols = slice(t * P, (t + 1) * P)
                    w_rest = small_w[:, 0, :]
                    step(dve.tensor_copy(choice[:, 0:2, cols], bank(j)[:, 0:2 * P].rearrange("p (a b) -> p a b", a=2)))
                    step(dve.tensor_copy(choice[:, 2, cols], bank(j)[:, 2 * P:3 * P]))
                    read_out(tt(w_rest, bank(j)[:, 2 * P:3 * P], choice[:, 2, cols], ALU.subtract), j)
                    step(dve.tensor_copy(choice[:, 3, cols], w_rest))
                    step(tt(choice[:, 4, cols], w_rest, choice[:, 3, cols], ALU.subtract))
                dve.wait_ge(extra_loaded["lanes"], 16 * (layer + 1))
                g0, q0 = 64 * layer, 128 * layer

                def over(k, rows, c0):
                    return choice[:, k, c0].unsqueeze(1).to_broadcast([P, rows, GROUP])

                def build_keys(half, g, i=0):
                    s, c0 = g % 2, bass.ds(i * (2 * GROUP) + g * GROUP, GROUP)
                    number = g0 + 32 * half + g
                    if half or g >= 2 or not isinstance(i, int):
                        dve.wait_ge(products, i * 4 + (q0 + 64 * half + 2 * g - 2))

                    tt(first_eq[:, s], lanes[:, half * HALF:(half + 1) * HALF, :], over(0, HALF, c0), ALU.is_equal)\
                        .then_inc(eq_ready, 1)
                    tt(second[:, s], lanes[:], over(1, N_KEYS, c0), ALU.is_equal)

                def build_weights(half, g, i=0):
                    s, c0 = g % 2, bass.ds(i * (2 * GROUP) + g * GROUP, GROUP)
                    dve.wait_ge(eq_ready, i * 2 + (g0 + 32 * half + g + 1))
                    for p in range(3):
                        last = tt(first[:, s, p], first_eq[:, s], over(2 + p, HALF, c0), ALU.mult)
                    last.then_inc(onehots, 1)

                def weigh(half, q, i=0):
                    dve.wait_ge(products, unit_wait(q0 + 64 * half + q + 1, i))
                    a = acts[:, half * HALF:(half + 1) * HALF, bass.ds(i * 16 + q * 4, 4)]
                    tt(a, banks[2 + q % 2][:, 0:4 * HALF].rearrange("p (c i) -> p i c", c=4), a, ALU.mult)\
                        .then_inc(weighted, 1)

                def gated_low(t, i=0):
                    dve.wait_ge(g_high, unit_wait(N_KEYS * layer + t + 1, i))
                    src = acts[:, bass.ds(i * 4 + t, 1), :].rearrange("p a b -> p (a b)")
                    tt(gl[:, t % SPLIT, :], src, gh[:, t % SPLIT, :].bitcast(F32), ALU.subtract).then_inc(g_low, 1)

                dve.wait_ge(gelu_done, N_KEYS * layer + HALF)
                low(u0 + HALF + 2)
                build_keys(0, 0)
                low(u0 + HALF + 3)
                build_weights(0, 0)
                low(u0 + HALF + LEAD)
                build_keys(0, 1)
                build_weights(0, 1)

                def weigh_and_build(half, k, i, ahead):
                    ahead(k, i)
                    weigh(half, k, i)
                    if k % 2:
                        build_keys(half, 2 + k // 2, i)
                    elif k:
                        build_weights(half, 2, i)
                    elif not isinstance(i, int):
                        build_weights(half, 1, i)

                def low_up(k, i):
                    low(u0 + HALF + LEAD + 1 + k, i)

                def low_down(k, i):
                    low(d0 + 1 + k, i)
                    gated_low(1 + k, i)

                for k in range(4):
                    weigh_and_build(0, k, 0, low_up)
                with dve.Fori(1, (HALF - LEAD) // 4) as i:
                    for k in range(4):
                        weigh_and_build(0, k, i, low_up)
                build_weights(0, HALF // 2 - 1)
                for q in range(HALF - LEAD, HALF):
                    weigh(0, q)
                dve.wait_ge(gelu_done, N_KEYS * (layer + 1))
                gated_low(0)
                build_keys(1, 0)
                low_down(0, 0)
                build_weights(1, 0)
                build_keys(1, 1)
                build_weights(1, 1)
                for k in range(4):
                    weigh_and_build(1, k, 0, lambda k, i: low_down(k + 1, i))
                with dve.Fori(1, HALF // 4 - 1) as i:
                    for k in range(4):
                        weigh_and_build(1, k, i, lambda k, i: low_down(k + 1, i))
                build_weights(1, HALF // 2 - 1)
                for k in range(HALF - 4, HALF):
                    if k < HALF - 2:
                        low_down(k + 1, 0)
                    weigh(1, k)
                with dve.Fori(0, HALF // 4) as i:
                    for k in range(HALF, HALF + 4):
                        low(d0 + k, i)
                        gated_low(k, i)
                issued[0] = d0 + N_KEYS
                lows(d0 + N_KEYS)
                dve.wait_ge(units_used, d0 + N_KEYS)
                for t in range(TT):
                    for c in range(2):
                        r = resid[:, t, c * CHUNK:(c + 1) * CHUNK]
                        step(tt(r, banks[4 + 2 * t + c][:, :], r, ALU.add))

            dve.wait_ge(const_loaded, 16 * N_CONST)
            norm("attn")
            for k in range(4, 8):
                j = J.of("qkv", k)
                lows(unit_of[j])
                wait_filled(dve, j)
                i = 2 * (k - 4)
                read_out(dve.tensor_copy(na_k[:, i:i + 2, :].rearrange("p a b -> p (a b)"), bank(j)[:, :]), j)
            lows(unit_of[J.of("qkv", 11)])
            dve.wait_ge(extra_loaded["bias"], 16)

            def na_finish(a, j, r):
                for t in range(TT):
                    ins = ts(na_o[:, t, a * HEAD:(a + 1) * HEAD], bank(j)[:, t * HEAD:(t + 1) * HEAD], r[:, t:t + 1],
                             None, ALU.mult)
                read_out(ins, j)

            attention("na", NA, na_heads, head_base["na"], lambda a: na_bias[:, a], 1.0, na_finish)
            split_low("na_oT", na_out, 4)
            add_out("wo")
            residual_ready(RES["wo"])
            norm("peer0")
            peer(0)
            residual_ready(RES["peer0"])
            u = view(C_U, KT, SEQ + 2)
            step(dve.memset(u[:, :, 0:1], 0.0))
            step(dve.memset(u[:, :, SEQ + 1:SEQ + 2], 0.0))
            norm("conv")
            cT, gT, y = view(C_C, KT, SEQ), view(C_GATE, KT, SEQ), view(C_Y, KT, SEQ)
            for k in range(4):
                j = J.of("conv_in", 8 + k)
                lows(unit_of[j])
                wait_read(dve, J.of("conv_in", 4 + k))
                wait_filled(dve, j)
                read_out(tt(u[:, 2 * k:2 * k + 2, 1:SEQ + 1], cT[:, 2 * k:2 * k + 2, :],
                            bank(j)[:, :].rearrange("p (a b) -> p a b", a=2), ALU.mult), j)
            for k in range(4):
                wait_read(dve, J.of("conv_in", k))
            for k in range(KT):
                step(ts(y[:, k], u[:, k, 0:SEQ], convw[:, k, 0:1], None, ALU.mult))
                for tap in (1, 2):
                    step(stt(y[:, k], u[:, k, tap:tap + SEQ], convw[:, k, tap:tap + 1], y[:, k], ALU.mult, ALU.add))
                tell(tt(y[:, k], y[:, k], gT[:, k], ALU.mult), conv_ready, k + 1)
            for k in range(KT):
                dve.wait_ge(x_high, XG["conv"] + k + 1)
                tell(tt(conv_out[1][:, k], y[:, k], conv_out[0][:, k].bitcast(F32), ALU.subtract), x_low, XG["conv"] + k + 1)
            add_out("conv_out")
            residual_ready(RES["conv"])
            norm("peer1")
            peer(1)
            residual_ready(RES["peer1"])
            norm_rows(1)
            residual_ready(RES["between"])
            norm("mem", view(0, TT, D), mem_in_T)
            lows(unit_of[J.of("mem1", 0)])
            norm("even")
            pos_f = small[:, 56:58]
            step(dve.tensor_copy(pos_f, pos_i[:]))
            dve.wait_ge(extra_loaded["masks"], 16 * 3)
            two_pi = 2 * math.pi
            c1 = float(np.float32(6.28125))
            c2 = float(np.float32(two_pi - c1))
            c3 = float(two_pi - c1 - c2)
            turns = view(E_TMP, TT, ROPES)
            for t in range(TT):
                step(ts(sinT[:, t], inv_freq[:], pos_f[:, t:t + 1], None, ALU.mult))
            step(ts(turns, sinT, 1.0 / two_pi, 12582912.0, ALU.mult, ALU.add))
            step(ts(turns, turns, 12582912.0, None, ALU.subtract))
            for c in (c1, c2, c3):
                step(stt(sinT, turns, -c, sinT, ALU.mult, ALU.add))
            step(ts(sinT, sinT, 3.1415925, -3.1415925, ALU.min, ALU.max))
            step(ts(cosT, sinT, -1.0, None, ALU.mult))
            step(tt(cosT, cosT, sinT, ALU.max))
            step(ts(cosT, cosT, -1.0, math.pi / 2, ALU.mult, ALU.add))
            tell(dve.nop(), angle_ready, 1)
            dve.wait_ge(tables, 1)

            def rope(dst, src, heads, hd, f0, dups=1):
                t, dst_v, src_v = src
                x = src_v.rearrange("p (h s f) -> p h s f", s=2, f=hd // 2)
                f = hd // 2
                a = view(E_TMP, heads, 2, f)
                b = view(E_TMP + 512, heads, 2, f)
                cos = cosT[:, t, f0:f0 + f]
                sin = sinT[:, t, f0:f0 + f]
                step(tt(a, x, cos.unsqueeze(1).unsqueeze(1).to_broadcast([P, heads, 2, f]), ALU.mult))
                step(tt(b, x, sin.unsqueeze(1).unsqueeze(1).to_broadcast([P, heads, 2, f]), ALU.mult))
                for o in dst_v:
                    step(tt(o[:, :, 0], a[:, :, 0], b[:, :, 1], ALU.subtract))
                    step(tt(o[:, :, 1], a[:, :, 1], b[:, :, 0], ALU.add))

            for k in range(18):
                lows(unit_of[J.of("even_in", k)])
                wait_read(dve, J.of("even_in", k))

            def as_heads(v, hd):
                return v.rearrange("p (h s f) -> p h s f", s=2, f=hd // 2)

            gates = ev_proj[:, :, EVEN["ng"]:EVEN["ng"] + 24]
            tell(tt(gates, gates, gate_b[:].unsqueeze(1).to_broadcast([P, TT, 24]), ALU.add), gate_in, 1)
            for t in range(TT):
                for name, dst in (("nq", e_nq), ("mq", e_mq), ("mk", e_mk)):
                    rope(None, (t, [as_heads(dst[:, t], HEAD)], ev_proj[:, t, EVEN[name]:EVEN[name] + 512]), 8, HEAD, 0)
                rope(None, (t, [as_heads(e_kc[:, t], HEAD)], ev_proj[:, t, EVEN["nkc"]:EVEN["nkc"] + 128]), 2, HEAD, 0)
                for name, dst in (("nks", e_ks), ("nkw", e_kw)):
                    outs = [dst[:, t, :, dup].rearrange("p g (s f) -> p g s f", s=2) for dup in range(2)]
                    rope(None, (t, outs, ev_proj[:, t, EVEN[name]:EVEN[name] + 128]), 2, HEAD, 0)
            tell(dve.nop(), roped, 1)
            step(dve.memset(cmp_small[:], 0.0))
            j = J.of("even_T", 7)
            wait_filled(dve, j)
            read_out(dve.tensor_copy(eT[:, EKC:EKC + 2, :].rearrange("p a b -> p (a b)"), bank(j)[:, :]), j)
            for kv, pe_sb in (("k", pe_k), ("v", pe_v)):
                by = cmp_T[kv].rearrange("p (n l) -> p l n", l=CMP_STRIDE)
                for part in range(2):
                    l0 = part * CMP_STRIDE
                    step(tt(ape[kv][:, l0:l0 + CMP_STRIDE], by[:, :, part:part + N_CMP],
                            pe_sb[:, l0:l0 + CMP_STRIDE].unsqueeze(2).to_broadcast([P, CMP_STRIDE, N_CMP]), ALU.add))
            tell(dve.nop(), cmp_ready, 1)
            for g in range(NSA_GROUPS):
                wait_read(dve, J.of("hid", g))
            step(dve.tensor_copy(hid_rep[:, :, 0:N_CMP], hid_sb[:, 1:2, 0:N_CMP].to_broadcast([P, 4, N_CMP])))
            tell(dve.nop(), cmp_ready, 2)
            step(dve.memset(vbd, 0.0))
            step(dve.memset(cmp_s, 0.0))
            for g in range(NSA_GROUPS):
                j = J.of("kvc", g)
                wait_filled(dve, j)
                step(dve.tensor_copy(kcT[:, g, 0:N_CMP], bank(j)[:, 0:N_CMP]))
                for i in range(4):
                    ins = dve.tensor_copy(vbd[32 * i:32 * i + 32, g, i, :], bank(j)[32 * i:32 * i + 32, 64:64 + HEAD])
                    if i < 3:
                        step(ins)
                read_out(ins, j)
            for par in range(2):
                j = J.of("cmp_S", par)
                wait_filled(dve, j)
                src = bank(j)[:, 0:128].rearrange("p (h t n) -> p h t n", h=4, t=TT)
                for t in range(TT):
                    dst = cmp_s[:, t, par:8:2, 0:N_CMP]
                    ins = stt(dst, src[:, :, t, 0:N_CMP], HEAD ** -0.5,
                              cmp_mask[:, 0, t:t + 1, 0:N_CMP].to_broadcast([P, 4, N_CMP]), ALU.mult, ALU.add)
                    if t == 0:
                        step(ins)
                read_out(ins, j)
            cs = cmp_s.rearrange("p t h n -> p (t h) n")[:, :, 0:N_CMP]
            cm = cmp_small[:, 256:272]
            step(dve.tensor_reduce(cm, cs, AX, ALU.max))
            tell(tt(cs, cs, cm.unsqueeze(2).to_broadcast([P, 16, N_CMP]), ALU.subtract), cmp_exp_in, 1)
            dve.wait_ge(cmp_exp, 1)
            dve.wait_ge(nsa_gate, 1)
            for t in range(TT):
                c = cmp_s[:, t, :, 0:N_CMP]
                step(tt(c, c, cmp_mask[:, 1, t:t + 1, 0:N_CMP].to_broadcast([P, 8, N_CMP]), ALU.mult))
            step(dve.tensor_reduce(cm, cs, AX, ALU.add))
            step(ts(cm, cm, 1e-30, None, ALU.max))
            step(dve.reciprocal(cm, cm))
            step(tt(cm.rearrange("p (t h) -> p t h", t=TT), cm.rearrange("p (t h) -> p t h", t=TT), gates[:, :, 0:8], ALU.mult))
            step(tt(cs, cs, cm.unsqueeze(2).to_broadcast([P, 16, N_CMP]), ALU.mult))
            tell(dve.nop(), cmp_ready, 3)
            for t in range(TT):
                j = J.of("cmp_O", t)
                wait_filled(dve, j)
                read_out(dve.tensor_copy(nsa_o[:, t], bank(j)[:, :]), j)
            dve.wait_ge(silu_done, 3)

            def ev_finish(a, j, r):
                name, h = ev_heads[a][:2]
                if name in ("nsa_s", "nsa_w"):
                    br = 1 if name == "nsa_s" else 2
                    step(tt(r, r, gates[:, :, br * 8 + h:br * 8 + h + 1].rearrange("p a b -> p (a b)"), ALU.mult))
                for t in range(TT):
                    o = bank(j)[:, t * HEAD:(t + 1) * HEAD]
                    if name in ("nsa_s", "nsa_w"):
                        dst = nsa_o[:, t, h * HEAD:(h + 1) * HEAD]
                        ins = stt(dst, o, r[:, t:t + 1], dst, ALU.mult, ALU.add)
                    else:
                        z = EVEN["mz" if name == "moba" else "ez"] + h * HEAD
                        dst = ev_proj[:, t, z:z + HEAD]
                        ins = stt(dst, o, r[:, t:t + 1], dst, ALU.mult, ALU.mult)
                read_out(ins, j)

            attention("ev", EV, ev_heads, head_base["ev"],
                      lambda a: None if ev_heads[a][0] == "mem_e" else causal[:], HEAD ** -0.5, ev_finish)
            z = ev_proj[:, :, EVEN["nz"]:EVEN["nz"] + 512]
            tell(tt(z, z, nsa_o, ALU.mult), y_ready, 1)
            split_low("even_yT", ev_out, 5)
            add_out("even_out")
            residual_ready(RES["even"])
            norm("odd")
            for k in range(26):
                lows(unit_of[J.of("odd_in", k)])
                wait_read(dve, J.of("odd_in", k))
            for t in range(TT):
                for name, dst in (("rq", o_q), ("rk", o_k)):
                    for hh in range(2):
                        c = ODD[name] + hh * 512
                        rope(None, (t, [as_heads(dst[:, t, hh * 512:(hh + 1) * 512], RET_QK)], od_proj[:, t, c:c + 512]),
                             2, RET_QK, ROPE)
            tell(dve.nop(), roped, 2)
            dve.wait_ge(extra_loaded["decay"], 16)
            dve.wait_ge(silu_done, 6)
            for kind, h in RET:
                if kind == "S":
                    j = J.of("ret", ret_job[kind, h])
                    wait_filled(dve, j)
                    if h >= 2:
                        wait_filled(dve, J.of("ret", ret_job["O", h - 2] + 1))
                    step(stt(ret_buf[:, h % 2, 0:2].rearrange("p a b -> p (a b)"), bank(j)[:, 0:SEQ], RET_QK ** -0.5,
                             decay[:, h, :], ALU.mult, ALU.mult))
                    ins = stt(ret_buf[:, h % 2, 2], bank(j)[:, SEQ:SEQ + P], RET_QK ** -0.5, decay[:, h, 0:P],
                              ALU.mult, ALU.mult)
                    read_out(ins, j)
                    tell(dve.nop(), ret_ready, h + 1)
                else:
                    for t in range(TT):
                        n = TT * h + t
                        j = J.of("ret", ret_job[kind, h] + t)
                        wait_filled(dve, j)
                        step(dve.bn_stats(bn[:, 0:6], bank(j)[:, :]))
                        tell(dve.bn_aggr(ret_stats[:, n, :], bn[:, 0:6]), ret_root_in, n + 1)
                        dve.wait_ge(ret_root, n + 1)
                        step(dve.reciprocal(small[:, 38:39], small[:, 30 + n:31 + n]))
                        o = view(E_TMP, RET_V)
                        read_out(ts(o, bank(j)[:, :], ret_stats[:, n, 0:1], small[:, 38:39], ALU.subtract, ALU.mult), j)
                        z = od_proj[:, t, ODD["rz"] + h * RET_V:ODD["rz"] + (h + 1) * RET_V]
                        step(tt(z, z, o, ALU.mult))

            def om_finish(a, j, r):
                for t in range(TT):
                    z = ODD["ez"] + a * HEAD
                    dst = od_proj[:, t, z:z + HEAD]
                    ins = stt(dst, bank(j)[:, t * HEAD:(t + 1) * HEAD], r[:, t:t + 1], dst, ALU.mult, ALU.mult)
                read_out(ins, j)

            attention("om", OM, om_heads, head_base["om"], lambda a: None, HEAD ** -0.5, om_finish)
            tell(dve.nop(), y_ready, 2)
            split_low("odd_yT", od_out, 9)
            add_out("odd_out")
            residual_ready(RES["odd"])
            norm_rows(2)
            tell(dve.nop(), final_ready, 1)


def window_bias(rel_bias):
    q, k = np.arange(SEQ)[:, None], np.arange(SEQ)[None, :]
    qc, kc = q % GRID_W, k % GRID_W
    row = k // GRID_W - q // GRID_W + MAX_WIN_ROWS - 1
    start = np.clip(qc - WIN_COLS // 2, 0, GRID_W - WIN_COLS)
    inside = (kc >= start) & (kc < start + WIN_COLS)
    col = np.clip(kc - qc + WIN_COLS - 1, 0, 2 * WIN_COLS - 2)
    full = np.where(inside[None], rel_bias[:, row, col], np.float32(NEG))
    return full.reshape(NA_HEADS, TT, P, SEQ).transpose(2, 0, 1, 3)


def constants():
    q, k = np.arange(SEQ)[:, None], np.arange(SEQ)[None, :]
    causal = np.where(k <= q, 0.0, NEG).reshape(TT, P, SEQ).transpose(1, 0, 2)
    n = np.arange(16)[None, :]
    seen = (n * CMP_STRIDE + CMP_LEN - 1 <= q) & (n < N_CMP)
    cmp_mask = np.stack([np.where(seen, 0.0, NEG), seen * 1.0]).reshape(2, TT, P, 16).transpose(2, 0, 1, 3)
    f = np.float32
    inv = np.concatenate([f(1) / f(10000.0) ** (np.arange(0, 64, 2, dtype=f) / f(64)),
                          f(1) / f(10000.0) ** np.linspace(0, 1, RET_ROPE, dtype=f)])
    log_g = np.log(f(1) - f(2) ** (f(-5) - np.arange(RET_HEADS, dtype=f))).astype(f)
    dist = (k[0][None, :] - np.arange(P)[:, None]).astype(f)
    decay = np.where(dist[:, None] >= 0, np.exp(np.maximum(dist, 0)[:, None] * log_g[None, :, None]), 0)
    c = {"c_ident": np.eye(P), "c_iota": np.arange(TOPK), "c_causal": causal, "c_cmp_mask": cmp_mask,
         "c_inv_freq": inv, "c_decay": decay}
    c = {name: np.ascontiguousarray(a, dtype=f) for name, a in c.items()}
    c["c_lanes"] = np.repeat(np.arange(N_KEYS), GROUP).reshape(N_KEYS, GROUP).astype(mybir.dt.np(BF16))
    return c


def kernel(**inputs):
    import concourse.bacc as _bacc
    from concourse.bass_utils import run_bass_kernel_spmd as _run

    i = {name: np.asarray(a) for name, a in inputs.items()}
    gains = np.stack([i["norm_mix"][0], i["norm_ffn"][0], i["norm_mix"][1], i["norm_ffn"][1],
                      i["mem_norm_g_2"], i["l0_norm_g_2"], i["l1_norm_g_2"]])
    arrays = {
        "x": i["x"][0], "mem": i["mem_2"][0],
        "positions": i["positions_2"].reshape(TT, P).T,
        "gains": gains.reshape(len(NORMS), KT, P).transpose(2, 0, 1),
        "norm_final": i["norm_final"], "final_norm": i["final_norm_g_2"],
        "attn_w_qkv": i["attn_w_qkv"][0], "attn_w_o": i["attn_w_o"][0],
        "na_bias": window_bias(i["attn_rel_bias"][0]),
        "conv_w_in": i["conv_w_in"][0], "conv_w_out": i["conv_w_out"][0],
        "conv_w": i["conv_w_conv"][0].reshape(3, KT, P).transpose(2, 1, 0),
        "peer_w_query": i["peer_w_query"],
        "keysT": i["peer_sub_keys"].reshape(2, HP, N_KEYS, P).transpose(0, 3, 1, 2),
        "w_upT": i["peer_w_up"].reshape(2 * N_KEYS, N_KEYS, KT, P).transpose(0, 3, 2, 1).reshape(2 * N_KEYS, P, KT * N_KEYS),
        "w_down": i["peer_w_down"].reshape(2 * N_KEYS, N_KEYS, D),
        "l0_w_in_2": i["l0_w_in_2"], "l0_w_out_2": i["l0_w_out_2"], "l0_w_mem_kv_2": i["l0_w_mem_kv_2"],
        "l1_w_in_2": i["l1_w_in_2"], "l1_w_out_2": i["l1_w_out_2"], "l1_w_mem_kv_2": i["l1_w_mem_kv_2"],
        "gate_b": i["l0_nsa_gate_b_2"],
        "pe_k": np.concatenate([i["l0_cmp_pe_k_2"].T] * 2), "pe_v": np.concatenate([i["l0_cmp_pe_v_2"].T] * 2),
        "w1_k": i["l0_cmp_w1_k_2"].transpose(1, 0, 2), "w1_v": i["l0_cmp_w1_v_2"].transpose(1, 0, 2),
        "w2_k": i["l0_cmp_w2_k_2"], "w2_v": i["l0_cmp_w2_v_2"],
        **constants(),
    }
    nc = _bacc.Bacc("TRN2", target_bir_lowering=False, num_devices=1)
    d, fed = {}, {}
    for name, a in arrays.items():
        a = np.ascontiguousarray(a)
        fed[f"in_{name}"] = a
        d[name] = nc.dram_tensor(f"in_{name}", a.shape, mybir.dt.from_np(a.dtype), kind="ExternalInput").ap()
    out = nc.dram_tensor("out_rows", (SEQ, D), F32, kind="ExternalOutput").ap()
    if DEBUG:
        d["dbg"] = nc.dram_tensor("dbg", (7, P, TT, D), F32, kind="ExternalOutput").ap()
    build(nc, d, out)
    r = _run(nc, [fed], core_ids=[0])
    return r.results[0]["out_rows"].reshape(1, SEQ, D)
```

```python
import math
from contextlib import ExitStack

import numpy as np

import concourse.bass as bass
from concourse import mybir

F32 = mybir.dt.float32
F32R = mybir.dt.float32r
BF16 = mybir.dt.bfloat16
U32 = mybir.dt.uint32
I32 = mybir.dt.int32
ALU = mybir.AluOpType
ACT = mybir.ActivationFunctionType
AX = mybir.AxisListType.X

P = 128
SEQ, D = 256, 1024
TT = SEQ // P
KT = D // P
CHUNK = 512
NEG = -1e30
LOWEST = -3.0e38
EPS = 1e-6

ROWS, GRID_W, WIN_COLS, MAX_WIN_ROWS = 4, 64, 16, 8
NA_HEADS, HEAD = 16, 64
PEER_HEADS, N_KEYS, TOPK = 8, 128, 16
HP = 2 * PEER_HEADS
HK = PEER_HEADS * TOPK

NSA_HEADS, NSA_GROUPS = 8, 2
CMP_LEN, CMP_STRIDE = 32, 16
N_CMP = (SEQ - CMP_LEN) // CMP_STRIDE + 1
MOBA_HEADS, MEM_HEADS = 8, 4
RET_HEADS, RET_QK, RET_V = 4, 256, 512
ROPE = 32
RET_ROPE = 128
ROPES = ROPE + RET_ROPE

EVEN = {}
_at = 0
for _name, _w in (("nq", 512), ("nkc", 128), ("nvc", 128), ("nks", 128), ("nvs", 128), ("nkw", 128),
                  ("nvw", 128), ("ng", 24), ("nz", 512), ("mq", 512), ("mk", 512), ("mv", 512),
                  ("mz", 512), ("eq", 256), ("ez", 256)):
    EVEN[_name] = _at
    _at += _w
EVEN_W = _at
EVEN_OUT = 1280
ODD = {"rq": 0, "rk": 1024, "rv": 2048, "rz": 4096, "eq": 6144, "ez": 6400}
ODD_W = 6656
ODD_OUT = 2304

NORMS = ("attn", "peer0", "conv", "peer1", "mem", "even", "odd")

ARENA = 32768
L_QT, L_KT, L_V, L_BIAS, L_O, L_OT = 0, 2048, 4096, 6144, 14336, 16384
P_LOW = 16384
P_QT, P_SC, P_KEYS, P_TOP = P_LOW, P_LOW + 4096, P_LOW + 8192, P_LOW + 10240
C_C, C_U, C_Y, C_YT = 2048, 4096, 8192, 10240
E_PROJ, E_T, E_ROPED = 0, 8752, 13872
E_NSA = 19968
M_K, M_V = 23344, 24368
E_W1K, E_W1V, E_APE, E_TMP = 25392, 27440, 29488, 30448
ROPE_AT = 31472
E_YT = E_T
O_PROJ, O_ROPED, O_T = 0, 13312, 17408
O_DECAY = 22016
O_YT = O_ROPED

UNIT = 1024
UKT = 2
RAW, SPLIT = 4, 2
HALF = N_KEYS // 2
GROUP = 8
WIDE, NARROW = 4, 4
CANDS = WIDE * TOPK + (TOPK - WIDE) * NARROW
MEM_SQUARES, MEM_SPLIT = HALF + 16, HALF + 34
STEP_COLUMNS, LOW_EVERY = 110, 1050
LEAD = 8


class Jobs:

    RINGS = {"all": range(8), "projection": range(4), "other": range(4, 8)}

    def __init__(self):
        self.at = {}
        self.bank, self.turn, self.own = [], [], []
        self.filled, self.told = [0] * 8, [0] * 8
        self.next = {ring: 0 for ring in self.RINGS}

    def add(self, name, count=1, own=True, ring="all"):
        for _ in range(count):
            b = self.RINGS[ring][self.next[ring] % len(self.RINGS[ring])]
            self.next[ring] += 1
            self.at.setdefault(name, []).append(len(self.bank))
            self.bank.append(b)
            self.turn.append(self.filled[b])
            self.filled[b] += 1
            self.told[b] += own
            self.own.append(self.told[b] if own else None)

    def of(self, name, k=0):
        return self.at[name][k]


CAUSAL = ("nsa_s", "nsa_w", "moba")


def key_tiles(family, t):
    return t + 1 if family in CAUSAL else TT


def weight_tiles(family):
    return [(kt, t) for kt in range(TT) for t in range(TT) if kt < key_tiles(family, t)]


LAG = {"S": 0, "T": 2, "O": 3}


def attention_order(heads):
    return [(kind, s - lag) for s in range(heads + LAG["O"]) for kind, lag in LAG.items() if 0 <= s - lag < heads]


def head_step(order, s):
    return [k for k, (kind, a) in enumerate(order) if a + LAG[kind] == s]


EVEN_ROPES = (("nq", 0), ("nq", 1), ("nkc", 0), ("nkc", 1), ("nks", 0), ("nks", 1), ("nkw", 0), ("nkw", 1),
              ("mq", 0), ("mq", 1), ("mk", 0), ("mk", 1))
ODD_CHUNKS = (0, 1, 2, 3, 12, 4, 5, 6, 7, 8, 9, 10, 11)
EVEN_PLAN = {
    (0, 3): [("rope", 0)], (1, 0): [("rope", 1)], (1, 2): [("even_T", 0), ("even_T", 1)],
    (1, 3): [("rope", 2), ("rope", 3)], (2, 0): [("rope", 4), ("rope", 5)],
    (2, 1): [("even_T", 2), ("cmp_blocks", 0)], (2, 3): [("rope", 6), ("rope", 7), ("hid", 0), ("gates", 0)],
    (3, 0): [("hid", 1), ("cmp_hidden", 0)], (3, 1): [("even_T", 3), ("even_T", 4)], (3, 2): [("kvc", 0), ("kvc", 1)],
    (3, 3): [("cmp_S", 0), ("cmp_S", 1), ("cmp_softmax", 0)], (4, 1): [("cmp_T", 0)], (4, 2): [("cmp_O", 0), ("cmp_O", 1)],
    (4, 3): [("rope", 8)], (5, 0): [("rope", 9)], (5, 2): [("even_T", 5), ("even_T", 6)],
    (5, 3): [("rope", 10)], (6, 0): [("rope", 11)], (6, 2): [("even_T", 7), ("even_T", 8)],
    (7, 3): [("silu", 0), ("silu", 1)], (8, 3): [("silu", 2), ("even_T", 9)],
}
ODD_PLAN = {
    (0, 3): [("rope", 0)], (1, 1): [("rope", 1)], (1, 2): [("odd_T", 0), ("odd_T", 1)],
    (1, 3): [("rope", 2)], (2, 1): [("rope", 3)], (2, 2): [("odd_T", 2), ("odd_T", 3)],
    (2, 3): [("rope", 4)], (3, 1): [("rope", 5)], (3, 2): [("odd_T", 4), ("odd_T", 5)],
    (3, 3): [("rope", 6)], (4, 1): [("rope", 7)], (4, 2): [("odd_T", 6), ("odd_T", 7)],
    (4, 3): [("silu", 4), ("odd_T", 8)],
    (8, 1): [("ret_S", 0)],
    (9, 3): [("silu", 0), ("ret_S", 1)], (10, 0): [("ret_O", 0)],
    (10, 3): [("silu", 1), ("ret_S", 2)], (11, 0): [("ret_O", 1)],
    (11, 3): [("silu", 2), ("ret_S", 3)], (12, 0): [("ret_O", 2)],
    (12, 3): [("silu", 3), ("ret_O", 3)],
}
CONV_CHUNKS = (2, 4, 0, 3, 5, 1)
EVEN_T_TILES = (0, 1, 7, 8, 9, 2, 3, 4, 5, 6)
EVEN_ROPED = (2, 2, 4, 6, 8, 10, 10, 12, 12, 0)


EVEN_CHUNKS = tuple(range(-(-EVEN_W // CHUNK)))
for _s in range(NSA_HEADS * 2 + MOBA_HEADS + MEM_HEADS + LAG["O"]):
    _c = 4 + _s // 4
    EVEN_PLAN.setdefault((_c, _s % 4) if _c < len(EVEN_CHUNKS) else (len(EVEN_CHUNKS), 0), []).append(("ev", _s))
for _s in range(MEM_HEADS + LAG["O"]):
    ODD_PLAN.setdefault((5 + _s // 4, _s % 4), []).append(("om", _s))


def build(nc, d, out):
    ctx = ExitStack()
    with ctx:
        def sb(name, shape, dt=F32):
            return ctx.enter_context(nc.sbuf_tensor(name, shape, dt))

        sems = {}

        def sem(name):
            if name not in sems:
                sems[name] = ctx.enter_context(nc.semaphore(name))
            return sems[name]

        place_at = [(nc.sbuf_base + 63) // 64 * 64]

        def place(name, shape, dt=F32, at=None):
            size = math.prod(shape[1:]) * (2 if dt == BF16 else 4)
            if at is None:
                at = place_at[0]
                place_at[0] += (size + 63) // 64 * 64
            place_of[name] = at
            return nc.alloc_sbuf_tensor_at(name, list(shape), dt, offset=at)

        place_of = {}
        resid = place("resid", [P, TT, D])
        xh, xl = place("xh", [P, KT, SEQ], F32R), place("xl", [P, KT, SEQ], F32R)
        raw = place("raw", [P, RAW, UNIT])
        wh, wl = place("wh", [P, SPLIT, UNIT], F32R), place("wl", [P, SPLIT, UNIT], F32R)
        arena = place("arena", [P, ARENA])
        aux = place("aux", [P, 5248])
        ident = place("ident", [P, P])
        gains = place("gains", [P, len(NORMS), KT])
        small = place("small", [P, 64])
        iota = place("iota", [P, TOPK])
        convw = place("convw", [P, KT, 3])
        pos_i = place("pos_i", [P, TT], I32)
        gate_b = place("gate_b", [P, 24])
        pe_k = place("pe_k", [P, CMP_LEN])
        pe_v = place("pe_v", [P, CMP_LEN])
        w2k = place("w2k", [P, 2, HEAD])
        w2v = place("w2v", [P, HEAD])
        ret_stats = place("ret_stats", [P, RET_HEADS * TT, 2])
        bn = place("bn", [P, 6])
        assert place_at[0] <= nc.sbuf_usable_end, (place_at[0], nc.sbuf_usable_end)

        def parts(name, words, tiles):
            size = tiles * SEQ
            return [place(f"{name}_{p}", [P, tiles, SEQ], F32R, place_of["arena"] + 4 * (words + k * size))
                    for k, p in enumerate("hl")]

        na_out = parts("na_out", L_OT, KT)
        conv_out = parts("conv_out", C_YT, KT)
        mem_in_T = parts("mem_in", E_T, KT)
        ev_out = parts("ev_out", E_YT, EVEN_OUT // P)
        od_out = parts("od_out", O_YT, ODD_OUT // P)
        x_in = [xh, xl]

        at = place_of["aux"]
        lanes = place("lanes", [P, N_KEYS, GROUP], BF16, at)
        at += 2 * N_KEYS * GROUP
        choice = place("choice", [P, 5, SEQ], BF16, at)
        at += 2 * 5 * SEQ
        second = place("second", [P, 2, N_KEYS, GROUP], BF16, at)
        at += 2 * 2 * N_KEYS * GROUP
        first_eq = place("first_eq", [P, 2, HALF, GROUP], BF16, at)
        at += 2 * 2 * HALF * GROUP
        first = place("first", [P, 2, 3, HALF, GROUP], BF16, at)
        at += 2 * 2 * 3 * HALF * GROUP
        gh, gl = (place(n, [P, SPLIT, SEQ], F32R, at + k * 4 * SPLIT * SEQ) for k, n in enumerate(("gh", "gl")))
        assert at + 8 * SPLIT * SEQ <= place_of["ident"]
        banks = [ctx.enter_context(nc.psum_tensor(f"bank{b}", [P, 512], F32)) for b in range(8)]

        def view(off, *shape):
            n = math.prod(shape)
            names = "abcd"[:len(shape)]
            v = arena[:, off:off + n]
            if len(shape) == 1:
                return v
            return v.rearrange(f"p ({' '.join(names)}) -> p {' '.join(names)}",
                               **{c: s for c, s in zip(names[1:], shape[1:])})

        def aux_view(off, *shape):
            n = math.prod(shape)
            names = "abcd"[:len(shape)]
            v = aux[:, off:off + n]
            if len(shape) == 1:
                return v
            return v.rearrange(f"p ({' '.join(names)}) -> p {' '.join(names)}",
                               **{c: s for c, s in zip(names[1:], shape[1:])})

        J = Jobs()
        units = []
        first_unit, chunk_end = {}, {}

        def weight(name, w, cols, order=None):
            first_unit[name], chunk_end[name] = len(units), []
            for c in order or range(-(-cols // CHUNK)):
                c0 = c * CHUNK
                n = min(CHUNK, cols - c0)
                for k0 in range(0, w.shape[0], UKT * P):
                    units.append((w[k0:k0 + UKT * P, c0:c0 + n].rearrange("(k p) n -> p k n", p=P), UKT, n))
                chunk_end[name].append(len(units))

        def experts(layer):
            first_unit[f"up{layer}"] = len(units)
            units.extend([None] * N_KEYS)
            first_unit[f"down{layer}"] = len(units)
            units.extend([None] * N_KEYS)

        weight("qkv", d["attn_w_qkv"], 3 * D)
        weight("wo", d["attn_w_o"], D)
        weight("query0", d["peer_w_query"][0], 2048)
        experts(0)
        weight("conv_in", d["conv_w_in"], 3 * D, CONV_CHUNKS)
        weight("conv_out", d["conv_w_out"], D)
        weight("query1", d["peer_w_query"][1], 2048)
        experts(1)
        weight("mem0", d["l0_w_mem_kv_2"], 512)
        weight("mem1", d["l1_w_mem_kv_2"], 512)
        weight("even_in", d["l0_w_in_2"], EVEN_W)
        weight("even_out", d["l0_w_out_2"], D)
        weight("odd_in", d["l1_w_in_2"], ODD_W, ODD_CHUNKS)
        weight("odd_out", d["l1_w_out_2"], D)

        NA = attention_order(NA_HEADS)
        SEC = [("nsa_s", NSA_HEADS), ("nsa_w", NSA_HEADS), ("moba", MOBA_HEADS), ("mem_e", MEM_HEADS)]
        J.add("norm_attn", 4); J.add("qkv", 12, own=False); J.add("na", len(NA)); J.add("na_oT", 4); J.add("wo", 4, own=False)
        J.add("norm_peer0", 4); J.add("query0", 8, own=False); J.add("scores0", 8); J.add("idxT0", 2)
        J.add("norm_conv", 4); J.add("conv_in", 12, own=False); J.add("conv_out", 4, own=False)
        J.add("norm_peer1", 4); J.add("query1", 8, own=False); J.add("scores1", 8); J.add("idxT1", 2)
        J.add("norm_mem", 4, ring="projection"); J.add("mem0", 2, own=False); J.add("mem1", 2, own=False)
        EV, OM = attention_order(sum(n for _, n in SEC)), attention_order(MEM_HEADS)

        def add_jobs(name, chunks, plan):
            for c in range(chunks + 1):
                if c < chunks:
                    J.add(name, 2, own=False, ring="projection")
                for u in range(KT // UKT):
                    for kind, k in plan.get((c, u), ()):
                        if kind in ("ev", "om"):
                            J.add(kind, len(head_step({"ev": EV, "om": OM}[kind], k)), ring="other")
                        elif kind == "ret_O":
                            J.add(kind, TT, ring="other")
                        elif kind in ("even_T", "hid", "kvc", "cmp_S", "cmp_T", "cmp_O", "odd_T", "ret_S"):
                            J.add(kind, ring="other")

        J.add("norm_even", 4)
        add_jobs("even_in", len(chunk_end["even_in"]), EVEN_PLAN)
        J.add("even_yT", 5); J.add("even_out", 4, own=False)
        J.add("norm_odd", 4)
        add_jobs("odd_in", len(ODD_CHUNKS), ODD_PLAN)
        J.add("odd_yT", 9); J.add("odd_out", 4, own=False)

        unit_of = {}
        for name, ends in chunk_end.items():
            for k, end in enumerate(ends):
                unit_of[J.of(name, 2 * k)] = unit_of[J.of(name, 2 * k + 1)] = end

        def bank(j):
            return banks[J.bank[j]]

        filled = [sem(f"bank{b}_filled") for b in range(8)]
        read = [sem(f"bank{b}_read") for b in range(8)]

        def wait_filled(eng, j):
            if j in unit_of:
                eng.wait_ge(units_used, unit_of[j])
            else:
                eng.wait_ge(filled[J.bank[j]], J.own[j])

        def wait_read(eng, j):
            eng.wait_ge(read[J.bank[j]], J.turn[j] + 1)

        counts = {}

        def count(name):
            counts[name] = counts.get(name, 0) + 1
            return counts[name]

        const_loaded = sem("const_loaded")
        N_CONST = 12
        norm_loaded = sem("identity_and_gains_loaded")
        x_loaded = sem("x_loaded")
        landed = [sem(f"raw{s}_landed") for s in range(RAW)]
        hi_ready, lo_ready = sem("unit_high_ready"), sem("unit_low_ready")
        units_used = sem("units_used")
        x_whole, x_high, x_low = sem("x_whole"), sem("x_high"), sem("x_low")
        extra_loaded = {n: sem(f"{n}_loaded") for n in ("bias", "keys", "cmpw", "decay", "gain", "mem", "masks", "lanes")}
        residual_ready = sem("residual_ready")
        RES = {n: i + 1 for i, n in enumerate(("wo", "peer0", "conv", "peer1", "between", "even", "odd"))}
        dve_step, act_step = sem("dve_step"), sem("act_step")
        squared, scale_ready = sem("norm_squared"), sem("norm_scale_ready")
        exponent = sem("exponent_set")
        summed, row_scale = sem("norm_summed"), sem("norm_row_scale")
        ret_shifted = sem("ret_variance_shifted")
        ret_var, ret_scale = sem("ret_variance"), sem("ret_scale")
        scores_shifted, weights_ready = sem("scores_shifted"), sem("weights_ready")
        top_ready, top_exp = sem("top_ready"), sem("top_exp")
        eq_ready, onehots = sem("first_keys_compared"), sem("onehots_ready")
        products, weighted = sem("router_products"), sem("experts_weighted")
        gelu_done = sem("gelu_done")
        g_high, g_low = sem("gated_high"), sem("gated_low")
        y_ready = sem("gated_y_ready")
        roped = sem("roped")
        cmp_ready, cmp_exp_in, cmp_exp = sem("cmp_ready"), sem("cmp_exp_in"), sem("cmp_exp")
        tables = sem("rope_tables")
        stored_out = sem("output_stored")
        nsa_gate = sem("nsa_gate")
        silu_done = sem("silu_done")
        ret_ready = sem("ret_scores_ready")
        conv_ready = sem("conv_ready")
        final_ready = sem("final_ready")
        gate_in = sem("gate_in")
        angle_ready = sem("angle_ready")

        def unit_wait(base, i):
            return i * 4 + base

        def split_groups():
            order, n = {}, 0
            for name, groups in (("norm_attn", 4), ("na_oT", 4), ("norm_peer0", 4), ("norm_conv", 4), ("conv", 4),
                                 ("norm_peer1", 4), ("norm_mem", 4), ("norm_even", 4), ("even_yT", 5),
                                 ("norm_odd", 4), ("odd_yT", 9)):
                order[name] = n
                n += groups
            return order

        XG = split_groups()
        s_buf = aux_view(0, 3, TT, SEQ)
        pT_buf = aux_view(1536, 2, 2 * TT, P)
        gain_bc = aux_view(2560, D)
        causal = aux_view(3584, TT, SEQ)
        cmp_mask = aux_view(4096, 2, TT, 16)
        inv_freq = aux_view(4160, ROPES)
        cmp_small = aux_view(4320, 320)
        squares = aux_view(0, 4, 512)
        scale = aux_view(2048, TT, P)
        x_tmp = aux_view(0, 4, 4 * P)
        acts = view(0, N_KEYS, SEQ)

        eT = view(E_T, 20, SEQ)
        EQ, EMQ, EMK, EEQ, EKC, EVC, EKS, EKW = 0, 4, 8, 12, 14, 15, 16, 18
        ev_proj = view(E_PROJ, TT, EVEN_W)
        od_proj = view(O_PROJ, TT, ODD_W)
        mem_kT = view(M_K, 2, 2, SEQ)
        mem_v = view(M_V, 2, TT, 256)
        oT = view(O_T, 18, SEQ)

        def half(t, h, a, b):
            r = (h % 2) * HEAD
            return t[r:r + HEAD, h // 2, a:b]

        ev_heads = []
        for name, n in SEC:
            for h in range(n):
                r, g = (h % 2) * HEAD, h // 4
                if name in ("nsa_s", "nsa_w"):
                    kt = (EKS if name == "nsa_s" else EKW) + g
                    v0 = EVEN["nvs" if name == "nsa_s" else "nvw"] + g * HEAD
                    ev_heads.append((name, h, eT[r:r + HEAD, EQ + h // 2, :], eT[r:r + HEAD, kt, :],
                                     [ev_proj[:, k, v0:v0 + HEAD] for k in range(TT)]))
                elif name == "moba":
                    v0 = EVEN["mv"] + h * HEAD
                    ev_heads.append((name, h, eT[r:r + HEAD, EMQ + h // 2, :],
                                     eT[r:r + HEAD, EMK + h // 2, :],
                                     [ev_proj[:, k, v0:v0 + HEAD] for k in range(TT)]))
                else:
                    ev_heads.append((name, h, eT[r:r + HEAD, EEQ + h // 2, :],
                                     mem_kT[r:r + HEAD, 0, h // 2, :],
                                     [mem_v[:, 0, k, h * HEAD:(h + 1) * HEAD] for k in range(TT)]))
        na_q, na_k = view(L_QT, KT, SEQ), view(L_KT, KT, SEQ)
        na_v, na_o = view(L_V, TT, D), view(L_O, TT, D)
        na_bias = view(L_BIAS, NA_HEADS, TT, SEQ)
        na_heads = [("na", h, half(na_q, h, 0, SEQ), half(na_k, h, 0, SEQ),
                     [na_v[:, k, h * HEAD:(h + 1) * HEAD] for k in range(TT)]) for h in range(NA_HEADS)]
        om_heads = [("mem_o", h, oT[(h % 2) * HEAD:(h % 2) * HEAD + HEAD, 16 + h // 2, :],
                     mem_kT[(h % 2) * HEAD:(h % 2) * HEAD + HEAD, 1, h // 2, :],
                     [mem_v[:, 1, k, h * HEAD:(h + 1) * HEAD] for k in range(TT)]) for h in range(MEM_HEADS)]
        head_base = {"na": 0, "ev": NA_HEADS, "om": NA_HEADS + len(ev_heads)}
        ev_T_src = []
        rp = E_ROPED
        e_nq, e_mq, e_mk = view(rp, TT, 512), view(rp + 1024, TT, 512), view(rp + 2048, TT, 512)
        e_kc = view(rp + 3072, TT, 128)
        e_ks, e_kw = view(rp + 3328, TT, NSA_GROUPS, 2, HEAD), view(rp + 3840, TT, NSA_GROUPS, 2, HEAD)
        for i in range(4):
            ev_T_src.append([e_nq[:, t, i * P:(i + 1) * P] for t in range(TT)])
        for i in range(4):
            ev_T_src.append([e_mq[:, t, i * P:(i + 1) * P] for t in range(TT)])
        for i in range(4):
            ev_T_src.append([e_mk[:, t, i * P:(i + 1) * P] for t in range(TT)])
        for i in range(2):
            ev_T_src.append([ev_proj[:, t, EVEN["eq"] + i * P:EVEN["eq"] + (i + 1) * P] for t in range(TT)])
        ev_T_src.append([e_kc[:, t, :] for t in range(TT)])
        ev_T_src.append([ev_proj[:, t, EVEN["nvc"]:EVEN["nvc"] + P] for t in range(TT)])
        for g in range(NSA_GROUPS):
            ev_T_src.append([e_ks[:, t, g].rearrange("p a b -> p (a b)") for t in range(TT)])
        for g in range(NSA_GROUPS):
            ev_T_src.append([e_kw[:, t, g].rearrange("p a b -> p (a b)") for t in range(TT)])
        ev_y_src = [ev_proj[:, :, EVEN["nz"] + i * P:EVEN["nz"] + (i + 1) * P] for i in range(4)]
        ev_y_src += [ev_proj[:, :, EVEN["mz"] + i * P:EVEN["mz"] + (i + 1) * P] for i in range(4)]
        ev_y_src += [ev_proj[:, :, EVEN["ez"] + i * P:EVEN["ez"] + (i + 1) * P] for i in range(2)]
        o_q, o_k = view(O_ROPED, TT, D), view(O_ROPED + 2048, TT, D)
        od_T_src = [[o_q[:, t, i * P:(i + 1) * P] for t in range(TT)] for i in range(8)]
        od_T_src += [[o_k[:, t, i * P:(i + 1) * P] for t in range(TT)] for i in range(8)]
        od_T_src += [[od_proj[:, t, ODD["eq"] + i * P:ODD["eq"] + (i + 1) * P] for t in range(TT)] for i in range(2)]
        od_y_src = [od_proj[:, :, ODD["rz"] + i * P:ODD["rz"] + (i + 1) * P] for i in range(16)]
        od_y_src += [od_proj[:, :, ODD["ez"] + i * P:ODD["ez"] + (i + 1) * P] for i in range(2)]
        decay = view(O_DECAY, RET_HEADS, SEQ)
        ret_buf = aux_view(3584, 2, 3, P)
        cosT, sinT = view(ROPE_AT, TT, ROPES), view(ROPE_AT + TT * ROPES, TT, ROPES)
        cmp_T = {"k": eT[:, EKC, :], "v": eT[:, EVC, :]}
        w1 = {"k": view(E_W1K, CMP_LEN, HEAD), "v": view(E_W1V, CMP_LEN, HEAD)}
        ape = {"k": view(E_APE, CMP_LEN, N_CMP), "v": view(E_APE + CMP_LEN * N_CMP, CMP_LEN, N_CMP)}
        hid_sb = cmp_small[:, 0:32].rearrange("p (a n) -> p a n", a=2)
        kcT = cmp_small[:, 32:64].rearrange("p (g n) -> p g n", g=2)
        hid_rep = cmp_small[:, 64:192].rearrange("p (i n) -> p i n", i=4)
        cmp_s = view(E_TMP, TT, NSA_HEADS, 32)
        vbd = view(E_APE, NSA_GROUPS, 4, HEAD)
        cmp_pT = view(E_TMP + 512, TT, NSA_GROUPS, P)
        nsa_o = view(E_NSA, TT, 512)

        def top_out(t, i):
            return view(P_TOP, TT, 3, HK)[:, t, i, :]

        NORM_ORDER = ("attn", "peer0", "conv", "peer1", "mem", "even", "odd")
        block = ctx.enter_context(nc.Block())

        @block.sync
        def _(sp):
            for t in range(TT):
                sp.dma_start(resid[:, t, :], d["x"][t * P:(t + 1) * P, :]).then_inc(x_loaded, 16)

            def load(n):
                src, kts, cols = units[n]
                if n >= RAW:
                    sp.wait_ge(lo_ready, n - RAW + 1)
                dst = raw[:, n % RAW, 0:kts * cols].rearrange("p (k n) -> p k n", k=kts)
                sp.dma_start(dst, src).then_inc(landed[n % RAW], 16)

            n = 0
            while n < len(units):
                if units[n] is not None:
                    load(n)
                    n += 1
                    continue
                layer = 0 if n == first_unit["up0"] else 1
                for name in ("w_upT", "w_down"):
                    with sp.Fori(0, N_KEYS // RAW) as i:
                        for k in range(RAW):
                            sp.wait_ge(lo_ready, unit_wait(n + k - RAW + 1, i))
                            src = d[name][bass.ds(i * RAW + (layer * N_KEYS + k), 1)]
                            sp.dma_start(raw[:, (n + k) % RAW, :], src.rearrange("a p n -> p (a n)"))\
                                .then_inc(landed[(n + k) % RAW], 16)
                    n += N_KEYS
            sp.wait_ge(final_ready, 1)
            for t in range(TT):
                sp.dma_start(out[t * P:(t + 1) * P, :], resid[:, t, :]).then_inc(stored_out, 16)
            sp.wait_ge(stored_out, 16 * TT)

        @block.gpsimd
        def _(pool):
            def const(dst, src):
                pool.dma_start(dst, src).then_inc(const_loaded, 16)

            pool.dma_start(ident[:], d["c_ident"]).then_inc(norm_loaded, 16)
            pool.dma_start(gains[:], d["gains"]).then_inc(norm_loaded, 16)

            def row_scales():
                n = count("norm_p")
                pool.wait_ge(squared, 4 * n)
                pool.tensor_tensor(small[:, 4:6], small[:, 0:4:2], small[:, 1:4:2], ALU.add).then_inc(summed, 1)
                pool.wait_ge(summed, 2 * n - 1)
                pool.tensor_scalar(small[:, 4:6], small[:, 4:6], D * EPS, None, ALU.add).then_inc(summed, 1)
                pool.wait_ge(summed, 2 * n)
                pool.tensor_tensor(small[:, 6:8], small[:, 4:6], small[:, 58:60], ALU.pow).then_inc(row_scale, 1)

            pool.memset(small[:, 58:60], -0.5).then_inc(exponent, 1)
            pool.wait_ge(exponent, 1)
            row_scales()
            pool.dma_start(na_bias, d["na_bias"]).then_inc(extra_loaded["bias"], 16)
            const(iota[:], d["c_iota"].partition_broadcast(P))
            const(convw[:], d["conv_w"])
            const(pos_i[:], d["positions"])
            const(gate_b[:], d["gate_b"].partition_broadcast(P))
            const(pe_k[:], d["pe_k"])
            const(pe_v[:], d["pe_v"])
            for dup in range(2):
                const(w2k[dup * HEAD:(dup + 1) * HEAD, 0, :], d["w2_k"])
                const(w2k[dup * HEAD:(dup + 1) * HEAD, 1, :], d["w2_k"])
            const(w2v[0:HEAD, :], d["w2_v"])
            const(w2v[HEAD:P, :], d["w2_v"])

            for layer, done in enumerate(("wo", "conv")):
                row_scales()
                pool.dma_start(view(P_KEYS, HP, N_KEYS), d["keysT"][layer])\
                    .then_inc(extra_loaded["keys"], 16)
                pool.wait_ge(x_low, XG[f"norm_peer{layer}"] + 4)
                pool.dma_start(lanes[:], d["c_lanes"].partition_broadcast(P)).then_inc(extra_loaded["lanes"], 16)
                if layer == 1:
                    pool.wait_ge(units_used, first_unit["down1"] + HALF)
                    for t in range(TT):
                        pool.dma_start(view(0, TT, D)[:, t, :], d["mem"][t * P:(t + 1) * P, :])\
                            .then_inc(extra_loaded["mem"], 16)
                    pool.wait_ge(weighted, 128 * (layer + 1))
                    pool.dma_start(gain_bc, d["norm_final"].partition_broadcast(P)).then_inc(extra_loaded["gain"], 16)
                    row_scales()
                row_scales()
            pool.dma_start(inv_freq, d["c_inv_freq"].partition_broadcast(P)).then_inc(extra_loaded["masks"], 16)
            pool.dma_start(causal, d["c_causal"]).then_inc(extra_loaded["masks"], 16)
            pool.dma_start(cmp_mask, d["c_cmp_mask"]).then_inc(extra_loaded["masks"], 16)
            row_scales()
            for kv in "kv":
                for g in range(NSA_GROUPS):
                    pool.dma_start(w1[kv][g * HEAD:(g + 1) * HEAD], d[f"w1_{kv}"])\
                        .then_inc(extra_loaded["cmpw"], 16)
            row_scales()
            pool.dma_start(decay, d["c_decay"]).then_inc(extra_loaded["decay"], 16)
            pool.dma_start(gain_bc, d["final_norm"].partition_broadcast(P)).then_inc(extra_loaded["gain"], 16)
            for n in range(TT * RET_HEADS):
                pool.wait_ge(ret_var, n + 1)
                pool.tensor_scalar(small[:, 4:5], ret_stats[:, n, 1:2], EPS, None, ALU.add).then_inc(ret_shifted, 1)
                pool.wait_ge(ret_shifted, n + 1)
                pool.tensor_tensor(small[:, 30 + n:31 + n], small[:, 4:5], small[:, 58:59], ALU.pow)\
                    .then_inc(ret_scale, 1)
            row_scales()

        @block.tensor
        def _(pe):
            at = [0]

            def take(name, k):
                j = J.of(name, k)
                assert j == at[0], (name, k, j, at[0])
                at[0] += 1
                if J.turn[j]:
                    pe.wait_ge(read[J.bank[j]], J.turn[j])
                return j

            def done(ins, j):
                ins.then_inc(filled[J.bank[j]], 1)

            unit = [0]

            def split_ready(name, n):
                pe.wait_ge(x_low, XG[name] + n)

            def norm(name, src=resid):
                for g in range(4):
                    j = take(f"norm_{name}", g)
                    t, k0 = g % 2, (g // 2) * 4
                    if g < 2:
                        pe.wait_ge(scale_ready, 2 * NORM_ORDER.index(name) + t + 1)
                    for k in range(4):
                        last = pe.matmul(bank(j)[:, k * P:(k + 1) * P], lhsT=src[:, t, (k0 + k) * P:(k0 + k + 1) * P],
                                         rhs=scale[:, t, :], start=True, stop=True)
                    done(last, j)

            def norm_parts(name):
                return lambda k0: split_ready(f"norm_{name}", 2 if k0 < 4 else 4)

            def project(name, forms, lhs, tiles=KT, k=0, after=lambda u: None, ready=None):
                for form in forms:
                    js = [take(name, k), take(name, k + 1)]
                    k += 2
                    for k0 in range(0, tiles, UKT):
                        n = unit[0]
                        cols = units[n][2]
                        if ready:
                            ready(k0)
                        w = [t[:, n % SPLIT, 0:UKT * cols].rearrange("p (k n) -> p k n", k=UKT) for t in (wh, wl)]
                        for part in range(2):
                            pe.wait_ge((hi_ready, lo_ready)[part], n + 1)
                            for kk in range(UKT):
                                kt = k0 + kk
                                for xp in range(2 - part):
                                    x = lhs[xp]
                                    flags = {"start": kt == 0 and part == 0 and xp == 0,
                                             "stop": kt == tiles - 1 and part == 1, "skip_group_check": True}
                                    for b in range(2):
                                        if form == "N":
                                            last = pe.matmul(bank(js[b])[:, 0:cols], lhsT=x[:, kt, b * P:(b + 1) * P],
                                                             rhs=w[part][:, kk, :], **flags)
                                        elif form == "T" or b == 0:
                                            for m in range(2):
                                                c0 = (2 * b + m) * P
                                                f = dict(flags, start=flags["start"] and m == 0)
                                                last = pe.matmul(bank(js[b])[:, m * SEQ:(m + 1) * SEQ],
                                                                 lhsT=w[part][:, kk, c0:c0 + P], rhs=x[:, kt, :], **f)
                                        else:
                                            for m in range(2):
                                                f = dict(flags, start=flags["start"] and m == 0)
                                                last = pe.matmul(bank(js[b])[:, m * 256:(m + 1) * 256],
                                                                 lhsT=x[:, kt, m * P:(m + 1) * P],
                                                                 rhs=w[part][:, kk, 256:512], **f)
                        last.then_inc(units_used, 1)
                        unit[0] += 1
                        after(k0 // UKT)

            def transposes(name, groups, ready):
                for k, group in enumerate(groups):
                    j = take(name, k)
                    ready(k)
                    for q, src in enumerate(group):
                        last = pe.transpose(bank(j)[:, q * P:(q + 1) * P], src, ident[:])
                    done(last, j)

            def attention(name, order, heads, base, some=None):
                for k in range(len(order)) if some is None else some:
                    kind, a = order[k]
                    j = take(name, k)
                    family, _, qT, kT, v = heads[a]
                    if kind == "S":
                        for t in range(TT):
                            keys = key_tiles(family, t) * P
                            last = pe.matmul(bank(j)[:, t * SEQ:t * SEQ + keys], lhsT=qT[:, t * P:(t + 1) * P],
                                             rhs=kT[:, 0:keys], start=True, stop=True)
                    elif kind == "T":
                        pe.wait_ge(weights_ready, base + a + 1)
                        for q, (kt, t) in enumerate(weight_tiles(family)):
                            last = pe.transpose(bank(j)[:, q * P:(q + 1) * P],
                                                s_buf[:, (base + a) % 3, t, kt * P:(kt + 1) * P], ident[:])
                    else:
                        wait_read(pe, J.of(name, order.index(("T", a))))
                        for t in range(TT):
                            n = key_tiles(family, t)
                            for kt in range(n):
                                last = pe.matmul(bank(j)[:, t * HEAD:(t + 1) * HEAD],
                                                 lhsT=pT_buf[:, (base + a) % 2, weight_tiles(family).index((kt, t)), :],
                                                 rhs=v[kt], start=(kt == 0), stop=(kt == n - 1))
                    done(last, j)

            def peer(layer):
                project(f"query{layer}", "TTTT", x_in, ready=norm_parts(f"peer{layer}"))
                qT = view(P_QT, HP, SEQ)
                keys = view(P_KEYS, HP, N_KEYS)
                pe.wait_ge(extra_loaded["keys"], 16 * (layer + 1))
                for k in range(8):
                    t, q = k // 4, k % 4
                    j = take(f"scores{layer}", k)
                    for i in range(2):
                        wait_read(pe, J.of(f"query{layer}", 2 * q + i))
                    for i in range(4):
                        last = pe.matmul(bank(j)[:, i * P:(i + 1) * P], lhsT=qT[:, 4 * q + i, t * P:(t + 1) * P],
                                         rhs=keys[:, 4 * q + i, :], start=True, stop=True)
                    done(last, j)
                u0, d0 = first_unit[f"up{layer}"], first_unit[f"down{layer}"]
                for j in range(at[0] - 8, at[0]):
                    wait_read(pe, j)
                g0, q0 = 64 * layer, 128 * layer

                def up(t, i=0):
                    n, b = u0 + t, t % 2
                    w = [x[:, n % SPLIT, :].rearrange("p (k e) -> p k e", k=KT) for x in (wh, wl)]
                    if t >= 2 or not isinstance(i, int):
                        pe.wait_ge(gelu_done, unit_wait(N_KEYS * layer + t - 1, i))
                    for part in range(2):
                        pe.wait_ge((hi_ready, lo_ready)[part], unit_wait(n + 1, i))
                        for k in range(KT):
                            for xp in range(2 - part):
                                last = pe.matmul(banks[b][:, 0:SEQ], lhsT=w[part][:, k, :], rhs=x_in[xp][:, k, :],
                                                 start=(k == 0 and part == 0 and xp == 0), stop=(k == KT - 1 and part == 1))
                    last.then_inc(units_used, 1)

                def down(t, i=0, start=False, stop=False):
                    n = d0 + t
                    g = [x[:, t % SPLIT, :] for x in (gh, gl)]
                    for part in range(2):
                        pe.wait_ge((hi_ready, lo_ready)[part], unit_wait(n + 1, i))
                        w = (wh, wl)[part][:, n % SPLIT, :]
                        for gp in range(2 - part):
                            if part == 0:
                                pe.wait_ge((g_high, g_low)[gp], unit_wait(N_KEYS * layer + t + 1, i))
                            for m in range(TT):
                                for h in range(2):
                                    last = pe.matmul(banks[4 + 2 * m + h][:, :], lhsT=g[gp][:, m * P:(m + 1) * P],
                                                     rhs=w[:, h * 512:(h + 1) * 512],
                                                     start=start and part == 0 and gp == 0, stop=stop and part == 1)
                    last.then_inc(units_used, 1)

                def router(half, q, i=0):
                    s, c0 = q // 2 % 2, q % 2 * 4
                    pe.wait_ge(onehots, i * 2 + (g0 + 32 * half + q // 2 + 1))
                    if half or q >= 2 or not isinstance(i, int):
                        pe.wait_ge(weighted, unit_wait(q0 + 64 * half + q - 1, i))
                    for c in range(4):
                        for p in range(3):
                            last = pe.matmul(banks[2 + q % 2][:, c * HALF:(c + 1) * HALF],
                                             lhsT=second[:, s, :, c0 + c], rhs=first[:, s, p, :, c0 + c],
                                             start=(p == 0), stop=(p == 2))
                    last.then_inc(products, 1)

                for t in range(2):
                    up(t)
                with pe.Fori(0, (HALF - 4) // 4) as i:
                    for t in range(2, 6):
                        up(t, i)
                for t in range(HALF - 2, HALF + LEAD - 2):
                    up(t)
                for t in range(TT):
                    j = take(f"idxT{layer}", t)
                    if t == 0:
                        pe.wait_ge(gelu_done, N_KEYS * layer + HALF + LEAD - 2)
                    pe.wait_ge(top_ready, 4 * layer + 2 + t + 1)
                    for i in range(3):
                        last = pe.transpose(bank(j)[:, i * P:(i + 1) * P], top_out(t, i), ident[:])
                    done(last, j)
                for t in range(TT):
                    wait_read(pe, J.of(f"idxT{layer}", t))
                for t in range(HALF + LEAD - 2, HALF + LEAD):
                    up(t)
                for k in range(4):
                    up(HALF + LEAD + k)
                    router(0, k)
                with pe.Fori(1, (HALF - LEAD) // 4) as i:
                    for k in range(4):
                        up(HALF + LEAD + k, i)
                        router(0, k, i)
                for q in range(HALF - LEAD, HALF):
                    router(0, q)
                for k in range(4):
                    down(k, start=(k == 0))
                    router(1, k)
                with pe.Fori(1, HALF // 4) as i:
                    for k in range(4):
                        down(k, i)
                        router(1, k, i)
                if layer == 1:
                    with pe.Fori(HALF // 4, 3 * HALF // 8) as i:
                        for k in range(4):
                            down(k, i)
                    norm("mem", view(0, TT, D))
                with pe.Fori((3 * HALF // 8) if layer else HALF // 4, N_KEYS // 4 - 1) as i:
                    for k in range(4):
                        down(k, i)
                for t in range(N_KEYS - 4, N_KEYS):
                    down(t, stop=(t == N_KEYS - 1))
                unit[0] += 2 * N_KEYS

            def even_steps(c, u):
                for kind, k in EVEN_PLAN.get((c, u), ()):
                    if kind == "even_T":
                        g = EVEN_T_TILES[k]
                        if EVEN_ROPED[k]:
                            pe.wait_ge(roped, EVEN_ROPED[k])
                        for chunk in {7: (1,), 6: (7, 8)}.get(g, ()):
                            for t in range(TT):
                                wait_read(pe, J.of("even_in", 2 * chunk + t))
                        j = take("even_T", k)
                        for q, src in enumerate(ev_T_src[i][t] for i in (2 * g, 2 * g + 1) for t in range(TT)):
                            last = pe.transpose(bank(j)[:, q * P:(q + 1) * P], src, ident[:])
                        done(last, j)
                    elif kind == "hid":
                        j, r = take("hid", k), k * HEAD
                        if k == 0:
                            pe.wait_ge(extra_loaded["cmpw"], 64)
                            pe.wait_ge(cmp_ready, 1)
                        for i, kv in enumerate("kv"):
                            for l in range(CMP_LEN):
                                last = pe.matmul(bank(j)[r:r + HEAD, i * 16:i * 16 + N_CMP],
                                                 lhsT=w1[kv][r:r + HEAD, l, :], rhs=ape[kv][r:r + HEAD, l, :],
                                                 start=(l == 0), stop=(l == CMP_LEN - 1))
                        done(last, j)
                    elif kind == "kvc":
                        j, r = take("kvc", k), k * HEAD
                        pe.wait_ge(cmp_ready, 2)
                        pe.matmul(bank(j)[:, 0:N_CMP], lhsT=w2k[r:r + HEAD].rearrange("p a b -> p (a b)"),
                                  rhs=hid_sb[r:r + HEAD, 0, 0:N_CMP], start=True, stop=True)
                        last = pe.matmul(bank(j)[:, 64:64 + HEAD], lhsT=hid_rep[r:r + HEAD].rearrange("p a b -> p (a b)"),
                                         rhs=w2v[r:r + HEAD, :], start=True, stop=True)
                        done(last, j)
                    elif kind == "cmp_S":
                        j = take("cmp_S", k)
                        for g in range(2):
                            wait_read(pe, J.of("kvc", g))
                            wait_read(pe, J.of("even_T", g))
                        for hh in range(4):
                            h = 2 * hh + k
                            for t in range(TT):
                                c0 = (hh * TT + t) * 16
                                last = pe.matmul(bank(j)[:, c0:c0 + N_CMP],
                                                 lhsT=eT[k * HEAD:k * HEAD + HEAD, EQ + hh, t * P:(t + 1) * P],
                                                 rhs=kcT[k * HEAD:k * HEAD + HEAD, h // 4, 0:N_CMP], start=True, stop=True)
                        done(last, j)
                    elif kind == "cmp_T":
                        j = take("cmp_T", 0)
                        pe.wait_ge(cmp_ready, 3)
                        for t in range(TT):
                            for g in range(NSA_GROUPS):
                                q = t * 2 + g
                                last = pe.transpose(bank(j)[:, q * P:(q + 1) * P],
                                                    cmp_s[:, t, 4 * g:4 * g + 4, :].rearrange("p a b -> p (a b)"), ident[:])
                        done(last, j)
                    elif kind == "cmp_O":
                        j = take("cmp_O", k)
                        wait_read(pe, J.of("cmp_T"))
                        for g in range(NSA_GROUPS):
                            last = pe.matmul(bank(j)[:, g * 256:(g + 1) * 256], lhsT=cmp_pT[:, k, g, :],
                                             rhs=vbd[:, g].rearrange("p a b -> p (a b)"), start=True, stop=True)
                        done(last, j)
                    elif kind == "ev":
                        for g in {0: (0, 1, 3), 8: (4,), 16: (5, 6, 7, 8), 24: (9,)}.get(k, ()):
                            wait_read(pe, J.of("even_T", g))
                        if k == 16 + LAG["O"]:
                            for j in (12, 13):
                                wait_read(pe, J.of("even_in", j))
                        attention("ev", EV, ev_heads, head_base["ev"], head_step(EV, k))

            def odd_steps(c, u):
                for kind, k in ODD_PLAN.get((c, u), ()):
                    if kind == "odd_T":
                        if k < 8:
                            pe.wait_ge(roped, len(EVEN_ROPES) + k // 2 * 2 + 2)
                        else:
                            for t in range(TT):
                                wait_read(pe, J.of("odd_in", 8 + t))
                        j = take("odd_T", k)
                        for q, src in enumerate(od_T_src[i][t] for i in (2 * k, 2 * k + 1) for t in range(TT)):
                            last = pe.transpose(bank(j)[:, q * P:(q + 1) * P], src, ident[:])
                        done(last, j)
                    elif kind == "ret_S":
                        j = take("ret_S", k)
                        wait_read(pe, J.of("odd_T", k))
                        wait_read(pe, J.of("odd_T", 4 + k))
                        for kt, q0, q1, c0 in ((0, 0, SEQ, 0), (1, P, SEQ, SEQ)):
                            for dd in range(2):
                                last = pe.matmul(bank(j)[:, c0:c0 + q1 - q0], lhsT=oT[:, 8 + 2 * k + dd, kt * P:(kt + 1) * P],
                                                 rhs=oT[:, 2 * k + dd, q0:q1], start=(dd == 0), stop=(dd == 1))
                        done(last, j)
                    elif kind == "ret_O":
                        pe.wait_ge(ret_ready, k + 1)
                        for t in range(TT):
                            wait_read(pe, J.of("odd_in", 2 * (5 + k) + t))
                        for t in range(TT):
                            j = take("ret_O", TT * k + t)
                            for kt in range(t + 1):
                                last = pe.matmul(bank(j)[:, :], lhsT=ret_buf[:, k % 2, t if kt == 0 else 2, :],
                                                 rhs=od_proj[:, kt, ODD["rv"] + k * RET_V:ODD["rv"] + (k + 1) * RET_V],
                                                 start=(kt == 0), stop=(kt == t))
                            done(last, j)
                    elif kind == "om":
                        if k == 0:
                            wait_read(pe, J.of("odd_T", 8))
                        attention("om", OM, om_heads, head_base["om"], head_step(OM, k))

            norm("attn")
            project("qkv", "TTTTNN", x_in, ready=norm_parts("attn"))
            pe.wait_ge(const_loaded, 16 * N_CONST)
            pe.wait_ge(norm_loaded, 16 * 2)
            for k in range(12):
                wait_read(pe, J.of("qkv", k))
            attention("na", NA, na_heads, head_base["na"])
            for a in range(NA_HEADS):
                wait_read(pe, J.of("na", NA.index(("O", a))))
            transposes("na_oT", [[na_o[:, t, i * P:(i + 1) * P] for i in (2 * g, 2 * g + 1) for t in range(TT)]
                                 for g in range(4)], lambda k: None)
            project("wo", "NN", na_out, ready=lambda k0: split_ready("na_oT", k0 // 2 + 1))
            norm("peer0")
            peer(0)
            norm("conv")
            project("conv_in", "TTTTTT", x_in, ready=norm_parts("conv"))
            project("conv_out", "NN", conv_out, ready=lambda k0: split_ready("conv", k0 // 2 + 1))
            norm("peer1")
            peer(1)
            project("mem0", "M", mem_in_T, ready=norm_parts("mem"))
            project("mem1", "M", mem_in_T)
            norm("even")
            for c in range(len(EVEN_CHUNKS) + 1):
                if c < len(EVEN_CHUNKS):
                    project("even_in", "N", x_in, k=2 * c, after=lambda u: even_steps(c, u), ready=norm_parts("even"))
                else:
                    even_steps(c, 0)
            pe.wait_ge(y_ready, 1)
            transposes("even_yT", [[ev_y_src[i][:, t, :] for i in (2 * g, 2 * g + 1) for t in range(TT)] for g in range(5)],
                       lambda k: None)
            project("even_out", "NN", ev_out, EVEN_OUT // P, ready=lambda k0: split_ready("even_yT", k0 // 2 + 1))
            norm("odd")
            for c in range(len(ODD_CHUNKS)):
                project("odd_in", "N", x_in, k=2 * c, after=lambda u: odd_steps(c, u), ready=norm_parts("odd"))
            pe.wait_ge(y_ready, 2)
            transposes("odd_yT", [[od_y_src[i][:, t, :] for i in (2 * g, 2 * g + 1) for t in range(TT)] for g in range(9)],
                       lambda k: None)
            project("odd_out", "NN", od_out, ODD_OUT // P, ready=lambda k0: split_ready("odd_yT", k0 // 2 + 1))
            assert at[0] == len(J.bank)

        @block.scalar
        def _(act):
            def step(ins):
                ins.then_inc(act_step, 1)
                act.wait_ge(act_step, count("act"))

            def evac(dst, j, src=None, func=ACT.Copy, scale=1.0):
                wait_filled(act, j)
                act.activation(dst, bank(j)[:, :] if src is None else src, func, scale=scale).then_inc(read[J.bank[j]], 1)
                wait_read(act, j)

            issued = [0]

            def high(n, i=0):
                kts, cols = (1, UNIT) if units[n] is None else units[n][1:]
                act.wait_ge(landed[n % RAW], i * 16 + 16 * (n // RAW + 1))
                if n >= SPLIT:
                    act.wait_ge(units_used, unit_wait(n - SPLIT + 1, i))
                act.activation(wh[:, n % SPLIT, 0:kts * cols], raw[:, n % RAW, 0:kts * cols], ACT.Copy)\
                    .then_inc(hi_ready, 1)

            def highs(end, ahead=SPLIT):
                while issued[0] < min(end + ahead, len(units)):
                    high(issued[0])
                    issued[0] += 1

            def split_x(name, dst, groups=4, whole=None):
                for g in range(groups):
                    n = XG[name] + g
                    if whole is None:
                        j = J.of(name, g)
                        wait_filled(act, j)
                        act.activation(dst[0][:, 2 * g:2 * g + 2, :].rearrange("p a b -> p (a b)"), bank(j)[:, :],
                                       ACT.Copy).then_inc(x_high, 1)
                    else:
                        act.wait_ge(x_whole, whole(g)[0])
                        act.activation(whole(g)[1], whole(g)[2], ACT.Copy).then_inc(x_high, 1)

            def norm_split(name, dst=x_in):
                t0 = NORM_ORDER.index(name) * 4

                def whole(g):
                    t, k0 = g % 2, (g // 2) * 4
                    return (t0 + g + 1, dst[0][:, k0:k0 + 4, t * P:(t + 1) * P],
                            x_tmp[:, g].rearrange("p (k q) -> p k q", k=4))

                split_x(f"norm_{name}", dst, whole=whole)

            def norm(src, ready, then=None):
                for p in range(4):
                    ready(p + 1)
                    c, t = p // 2, p % 2
                    act.activation(squares[:, p], src[:, t, c * 512:(c + 1) * 512], ACT.Square,
                                   accum_out=small[:, 2 * t + c:2 * t + c + 1]).then_inc(squared, 1)
                if then:
                    highs(first_unit[then])

            def attention(name, order, heads, base, some=None):
                for kind, a in order if some is None else [order[k] for k in some]:
                    n, family = base + a, heads[a][0]
                    if kind == "S":
                        act.wait_ge(scores_shifted, n + 1)
                        for t in range(TT):
                            row = s_buf[:, n % 3, t, 0:key_tiles(family, t) * P]
                            ins = act.activation(row, row, ACT.Exp,
                                                 bias=small[:, 8 + (n % 4) * 2 + t:9 + (n % 4) * 2 + t],
                                                 accum_out=small[:, 16 + (n % 4) * 2 + t:17 + (n % 4) * 2 + t])
                            if t == 0:
                                step(ins)
                        ins.then_inc(weights_ready, 1)
                        act.wait_ge(weights_ready, n + 1)
                    elif kind == "T":
                        j, w = J.of(name, order.index(("T", a))), len(weight_tiles(family)) * P
                        evac(pT_buf[:, n % 2].rearrange("p a b -> p (a b)")[:, 0:w], j, bank(j)[:, 0:w])

            def peer(layer):
                norm_split(f"peer{layer}")
                qT = view(P_QT, HP, SEQ)
                for k in range(8):
                    highs(unit_of[J.of(f"query{layer}", k)])
                    evac(qT[:, 2 * k:2 * k + 2, :].rearrange("p a b -> p (a b)"), J.of(f"query{layer}", k))
                sc = view(P_SC, TT, HP, N_KEYS)
                for k in range(8):
                    t, q = k // 4, k % 4
                    evac(sc[:, t, 4 * q:4 * q + 4, :].rearrange("p a b -> p (a b)"), J.of(f"scores{layer}", k))
                u0, d0 = first_unit[f"up{layer}"], first_unit[f"down{layer}"]
                assert issued[0] == u0 + SPLIT

                def gelu(t, i=0):
                    act.wait_ge(units_used, unit_wait(u0 + t + 1, i))
                    dst = acts[:, bass.ds(i * 4 + t, 1), :].rearrange("p a b -> p (a b)")
                    act.activation(dst, banks[t % 2][:, 0:SEQ], ACT.Gelu).then_inc(gelu_done, 1)

                def tiles(t0, t1):
                    with act.Fori(0, (t1 - t0) // 4) as i:
                        for k in range(4):
                            gelu(t0 + k, i)
                            high(u0 + t0 + k + SPLIT, i)

                tiles(0, HALF + LEAD - 4)
                for t in range(TT):
                    act.wait_ge(top_ready, 4 * layer + t + 1)
                    g = top_out(t, 2)
                    act.activation(g, g, ACT.Exp).then_inc(top_exp, 1)
                tiles(HALF + LEAD - 4, N_KEYS)

                def gated_high(t, i=0):
                    if t >= SPLIT or not isinstance(i, int):
                        act.wait_ge(units_used, unit_wait(d0 + t - SPLIT + 1, i))
                    src = acts[:, bass.ds(i * 4 + t, 1), :].rearrange("p a b -> p (a b)")
                    act.activation(gh[:, t % SPLIT, :], src, ACT.Copy).then_inc(g_high, 1)

                act.wait_ge(weighted, 128 * layer + 64)
                for t in range(SPLIT):
                    gated_high(t)
                with act.Fori(0, HALF // 4 - 1) as i:
                    for k in range(2, 6):
                        high(d0 + k, i)
                        gated_high(k, i)
                for t in range(HALF - 2, HALF):
                    high(d0 + t)
                    gated_high(t)
                act.wait_ge(weighted, 128 * layer + 128)

                def gated_tiles(t0, t1):
                    with act.Fori(0, (t1 - t0) // 4) as i:
                        for k in range(t0, t0 + 4):
                            high(d0 + k, i)
                            gated_high(k, i)
                    for t in range(t1 - (t1 - t0) % 4, t1):
                        high(d0 + t)
                        gated_high(t)

                if layer == 0:
                    gated_tiles(HALF, N_KEYS)
                else:
                    gated_tiles(HALF, MEM_SQUARES)
                    norm(view(0, TT, D), lambda p: act.wait_ge(extra_loaded["mem"], 16 * TT))
                    gated_tiles(MEM_SQUARES, MEM_SPLIT)
                    norm_split("mem", mem_in_T)
                    gated_tiles(MEM_SPLIT, N_KEYS)
                issued[0] = d0 + N_KEYS
                if layer == 1:
                    highs(first_unit["mem0"])

            def even_steps(c, u):
                for kind, k in EVEN_PLAN.get((c, u), ()):
                    if kind == "even_T" and k != 2:
                        g = EVEN_T_TILES[k]
                        evac(eT[:, 2 * g:2 * g + 2, :].rearrange("p a b -> p (a b)"), J.of("even_T", k))
                    elif kind == "hid":
                        r, j = k * HEAD, J.of("hid", k)
                        evac(hid_sb[r:r + HEAD, :, 0:N_CMP], j,
                             bank(j)[r:r + HEAD, 0:32].rearrange("p (a n) -> p a n", a=2)[:, :, 0:N_CMP], ACT.Silu)
                    elif kind == "gates":
                        act.wait_ge(gate_in, 1)
                        gates = ev_proj[:, :, EVEN["ng"]:EVEN["ng"] + 24]
                        act.activation(gates, gates, ACT.Sigmoid).then_inc(nsa_gate, 1)
                    elif kind == "cmp_softmax":
                        act.wait_ge(cmp_exp_in, 1)
                        cs = cmp_s.rearrange("p t h n -> p (t h) n")[:, :, 0:N_CMP]
                        act.activation(cs, cs, ACT.Exp).then_inc(cmp_exp, 1)
                    elif kind == "cmp_T":
                        evac(cmp_pT.rearrange("p t g q -> p (t g q)"), J.of("cmp_T"))
                    elif kind == "silu":
                        name, w = (("nz", 512), ("mz", 512), ("ez", 256))[k]
                        z = ev_proj[:, :, EVEN[name]:EVEN[name] + w]
                        act.activation(z, z, ACT.Silu).then_inc(silu_done, 1)
                    elif kind == "ev":
                        attention("ev", EV, ev_heads, head_base["ev"], head_step(EV, k))

            def odd_steps(c, u):
                for kind, k in ODD_PLAN.get((c, u), ()):
                    if kind == "odd_T":
                        evac(oT[:, 2 * k:2 * k + 2, :].rearrange("p a b -> p (a b)"), J.of("odd_T", k))
                    elif kind == "silu":
                        z = od_proj[:, :, ODD["rz"] + k * RET_V:ODD["rz"] + (k + 1) * RET_V] if k < RET_HEADS \
                            else od_proj[:, :, ODD["ez"]:ODD["ez"] + 256]
                        act.activation(z, z, ACT.Silu).then_inc(silu_done, 1)
                    elif kind == "om":
                        attention("om", OM, om_heads, head_base["om"], head_step(OM, k))

            def updated(name):
                return lambda p: act.wait_ge(residual_ready, 4 * (RES[name] - 1) + p)

            norm(resid, lambda p: act.wait_ge(x_loaded, 16 * TT), "qkv")
            norm_split("attn")
            for k in range(4):
                highs(unit_of[J.of("qkv", k)])
                evac(na_q[:, 2 * k:2 * k + 2, :].rearrange("p a b -> p (a b)"), J.of("qkv", k), scale=HEAD ** -0.5)
            for k in range(8, 12):
                c, t = (k - 8) // 2, k % 2
                highs(unit_of[J.of("qkv", k)])
                evac(na_v[:, t, c * CHUNK:(c + 1) * CHUNK], J.of("qkv", k))
            attention("na", NA, na_heads, head_base["na"])
            split_x("na_oT", na_out)
            highs(unit_of[J.of("wo", 3)], 0)
            norm(resid, updated("wo"), "query0")
            peer(0)
            norm(resid, updated("peer0"), "conv_in")
            norm_split("conv")
            cT = view(C_C, KT, SEQ)
            for h in range(2):
                for k in range(2):
                    j, i = J.of("conv_in", 6 * h + k), 4 * h + 2 * k
                    highs(unit_of[j])
                    evac(cT[:, i:i + 2, :].rearrange("p a b -> p (a b)"), j)
                highs(unit_of[J.of("conv_in", 6 * h + 4)])
                for g in range(2 * h, 2 * h + 2):
                    act.wait_ge(conv_ready, g + 1)
                    act.activation(conv_out[0][:, 2 * g:2 * g + 2], view(C_Y, KT, SEQ)[:, 2 * g:2 * g + 2], ACT.Copy)\
                        .then_inc(x_high, 1)
            highs(unit_of[J.of("conv_out", 3)], 0)
            norm(resid, updated("conv"), "query1")
            peer(1)
            norm(resid, updated("peer1"))
            highs(first_unit["mem1"], 0)
            norm(resid, updated("between"))
            for l in range(2):
                highs(unit_of[J.of(f"mem{l}", 0)], 0)
                evac(mem_kT[:, l].rearrange("p a b -> p (a b)"), J.of(f"mem{l}", 0))
                evac(mem_v[:, l].rearrange("p a b -> p (a b)"), J.of(f"mem{l}", 1))
            highs(first_unit["even_in"])
            norm_split("even")
            act.wait_ge(angle_ready, 1)
            act.activation(view(ROPE_AT, 2 * TT * ROPES), view(ROPE_AT, 2 * TT * ROPES), ACT.Sin).then_inc(tables, 1)
            act.wait_ge(tables, 1)
            for c in range(len(EVEN_CHUNKS) + 1):
                for u in range(KT // UKT):
                    if c < len(EVEN_CHUNKS):
                        highs(first_unit["even_in"] + KT // UKT * c + u + 1)
                        if u == KT // UKT - 1:
                            n = min(CHUNK, EVEN_W - c * CHUNK)
                            for t in range(TT):
                                j = J.of("even_in", 2 * c + t)
                                evac(ev_proj[:, t, c * CHUNK:c * CHUNK + n], j, bank(j)[:, 0:n])
                    even_steps(c, u)
            split_x("even_yT", ev_out, groups=5)
            highs(unit_of[J.of("even_out", 3)], 0)
            norm(resid, updated("even"), "odd_in")
            norm_split("odd")
            for c, cols in enumerate(ODD_CHUNKS):
                for u in range(KT // UKT):
                    highs(first_unit["odd_in"] + KT // UKT * c + u + 1)
                    if u == KT // UKT - 1:
                        for t in range(TT):
                            evac(od_proj[:, t, cols * CHUNK:(cols + 1) * CHUNK], J.of("odd_in", 2 * c + t))
                    odd_steps(c, u)
            split_x("odd_yT", od_out, groups=9)
            highs(unit_of[J.of("odd_out", 3)])
            norm(resid, updated("odd"))

        @block.vector
        def _(dve):
            def step(ins):
                ins.then_inc(dve_step, 1)
                dve.wait_ge(dve_step, count("dve"))

            def tell(ins, s, n):
                ins.then_inc(s, 1)
                dve.wait_ge(s, n)

            def read_out(ins, j):
                ins.then_inc(read[J.bank[j]], 1)
                wait_read(dve, j)

            tt, ts, stt = dve.tensor_tensor, dve.tensor_scalar, dve.scalar_tensor_tensor
            issued = [0]

            def low(n, i=0):
                kts, cols = (1, UNIT) if units[n] is None else units[n][1:]
                dve.wait_ge(hi_ready, unit_wait(n + 1, i))
                tt(wl[:, n % SPLIT, 0:kts * cols], raw[:, n % RAW, 0:kts * cols],
                   wh[:, n % SPLIT, 0:kts * cols].bitcast(F32), ALU.subtract).then_inc(lo_ready, 1)

            def lows(end, ahead=SPLIT):
                while issued[0] < min(end + ahead, len(units)):
                    low(issued[0])
                    issued[0] += 1

            def split_low(name, dst, groups):
                for g in range(groups):
                    n, j = XG[name] + g, J.of(name, g)
                    dve.wait_ge(x_high, n + 1)
                    hi = dst[0][:, 2 * g:2 * g + 2, :].rearrange("p a b -> p (a b)")
                    lo = dst[1][:, 2 * g:2 * g + 2, :].rearrange("p a b -> p (a b)")
                    tell(tt(lo, bank(j)[:, :], hi.bitcast(F32), ALU.subtract), x_low, n + 1)
                    read_out(dve.nop(), j)

            def row_scales():
                dve.wait_ge(row_scale, count("norm_v"))

            def norm_scale(name):
                row_scales()
                for t in range(TT):
                    tell(ts(scale[:, t, :], ident[:], small[:, 6 + t:7 + t], math.sqrt(D), ALU.mult, ALU.mult),
                         scale_ready, 2 * NORM_ORDER.index(name) + t + 1)

            def norm_parts(name, then=None, dst=x_in):
                i, w0, x0 = NORMS.index(name), 4 * NORM_ORDER.index(name), XG[f"norm_{name}"]

                def whole(g):
                    j = J.of(f"norm_{name}", g)
                    k0 = (g // 2) * 4
                    wait_filled(dve, j)
                    gain = gains[:, i, k0:k0 + 4].unsqueeze(2).to_broadcast([P, 4, P])
                    tell(tt(x_tmp[:, g].rearrange("p (k q) -> p k q", k=4),
                            bank(j)[:, :].rearrange("p (k q) -> p k q", k=4), gain, ALU.mult), x_whole, w0 + g + 1)
                    read_out(dve.nop(), j)

                def lower(g):
                    t, k0 = g % 2, (g // 2) * 4
                    dve.wait_ge(x_high, x0 + g + 1)
                    tell(tt(dst[1][:, k0:k0 + 4, t * P:(t + 1) * P], x_tmp[:, g].rearrange("p (k q) -> p k q", k=4),
                            dst[0][:, k0:k0 + 4, t * P:(t + 1) * P].bitcast(F32), ALU.subtract), x_low, x0 + g + 1)

                whole(0)
                whole(1)
                lower(0)
                whole(2)
                lower(1)
                if then:
                    lows(first_unit[then], 1)
                whole(3)
                lower(2)
                lower(3)
                if then:
                    lows(first_unit[then], 2)

            def norm(name, then):
                norm_scale(name)
                norm_parts(name, then)

            def norm_rows(n):
                row_scales()
                step(ts(small[:, 6:8], small[:, 6:8], math.sqrt(D), None, ALU.mult))
                dve.wait_ge(extra_loaded["gain"], 16 * n)
                for c in range(2):
                    for t in range(TT):
                        r = resid[:, t, c * CHUNK:(c + 1) * CHUNK]
                        updated(stt(r, r, small[:, 6 + t:7 + t], gain_bc[:, c * CHUNK:(c + 1) * CHUNK], ALU.mult, ALU.mult))

            def updated(ins):
                tell(ins, residual_ready, count("residual"))

            def add_out(name):
                for k in range(4):
                    c, t = k // 2, k % 2
                    j = J.of(name, k)
                    lows(unit_of[j], SPLIT if c == 0 else 0)
                    wait_filled(dve, j)
                    r = resid[:, t, c * CHUNK:(c + 1) * CHUNK]
                    updated(tt(r, bank(j)[:, :], r, ALU.add))
                    read_out(dve.nop(), j)

            def attention(name, order, heads, base, mask, scale, finish, some=None):
                for kind, a in order if some is None else [order[k] for k in some]:
                    n = base + a
                    if kind == "S":
                        j = J.of(name, order.index(("S", a)))
                        wait_filled(dve, j)
                        s = s_buf[:, n % 3]
                        m = mask(a)
                        top = small[:, 8 + (n % 4) * 2:10 + (n % 4) * 2]
                        if heads[a][0] in CAUSAL:
                            for t in range(TT):
                                w = key_tiles(heads[a][0], t) * P
                                ins = stt(s[:, t, 0:w], bank(j)[:, t * SEQ:t * SEQ + w], scale, m[:, t, 0:w],
                                          ALU.mult, ALU.add)
                            read_out(ins, j)
                            for t in range(TT):
                                w = key_tiles(heads[a][0], t) * P
                                ins = dve.tensor_reduce(top[:, t:t + 1], s[:, t, 0:w], AX, ALU.max, negate=True)
                            tell(ins, scores_shifted, n + 1)
                            continue
                        src = bank(j)[:, :].rearrange("p (t k) -> p t k", t=TT)
                        if m is None:
                            read_out(ts(s, src, scale, None, ALU.mult), j)
                        else:
                            read_out(stt(s, src, scale, m, ALU.mult, ALU.add), j)
                        tell(dve.tensor_reduce(top, s, AX, ALU.max, negate=True),
                             scores_shifted, n + 1)
                    elif kind == "O":
                        j = J.of(name, order.index(("O", a)))
                        r = small[:, 24 + (n % 2) * 2:26 + (n % 2) * 2]
                        dve.wait_ge(weights_ready, n + 1)
                        step(dve.reciprocal(r, small[:, 16 + (n % 4) * 2:18 + (n % 4) * 2]))
                        wait_filled(dve, j)
                        finish(a, j, r)

            def peer(layer):
                u0, d0 = first_unit[f"up{layer}"], first_unit[f"down{layer}"]
                lows(u0)
                sc = view(P_SC, TT, HP, N_KEYS)
                done, tile = [0], [SPLIT]

                def between(columns):
                    done[0] += columns + STEP_COLUMNS
                    if done[0] >= LOW_EVERY and tile[0] < HALF + LEAD - 4:
                        low(u0 + tile[0])
                        tile[0] += 1
                        done[0] = 0
                at = P_TOP + TT * 3 * HK
                off = [at]

                def scratch(*shape):
                    v = view(off[0], *shape)
                    off[0] += math.prod(shape)
                    return v

                sv = scratch(HP, TOPK)
                si = scratch(HP, TOPK)
                si_f = scratch(HP, TOPK)
                rest = scratch(N_KEYS)
                cand = scratch(PEER_HEADS, CANDS)
                rest2 = scratch(CANDS)
                best = scratch(PEER_HEADS, TOPK)
                pos_u = scratch(PEER_HEADS, TOPK)
                part = scratch(5, HK)
                part_f = scratch(5, HK)
                pick = view(P_KEYS, PEER_HEADS, TOPK, TOPK)
                red = scratch(PEER_HEADS)
                small_w = scratch(1, P)
                assert off[0] <= ARENA

                def top16(values, index, src, tmp):
                    pstep(dve.max(values[:, 0:8], src))
                    pstep(dve.max_index(index[:, 0:8].bitcast(U32), values[:, 0:8], src))
                    pstep(dve.match_replace(tmp, values[:, 0:8], src, LOWEST))
                    pstep(dve.max(values[:, 8:16], tmp))
                    pstep(dve.max_index(index[:, 8:16].bitcast(U32), values[:, 8:16], tmp))

                def pstep(ins, columns=HK):
                    step(ins)
                    between(columns)

                wait_read(dve, J.of(f"scores{layer}", 7))
                for t in range(TT):
                    for hp in range(HP):
                        if hp % 4 == 0:
                            wait_read(dve, J.of(f"scores{layer}", 4 * t + hp // 4))
                        top16(sv[:, hp], si[:, hp], sc[:, t, hp], rest)
                    pstep(dve.tensor_copy(si_f, si.bitcast(U32)))
                    svh = sv.rearrange("p (h s) k -> p h s k", s=2)
                    for a0, a1, nb, c0 in ((0, WIDE, TOPK, 0), (WIDE, TOPK, NARROW, WIDE * TOPK)):
                        size = (a1 - a0) * nb
                        pstep(tt(cand[:, :, c0:c0 + size].rearrange("p h (a b) -> p h a b", b=nb),
                                 svh[:, :, 0, a0:a1].unsqueeze(3).to_broadcast([P, PEER_HEADS, a1 - a0, nb]),
                                 svh[:, :, 1, 0:nb].unsqueeze(2).to_broadcast([P, PEER_HEADS, a1 - a0, nb]), ALU.add), PEER_HEADS * size)
                    for h in range(PEER_HEADS):
                        top16(best[:, h], pos_u[:, h], cand[:, h], rest2)
                    g = top_out(t, 2).rearrange("p (h k) -> p h k", k=TOPK)
                    tell(tt(g, best, best[:, :, 0:1].to_broadcast([P, PEER_HEADS, TOPK]), ALU.subtract),
                         top_ready, 4 * layer + t + 1)
                    pu = pos_u.rearrange("p h k -> p (h k)").bitcast(U32)
                    for i, (n, op) in enumerate(((4, ALU.logical_shift_right), (2, ALU.logical_shift_right),
                                                 (NARROW - 1, ALU.bitwise_and), (TOPK - NARROW, ALU.bitwise_and),
                                                 (0, ALU.logical_shift_right))):
                        pstep(ts(part[:, i].bitcast(U32), pu, n, None, op))
                    pstep(dve.tensor_copy(part_f, part.bitcast(U32)), 5 * HK)
                    pstep(stt(part_f[:, 0], part_f[:, 1], float(WIDE * TOPK // NARROW - WIDE), part_f[:, 0],
                              ALU.subtract, ALU.max))
                    pstep(stt(part_f[:, 3], part_f[:, 4], float(WIDE * TOPK), part_f[:, 3], ALU.is_lt, ALU.mult))
                    pstep(tt(part_f[:, 1], part_f[:, 2], part_f[:, 3], ALU.add))
                    sih = si_f.rearrange("p (h s) k -> p h s k", s=2)
                    for i in range(2):
                        a = part_f[:, i].rearrange("p (h k) -> p h k", k=TOPK).unsqueeze(3)\
                            .to_broadcast([P, PEER_HEADS, TOPK, TOPK])
                        lane = iota[:, 0:TOPK].unsqueeze(1).unsqueeze(1).to_broadcast([P, PEER_HEADS, TOPK, TOPK])
                        pstep(tt(pick, a, lane, ALU.is_equal), HK * TOPK)
                        pstep(tt(pick, pick, sih[:, :, i].unsqueeze(2).to_broadcast([P, PEER_HEADS, TOPK, TOPK]), ALU.mult),
                              HK * TOPK)
                        pstep(dve.tensor_reduce(top_out(t, i).rearrange("p (h k) -> p h k", k=TOPK), pick, AX, ALU.add),
                              HK * TOPK)
                while tile[0] < HALF + LEAD - 4:
                    low(u0 + tile[0])
                    tile[0] += 1
                for t in range(TT):
                    n = TT * layer + t
                    low(u0 + HALF + LEAD - 4 + t)
                    g = top_out(t, 2).rearrange("p (h k) -> p h k", k=TOPK)
                    dve.wait_ge(top_exp, n + 1)
                    step(dve.tensor_reduce(red, g, AX, ALU.add))
                    step(dve.reciprocal(red, red))
                    tell(tt(g, g, red.unsqueeze(2).to_broadcast([P, PEER_HEADS, TOPK]), ALU.mult), top_ready, 4 * layer + 2 + t + 1)
                for t in range(TT):
                    j = J.of(f"idxT{layer}", t)
                    wait_filled(dve, j)
                    cols = slice(t * P, (t + 1) * P)
                    w_rest = small_w[:, 0, :]
                    step(dve.tensor_copy(choice[:, 0:2, cols], bank(j)[:, 0:2 * P].rearrange("p (a b) -> p a b", a=2)))
                    step(dve.tensor_copy(choice[:, 2, cols], bank(j)[:, 2 * P:3 * P]))
                    read_out(tt(w_rest, bank(j)[:, 2 * P:3 * P], choice[:, 2, cols], ALU.subtract), j)
                    step(dve.tensor_copy(choice[:, 3, cols], w_rest))
                    step(tt(choice[:, 4, cols], w_rest, choice[:, 3, cols], ALU.subtract))
                dve.wait_ge(extra_loaded["lanes"], 16 * (layer + 1))
                g0, q0 = 64 * layer, 128 * layer

                def over(k, rows, c0):
                    return choice[:, k, c0].unsqueeze(1).to_broadcast([P, rows, GROUP])

                def build_keys(half, g, i=0):
                    s, c0 = g % 2, bass.ds(i * (2 * GROUP) + g * GROUP, GROUP)
                    number = g0 + 32 * half + g
                    if half or g >= 2 or not isinstance(i, int):
                        dve.wait_ge(products, i * 4 + (q0 + 64 * half + 2 * g - 2))

                    tt(first_eq[:, s], lanes[:, half * HALF:(half + 1) * HALF, :], over(0, HALF, c0), ALU.is_equal)\
                        .then_inc(eq_ready, 1)
                    tt(second[:, s], lanes[:], over(1, N_KEYS, c0), ALU.is_equal)

                def build_weights(half, g, i=0):
                    s, c0 = g % 2, bass.ds(i * (2 * GROUP) + g * GROUP, GROUP)
                    dve.wait_ge(eq_ready, i * 2 + (g0 + 32 * half + g + 1))
                    for p in range(3):
                        last = tt(first[:, s, p], first_eq[:, s], over(2 + p, HALF, c0), ALU.mult)
                    last.then_inc(onehots, 1)

                def weigh(half, q, i=0):
                    dve.wait_ge(products, unit_wait(q0 + 64 * half + q + 1, i))
                    a = acts[:, half * HALF:(half + 1) * HALF, bass.ds(i * 16 + q * 4, 4)]
                    tt(a, banks[2 + q % 2][:, 0:4 * HALF].rearrange("p (c i) -> p i c", c=4), a, ALU.mult)\
                        .then_inc(weighted, 1)

                def gated_low(t, i=0):
                    dve.wait_ge(g_high, unit_wait(N_KEYS * layer + t + 1, i))
                    src = acts[:, bass.ds(i * 4 + t, 1), :].rearrange("p a b -> p (a b)")
                    tt(gl[:, t % SPLIT, :], src, gh[:, t % SPLIT, :].bitcast(F32), ALU.subtract).then_inc(g_low, 1)

                dve.wait_ge(gelu_done, N_KEYS * layer + HALF)
                low(u0 + HALF + LEAD - 2)
                build_keys(0, 0)
                low(u0 + HALF + LEAD - 1)
                build_weights(0, 0)
                low(u0 + HALF + LEAD)
                build_keys(0, 1)
                build_weights(0, 1)

                def weigh_and_build(half, k, i, ahead):
                    ahead(k, i)
                    weigh(half, k, i)
                    if k % 2:
                        build_keys(half, 2 + k // 2, i)
                    elif k:
                        build_weights(half, 2, i)
                    elif not isinstance(i, int) or i:
                        build_weights(half, 1, i)

                def low_up(k, i):
                    low(u0 + HALF + LEAD + 1 + k, i)

                def low_down(k, i):
                    low(d0 + 1 + k, i)
                    gated_low(1 + k, i)

                for k in range(4):
                    weigh_and_build(0, k, 0, low_up)
                with dve.Fori(1, (HALF - LEAD) // 4) as i:
                    for k in range(4):
                        weigh_and_build(0, k, i, low_up)
                for i in range((HALF - LEAD) // 4, HALF // 4 - 1):
                    for k in range(4):
                        weigh_and_build(0, k, i, lambda k, i: None)
                build_weights(0, HALF // 2 - 1)
                for q in range(HALF - 4, HALF):
                    weigh(0, q)
                dve.wait_ge(gelu_done, N_KEYS * (layer + 1))
                gated_low(0)
                build_keys(1, 0)
                low_down(0, 0)
                build_weights(1, 0)
                build_keys(1, 1)
                build_weights(1, 1)
                for k in range(4):
                    weigh_and_build(1, k, 0, lambda k, i: low_down(k + 1, i))
                with dve.Fori(1, HALF // 4 - 1) as i:
                    for k in range(4):
                        weigh_and_build(1, k, i, lambda k, i: low_down(k + 1, i))
                build_weights(1, HALF // 2 - 1)
                for k in range(HALF - 4, HALF):
                    if k < HALF - 2:
                        low_down(k + 1, 0)
                    weigh(1, k)

                def gated_tiles(t0, t1):
                    with dve.Fori(0, (t1 - t0) // 4) as i:
                        for k in range(t0, t0 + 4):
                            low(d0 + k, i)
                            gated_low(k, i)
                    for t in range(t1 - (t1 - t0) % 4, t1):
                        low(d0 + t)
                        gated_low(t)

                if layer == 0:
                    gated_tiles(HALF, N_KEYS)
                else:
                    gated_tiles(HALF, MEM_SQUARES)
                    norm_scale("mem")
                    gated_tiles(MEM_SQUARES, MEM_SPLIT)
                    norm_parts("mem", dst=mem_in_T)
                    gated_tiles(MEM_SPLIT, N_KEYS)
                issued[0] = d0 + N_KEYS
                if layer == 1:
                    lows(first_unit["mem0"])
                dve.wait_ge(units_used, d0 + N_KEYS)
                for c in range(2):
                    for t in range(TT):
                        r = resid[:, t, c * CHUNK:(c + 1) * CHUNK]
                        updated(tt(r, banks[4 + 2 * t + c][:, :], r, ALU.add))

            dve.wait_ge(norm_loaded, 16 * 2)
            norm("attn", "qkv")
            dve.wait_ge(const_loaded, 16 * N_CONST)
            for k in range(4, 8):
                j = J.of("qkv", k)
                lows(unit_of[j])
                wait_filled(dve, j)
                i = 2 * (k - 4)
                read_out(dve.tensor_copy(na_k[:, i:i + 2, :].rearrange("p a b -> p (a b)"), bank(j)[:, :]), j)
            lows(unit_of[J.of("qkv", 11)])
            dve.wait_ge(extra_loaded["bias"], 16)

            def na_finish(a, j, r):
                for t in range(TT):
                    ins = ts(na_o[:, t, a * HEAD:(a + 1) * HEAD], bank(j)[:, t * HEAD:(t + 1) * HEAD], r[:, t:t + 1],
                             None, ALU.mult)
                read_out(ins, j)

            attention("na", NA, na_heads, head_base["na"], lambda a: na_bias[:, a], 1.0, na_finish)
            split_low("na_oT", na_out, 4)
            add_out("wo")
            norm("peer0", "query0")
            peer(0)
            u = view(C_U, KT, SEQ + 2)
            step(dve.memset(u[:, :, 0:1], 0.0))
            step(dve.memset(u[:, :, SEQ + 1:SEQ + 2], 0.0))
            norm("conv", "conv_in")
            cT, y = view(C_C, KT, SEQ), view(C_Y, KT, SEQ)
            for h in range(2):
                for k in range(2):
                    j, i = J.of("conv_in", 6 * h + 2 + k), 4 * h + 2 * k
                    lows(unit_of[j])
                    wait_read(dve, J.of("conv_in", 6 * h + k))
                    wait_filled(dve, j)
                    read_out(tt(u[:, i:i + 2, 1:SEQ + 1], cT[:, i:i + 2, :],
                                bank(j)[:, :].rearrange("p (a b) -> p a b", a=2), ALU.mult), j)
                for i in range(4):
                    k = 4 * h + i
                    step(ts(y[:, k], u[:, k, 0:SEQ], convw[:, k, 0:1], None, ALU.mult))
                    for tap in (1, 2):
                        step(stt(y[:, k], u[:, k, tap:tap + SEQ], convw[:, k, tap:tap + 1], y[:, k], ALU.mult, ALU.add))
                    lows(first_unit["conv_in"] + KT // UKT * (3 * h + 2) + i + 1)
                for k in range(2):
                    g, j = 2 * h + k, J.of("conv_in", 6 * h + 4 + k)
                    pair = y[:, 2 * g:2 * g + 2]
                    wait_filled(dve, j)
                    tell(tt(pair, pair, bank(j)[:, :].rearrange("p (a b) -> p a b", a=2), ALU.mult), conv_ready, g + 1)
                    read_out(dve.nop(), j)
                for g in range(2 * h, 2 * h + 2):
                    n = XG["conv"] + g + 1
                    dve.wait_ge(x_high, n)
                    tell(tt(conv_out[1][:, 2 * g:2 * g + 2], y[:, 2 * g:2 * g + 2],
                            conv_out[0][:, 2 * g:2 * g + 2].bitcast(F32), ALU.subtract), x_low, n)
            add_out("conv_out")
            norm("peer1", "query1")
            peer(1)
            lows(first_unit["mem0"] + 3, 0)
            norm_rows(1)
            lows(first_unit["mem1"], 0)
            norm_scale("even")
            lows(unit_of[J.of("mem1", 0)], 0)
            norm_parts("even", "even_in")
            pos_f = small[:, 56:58]
            step(dve.tensor_copy(pos_f, pos_i[:]))
            dve.wait_ge(extra_loaded["masks"], 16 * 3)
            two_pi = 2 * math.pi
            c1 = float(np.float32(6.28125))
            c2 = float(np.float32(two_pi - c1))
            c3 = float(two_pi - c1 - c2)
            turns = view(E_TMP, TT, ROPES)
            for t in range(TT):
                step(ts(sinT[:, t], inv_freq[:], pos_f[:, t:t + 1], None, ALU.mult))
            step(ts(turns, sinT, 1.0 / two_pi, 12582912.0, ALU.mult, ALU.add))
            step(ts(turns, turns, 12582912.0, None, ALU.subtract))
            for c in (c1, c2, c3):
                step(stt(sinT, turns, -c, sinT, ALU.mult, ALU.add))
            step(ts(sinT, sinT, 3.1415925, -3.1415925, ALU.min, ALU.max))
            step(ts(cosT, sinT, -1.0, None, ALU.mult))
            step(tt(cosT, cosT, sinT, ALU.max))
            step(ts(cosT, cosT, -1.0, math.pi / 2, ALU.mult, ALU.add))
            tell(dve.nop(), angle_ready, 1)
            dve.wait_ge(tables, 1)

            def rope(t, dst_v, src_v, heads, hd, f0):
                x = src_v.rearrange("p (h s f) -> p h s f", s=2, f=hd // 2)
                f = hd // 2
                a = view(E_TMP, heads, 2, f)
                b = view(E_TMP + 512, heads, 2, f)
                cos = cosT[:, t, f0:f0 + f]
                sin = sinT[:, t, f0:f0 + f]
                step(tt(a, x, cos.unsqueeze(1).unsqueeze(1).to_broadcast([P, heads, 2, f]), ALU.mult))
                step(tt(b, x, sin.unsqueeze(1).unsqueeze(1).to_broadcast([P, heads, 2, f]), ALU.mult))
                for o in dst_v:
                    step(tt(o[:, :, 0], a[:, :, 0], b[:, :, 1], ALU.subtract))
                    step(tt(o[:, :, 1], a[:, :, 1], b[:, :, 0], ALU.add))

            def as_heads(v, hd):
                return v.rearrange("p (h s f) -> p h s f", s=2, f=hd // 2)

            def chunks_read(name, a, b, chunks):
                for c in range(a // CHUNK, (b - 1) // CHUNK + 1):
                    for t in range(TT):
                        wait_read(dve, J.of(name, 2 * chunks.index(c) + t))

            gates = ev_proj[:, :, EVEN["ng"]:EVEN["ng"] + 24]
            cs = cmp_s.rearrange("p t h n -> p (t h) n")[:, :, 0:N_CMP]
            cm = cmp_small[:, 256:272]

            def even_steps(c, u):
                for kind, k in EVEN_PLAN.get((c, u), ()):
                    if kind == "rope":
                        name, t = EVEN_ROPES[k]
                        w = 512 if name in ("nq", "mq", "mk") else 128
                        chunks_read("even_in", EVEN[name], EVEN[name] + w, EVEN_CHUNKS)
                        if w == 512:
                            outs = [as_heads({"nq": e_nq, "mq": e_mq, "mk": e_mk}[name][:, t], HEAD)]
                        elif name == "nkc":
                            outs = [as_heads(e_kc[:, t], HEAD)]
                        else:
                            outs = [{"nks": e_ks, "nkw": e_kw}[name][:, t, :, dup].rearrange("p g (s f) -> p g s f", s=2)
                                    for dup in range(2)]
                        rope(t, outs, ev_proj[:, t, EVEN[name]:EVEN[name] + w], w // HEAD, HEAD, 0)
                        tell(dve.nop(), roped, k + 1)
                    elif kind == "cmp_blocks":
                        step(dve.memset(cmp_small[:], 0.0))
                        j = J.of("even_T", 2)
                        wait_filled(dve, j)
                        read_out(dve.tensor_copy(eT[:, EKC:EKC + 2, :].rearrange("p a b -> p (a b)"), bank(j)[:, :]), j)
                        for kv, pe_sb in (("k", pe_k), ("v", pe_v)):
                            by = cmp_T[kv].rearrange("p (n l) -> p l n", l=CMP_STRIDE)
                            for part in range(2):
                                l0 = part * CMP_STRIDE
                                step(tt(ape[kv][:, l0:l0 + CMP_STRIDE], by[:, :, part:part + N_CMP],
                                        pe_sb[:, l0:l0 + CMP_STRIDE].unsqueeze(2).to_broadcast([P, CMP_STRIDE, N_CMP]),
                                        ALU.add))
                        tell(dve.nop(), cmp_ready, 1)
                    elif kind == "cmp_hidden":
                        for g in range(NSA_GROUPS):
                            wait_read(dve, J.of("hid", g))
                        step(dve.tensor_copy(hid_rep[:, :, 0:N_CMP], hid_sb[:, 1:2, 0:N_CMP].to_broadcast([P, 4, N_CMP])))
                        tell(dve.nop(), cmp_ready, 2)
                        step(dve.memset(vbd, 0.0))
                    elif kind == "gates":
                        chunks_read("even_in", EVEN["ng"], EVEN["ng"] + 24, EVEN_CHUNKS)
                        tell(tt(gates, gates, gate_b[:].unsqueeze(1).to_broadcast([P, TT, 24]), ALU.add), gate_in, 1)
                    elif kind == "kvc":
                        j = J.of("kvc", k)
                        wait_filled(dve, j)
                        step(dve.tensor_copy(kcT[:, k, 0:N_CMP], bank(j)[:, 0:N_CMP]))
                        for i in range(4):
                            ins = dve.tensor_copy(vbd[32 * i:32 * i + 32, k, i, :], bank(j)[32 * i:32 * i + 32, 64:64 + HEAD])
                            if i < 3:
                                step(ins)
                        read_out(ins, j)
                    elif kind == "cmp_S":
                        if k == 0:
                            step(dve.memset(cmp_s, 0.0))
                        j = J.of("cmp_S", k)
                        wait_filled(dve, j)
                        src = bank(j)[:, 0:128].rearrange("p (h t n) -> p h t n", h=4, t=TT)
                        for t in range(TT):
                            ins = stt(cmp_s[:, t, k:8:2, 0:N_CMP], src[:, :, t, 0:N_CMP], HEAD ** -0.5,
                                      cmp_mask[:, 0, t:t + 1, 0:N_CMP].to_broadcast([P, 4, N_CMP]), ALU.mult, ALU.add)
                            if t == 0:
                                step(ins)
                        read_out(ins, j)
                    elif kind == "cmp_softmax":
                        step(dve.tensor_reduce(cm, cs, AX, ALU.max))
                        tell(tt(cs, cs, cm.unsqueeze(2).to_broadcast([P, 16, N_CMP]), ALU.subtract), cmp_exp_in, 1)
                        dve.wait_ge(cmp_exp, 1)
                        dve.wait_ge(nsa_gate, 1)
                        for t in range(TT):
                            row = cmp_s[:, t, :, 0:N_CMP]
                            step(tt(row, row, cmp_mask[:, 1, t:t + 1, 0:N_CMP].to_broadcast([P, 8, N_CMP]), ALU.mult))
                        step(dve.tensor_reduce(cm, cs, AX, ALU.add))
                        step(ts(cm, cm, 1e-30, None, ALU.max))
                        step(dve.reciprocal(cm, cm))
                        by_tile = cm.rearrange("p (t h) -> p t h", t=TT)
                        step(tt(by_tile, by_tile, gates[:, :, 0:8], ALU.mult))
                        step(tt(cs, cs, cm.unsqueeze(2).to_broadcast([P, 16, N_CMP]), ALU.mult))
                        tell(dve.nop(), cmp_ready, 3)
                    elif kind == "cmp_O":
                        j = J.of("cmp_O", k)
                        wait_filled(dve, j)
                        read_out(dve.tensor_copy(nsa_o[:, k], bank(j)[:, :]), j)

            def even_heads(c, u):
                for kind, k in EVEN_PLAN.get((c, u), ()):
                    if kind == "ev":
                        attention("ev", EV, ev_heads, head_base["ev"],
                                  lambda a: None if ev_heads[a][0] == "mem_e" else causal, HEAD ** -0.5, ev_finish,
                                  head_step(EV, k))

            def ev_finish(a, j, r):
                name, h = ev_heads[a][:2]
                if name in ("nsa_s", "nsa_w"):
                    br = 1 if name == "nsa_s" else 2
                    step(tt(r, r, gates[:, :, br * 8 + h:br * 8 + h + 1].rearrange("p a b -> p (a b)"), ALU.mult))
                elif h == 0:
                    dve.wait_ge(silu_done, 2 if name == "moba" else 3)
                for t in range(TT):
                    o = bank(j)[:, t * HEAD:(t + 1) * HEAD]
                    if name in ("nsa_s", "nsa_w"):
                        dst = nsa_o[:, t, h * HEAD:(h + 1) * HEAD]
                        ins = stt(dst, o, r[:, t:t + 1], dst, ALU.mult, ALU.add)
                    else:
                        z = EVEN["mz" if name == "moba" else "ez"] + h * HEAD
                        dst = ev_proj[:, t, z:z + HEAD]
                        ins = stt(dst, o, r[:, t:t + 1], dst, ALU.mult, ALU.mult)
                read_out(ins, j)

            for c in range(len(EVEN_CHUNKS) + 1):
                for u in range(KT // UKT):
                    even_heads(c, u)
                    if c < len(EVEN_CHUNKS):
                        lows(first_unit["even_in"] + KT // UKT * c + u + 1)
                    even_steps(c, u)
            z = ev_proj[:, :, EVEN["nz"]:EVEN["nz"] + 512]
            tell(tt(z, z, nsa_o, ALU.mult), y_ready, 1)
            split_low("even_yT", ev_out, 5)
            add_out("even_out")
            norm("odd", "odd_in")

            def om_finish(a, j, r):
                if a == 0:
                    dve.wait_ge(silu_done, 4)
                for t in range(TT):
                    z = ODD["ez"] + a * HEAD
                    dst = od_proj[:, t, z:z + HEAD]
                    ins = stt(dst, bank(j)[:, t * HEAD:(t + 1) * HEAD], r[:, t:t + 1], dst, ALU.mult, ALU.mult)
                read_out(ins, j)

            def odd_steps(c, u):
                for kind, k in ODD_PLAN.get((c, u), ()):
                    if kind == "rope":
                        name, hh, t = ("rq", "rk")[k // 4], k // 2 % 2, k % 2
                        a = ODD[name] + hh * 512
                        chunks_read("odd_in", a, a + 512, ODD_CHUNKS)
                        dst = (o_q, o_k)[k // 4][:, t, hh * 512:(hh + 1) * 512]
                        rope(t, [as_heads(dst, RET_QK)], od_proj[:, t, a:a + 512], 2, RET_QK, ROPE)
                        tell(dve.nop(), roped, len(EVEN_ROPES) + k + 1)
                    elif kind == "ret_S":
                        j = J.of("ret_S", k)
                        wait_filled(dve, j)
                        if k == 0:
                            dve.wait_ge(extra_loaded["decay"], 16)
                        if k >= 2:
                            wait_filled(dve, J.of("ret_O", TT * (k - 2) + 1))
                        step(stt(ret_buf[:, k % 2, 0:2].rearrange("p a b -> p (a b)"), bank(j)[:, 0:SEQ], RET_QK ** -0.5,
                                 decay[:, k, :], ALU.mult, ALU.mult))
                        ins = stt(ret_buf[:, k % 2, 2], bank(j)[:, SEQ:SEQ + P], RET_QK ** -0.5, decay[:, k, 0:P],
                                  ALU.mult, ALU.mult)
                        read_out(ins, j)
                        tell(dve.nop(), ret_ready, k + 1)
                    elif kind == "ret_O":
                        dve.wait_ge(silu_done, 5 + k)
                        for t in range(TT):
                            n = TT * k + t
                            j = J.of("ret_O", n)
                            wait_filled(dve, j)
                            step(dve.bn_stats(bn[:, 0:6], bank(j)[:, :]))
                            tell(dve.bn_aggr(ret_stats[:, n, :], bn[:, 0:6]), ret_var, n + 1)
                            dve.wait_ge(ret_scale, n + 1)
                            o = view(E_TMP, RET_V)
                            read_out(ts(o, bank(j)[:, :], ret_stats[:, n, 0:1], small[:, 30 + n:31 + n], ALU.subtract, ALU.mult), j)
                            z = od_proj[:, t, ODD["rz"] + k * RET_V:ODD["rz"] + (k + 1) * RET_V]
                            step(tt(z, z, o, ALU.mult))

            def odd_heads(c, u):
                for kind, k in ODD_PLAN.get((c, u), ()):
                    if kind == "om":
                        attention("om", OM, om_heads, head_base["om"], lambda a: None, HEAD ** -0.5, om_finish,
                                  head_step(OM, k))

            for c in range(len(ODD_CHUNKS)):
                for u in range(KT // UKT):
                    odd_heads(c, u)
                    lows(first_unit["odd_in"] + KT // UKT * c + u + 1)
                    odd_steps(c, u)
            tell(dve.nop(), y_ready, 2)
            split_low("odd_yT", od_out, 9)
            add_out("odd_out")
            norm_rows(2)
            tell(dve.nop(), final_ready, 1)


def window_bias(rel_bias):
    q, k = np.arange(SEQ)[:, None], np.arange(SEQ)[None, :]
    qc, kc = q % GRID_W, k % GRID_W
    row = k // GRID_W - q // GRID_W + MAX_WIN_ROWS - 1
    start = np.clip(qc - WIN_COLS // 2, 0, GRID_W - WIN_COLS)
    inside = (kc >= start) & (kc < start + WIN_COLS)
    col = np.clip(kc - qc + WIN_COLS - 1, 0, 2 * WIN_COLS - 2)
    full = np.where(inside[None], rel_bias[:, row, col], np.float32(NEG))
    return full.reshape(NA_HEADS, TT, P, SEQ).transpose(2, 0, 1, 3)


def constants():
    q, k = np.arange(SEQ)[:, None], np.arange(SEQ)[None, :]
    causal = np.where(k <= q, 0.0, NEG).reshape(TT, P, SEQ).transpose(1, 0, 2)
    n = np.arange(16)[None, :]
    seen = (n * CMP_STRIDE + CMP_LEN - 1 <= q) & (n < N_CMP)
    cmp_mask = np.stack([np.where(seen, 0.0, NEG), seen * 1.0]).reshape(2, TT, P, 16).transpose(2, 0, 1, 3)
    f = np.float32
    inv = np.concatenate([f(1) / f(10000.0) ** (np.arange(0, 64, 2, dtype=f) / f(64)),
                          f(1) / f(10000.0) ** np.linspace(0, 1, RET_ROPE, dtype=f)])
    log_g = np.log(f(1) - f(2) ** (f(-5) - np.arange(RET_HEADS, dtype=f))).astype(f)
    dist = (k[0][None, :] - np.arange(P)[:, None]).astype(f)
    decay = np.where(dist[:, None] >= 0, np.exp(np.maximum(dist, 0)[:, None] * log_g[None, :, None]), 0)
    c = {"c_ident": np.eye(P), "c_iota": np.arange(TOPK), "c_causal": causal, "c_cmp_mask": cmp_mask,
         "c_inv_freq": inv, "c_decay": decay}
    c = {name: np.ascontiguousarray(a, dtype=f) for name, a in c.items()}
    c["c_lanes"] = np.repeat(np.arange(N_KEYS), GROUP).reshape(N_KEYS, GROUP).astype(mybir.dt.np(BF16))
    return c


def kernel(**inputs):
    import concourse.bacc as _bacc
    from concourse.bass_utils import run_bass_kernel_spmd as _run

    i = {name: np.asarray(a) for name, a in inputs.items()}
    gains = np.stack([i["norm_mix"][0], i["norm_ffn"][0], i["norm_mix"][1], i["norm_ffn"][1],
                      i["mem_norm_g_2"], i["l0_norm_g_2"], i["l1_norm_g_2"]])
    arrays = {
        "x": i["x"][0], "mem": i["mem_2"][0],
        "positions": i["positions_2"].reshape(TT, P).T,
        "gains": gains.reshape(len(NORMS), KT, P).transpose(2, 0, 1),
        "norm_final": i["norm_final"], "final_norm": i["final_norm_g_2"],
        "attn_w_qkv": i["attn_w_qkv"][0], "attn_w_o": i["attn_w_o"][0],
        "na_bias": window_bias(i["attn_rel_bias"][0]),
        "conv_w_in": i["conv_w_in"][0], "conv_w_out": i["conv_w_out"][0],
        "conv_w": i["conv_w_conv"][0].reshape(3, KT, P).transpose(2, 1, 0),
        "peer_w_query": i["peer_w_query"],
        "keysT": i["peer_sub_keys"].reshape(2, HP, N_KEYS, P).transpose(0, 3, 1, 2),
        "w_upT": i["peer_w_up"].reshape(2 * N_KEYS, N_KEYS, KT, P).transpose(0, 3, 2, 1).reshape(2 * N_KEYS, P, KT * N_KEYS),
        "w_down": i["peer_w_down"].reshape(2 * N_KEYS, N_KEYS, D),
        "l0_w_in_2": i["l0_w_in_2"], "l0_w_out_2": i["l0_w_out_2"], "l0_w_mem_kv_2": i["l0_w_mem_kv_2"],
        "l1_w_in_2": i["l1_w_in_2"], "l1_w_out_2": i["l1_w_out_2"], "l1_w_mem_kv_2": i["l1_w_mem_kv_2"],
        "gate_b": i["l0_nsa_gate_b_2"],
        "pe_k": np.concatenate([i["l0_cmp_pe_k_2"].T] * 2), "pe_v": np.concatenate([i["l0_cmp_pe_v_2"].T] * 2),
        "w1_k": i["l0_cmp_w1_k_2"].transpose(1, 0, 2), "w1_v": i["l0_cmp_w1_v_2"].transpose(1, 0, 2),
        "w2_k": i["l0_cmp_w2_k_2"], "w2_v": i["l0_cmp_w2_v_2"],
        **constants(),
    }
    nc = _bacc.Bacc("TRN2", target_bir_lowering=False, num_devices=1)
    d, fed = {}, {}
    for name, a in arrays.items():
        a = np.ascontiguousarray(a)
        fed[f"in_{name}"] = a
        d[name] = nc.dram_tensor(f"in_{name}", a.shape, mybir.dt.from_np(a.dtype), kind="ExternalInput").ap()
    out = nc.dram_tensor("out_rows", (SEQ, D), F32, kind="ExternalOutput").ap()
    build(nc, d, out)
    r = _run(nc, [fed], core_ids=[0])
    return r.results[0]["out_rows"].reshape(1, SEQ, D)
```
